# Optimizing a Trainium2 kernel written in Bass

```python
import jax, jax.numpy as jnp
from jax import lax
import numpy as np
import math

D_MODEL = 1024
BATCH = 1
SEQ = 512
DEPTH = 2

BRANCH_W = D_MODEL // 2
N_BRANCHES = 3
POOL_WINDOWS = (2, 4, 8, 16)
POOL_GROUPS = 4
POOL_GROUP_W = BRANCH_W // POOL_GROUPS
RET_HEADS = 4
RET_HEAD_DIM = BRANCH_W // RET_HEADS
RET_CHUNK = 128
ROPE_BASE = 10000.0
RWKV_HEAD_DIM = 64
RWKV_HEADS = BRANCH_W // RWKV_HEAD_DIM
RWKV_W_LORA = 64
RWKV_A_LORA = 64
RWKV_SHIFT_W = 3 * BRANCH_W + RWKV_W_LORA + RWKV_A_LORA
IN_SPLIT_SIZES = (BRANCH_W, BRANCH_W, BRANCH_W, BRANCH_W, BRANCH_W, BRANCH_W,
                  RWKV_SHIFT_W, BRANCH_W, N_BRANCHES * D_MODEL)
D_IN = sum(IN_SPLIT_SIZES)
NORM_EPS = 1e-6
RET_NORM_EPS = 1e-5
RWKV_NORM_EPS = 64e-5


def rms_norm(x, g):
    x32 = x.astype(jnp.float32)
    y = x32 * lax.rsqrt(jnp.mean(x32 * x32, axis=-1, keepdims=True) + NORM_EPS)
    return (y * g).astype(x.dtype)

def head_norm(x, eps):
    x32 = x.astype(jnp.float32)
    mu = jnp.mean(x32, axis=-1, keepdims=True)
    xc = x32 - mu
    var = jnp.mean(xc * xc, axis=-1, keepdims=True)
    return xc * lax.rsqrt(var + eps)

def causal_pool_mixer(u, pool_w, pool_scale):
    B, T, _ = u.shape
    u32 = u.astype(jnp.float32)
    cs_pad = jnp.pad(jnp.cumsum(u32, axis=1), ((0, 0), (1, 0), (0, 0)))
    t_idx = jnp.arange(T)
    outs = []
    for gi, w in enumerate(POOL_WINDOWS):
        sl = slice(gi * POOL_GROUP_W, (gi + 1) * POOL_GROUP_W)
        c = cs_pad[..., sl]
        lower = jnp.pad(c[:, :T + 1 - w], ((0, 0), (w - 1, 0), (0, 0)))
        win_sum = c[:, 1:] - lower
        count = jnp.minimum(t_idx + 1, w).astype(jnp.float32)[None, :, None]
        outs.append(win_sum / count - u32[..., sl])
    d = jnp.stack(outs, axis=2).astype(u.dtype)
    y = jnp.einsum('btgc,gcd->btgd', d, pool_w).reshape(B, T, BRANCH_W)
    return y * pool_scale

def rotary(x, positions):
    half = x.shape[-1] // 2
    freqs = ROPE_BASE ** (-jnp.arange(half, dtype=jnp.float32) / half)
    ang = positions.astype(jnp.float32)[..., None] * freqs
    cos = jnp.cos(ang)[:, :, None, :]
    sin = jnp.sin(ang)[:, :, None, :]
    x32 = x.astype(jnp.float32)
    x1, x2 = x32[..., :half], x32[..., half:]
    return jnp.concatenate([x1 * cos - x2 * sin, x1 * sin + x2 * cos], axis=-1)

def retention(q, k, v, positions, ret_norm_g):
    dtype = q.dtype
    B, T, _ = q.shape
    H, dh, C = RET_HEADS, RET_HEAD_DIM, RET_CHUNK
    N = T // C
    qh = rotary(q.reshape(B, T, H, dh), positions)
    kh = rotary(k.reshape(B, T, H, dh), positions) * (dh ** -0.5)
    vh = v.reshape(B, T, H, dh).astype(jnp.float32)

    def to_chunks(a):
        return a.reshape(B, N, C, H, dh).transpose(0, 3, 1, 2, 4)

    qc, kc, vc = to_chunks(qh), to_chunks(kh), to_chunks(vh)
    log_gamma = jnp.log1p(-(2.0 ** (-5.0 - jnp.arange(H, dtype=jnp.float32))))
    i = jnp.arange(C, dtype=jnp.float32)
    diff = i[:, None] - i[None, :]
    decay_mask = jnp.where(diff >= 0,
                           jnp.exp(log_gamma[:, None, None] * jnp.maximum(diff, 0.0)),
                           0.0)
    scores = jnp.einsum('bhnid,bhnjd->bhnij', qc, kc) * decay_mask[None, :, None]
    o_intra = jnp.einsum('bhnij,bhnje->bhnie', scores, vc)
    k_tail = kc * jnp.exp(log_gamma[:, None] * (C - 1 - i))[None, :, None, :, None]
    kv = jnp.einsum('bhnjd,bhnje->bhnde', k_tail, vc)
    chunk_decay = jnp.exp(log_gamma * C)[None, :, None, None]

    def step(R, kv_n):
        return chunk_decay * R + kv_n, R

    _, R_prev = lax.scan(step, jnp.zeros((B, H, dh, dh), jnp.float32), jnp.moveaxis(kv, 2, 0))
    R_prev = jnp.moveaxis(R_prev, 0, 2)
    q_dec = qc * jnp.exp(log_gamma[:, None] * (i + 1.0))[None, :, None, :, None]
    o = o_intra + jnp.einsum('bhnid,bhnde->bhnie', q_dec, R_prev)
    o = o.transpose(0, 2, 3, 1, 4).reshape(B, T, H, dh)
    o = head_norm(o, RET_NORM_EPS).reshape(B, T, BRANCH_W) * ret_norm_g
    return o.astype(dtype)

def rwkv7_time_mix(p, shift_mu, w0, w2, a0, a2, k_k, k_a, r_k, ln_w, ln_b):
    dtype = p.dtype
    B, T, _ = p.shape
    H, N = RWKV_HEADS, RWKV_HEAD_DIM
    p_prev = jnp.pad(p[:, :-1], ((0, 0), (1, 0), (0, 0)))
    p = p + (p_prev - p) * shift_mu
    split_pts = (BRANCH_W, BRANCH_W + RWKV_W_LORA, 2 * BRANCH_W + RWKV_W_LORA,
                 3 * BRANCH_W + RWKV_W_LORA)
    r, wl, k, v, al = jnp.split(p, split_pts, axis=-1)
    w = -jax.nn.softplus(-(w0 + jnp.tanh(wl) @ w2)) - 0.5
    decay = jnp.exp(-jnp.exp(w.astype(jnp.float32)))
    a = jax.nn.sigmoid(a0 + al @ a2)

    def heads(z):
        return z.reshape(B, T, H, N).astype(jnp.float32)

    kk = heads(k * k_k)
    kk = kk / jnp.maximum(jnp.sqrt(jnp.sum(kk * kk, axis=-1, keepdims=True)), 1e-12)
    k = k * (1.0 + (a - 1.0) * k_a)
    r_h, k_h, v_h, a_h, w_h = heads(r), heads(k), heads(v), heads(a), heads(decay)
    xs = tuple(jnp.moveaxis(z, 1, 0) for z in (r_h, w_h, k_h, v_h, -kk, kk * a_h))

    def step(S, inp):
        r_t, w_t, k_t, v_t, a_t, b_t = inp
        sa = jnp.einsum('bhvk,bhk->bhv', S, a_t)
        S = (S * w_t[:, :, None, :] + sa[..., None] * b_t[:, :, None, :]
             + v_t[..., None] * k_t[:, :, None, :])
        return S, jnp.einsum('bhvk,bhk->bhv', S, r_t)

    _, y = lax.scan(step, jnp.zeros((B, H, N, N), jnp.float32), xs)
    y = jnp.moveaxis(y, 0, 1)
    y = head_norm(y, RWKV_NORM_EPS).reshape(B, T, BRANCH_W) * ln_w + ln_b
    bonus = jnp.sum(r_h * k_h * r_k, axis=-1, keepdims=True) * v_h
    y = y + bonus.reshape(B, T, BRANCH_W)
    return y.astype(dtype)

def hybrid_layer(x, c_act, positions, norm_g, w_ada, b_ada, w_in, pool_w, pool_scale,
                 ret_norm_g, shift_mu, w0, w2, a0, a2, k_k, k_a, r_k, ln_w, ln_b,
                 w_branch, w_out):
    B, T, D = x.shape
    mod = c_act @ w_ada + b_ada
    shift, scale, gate = jnp.split(mod[:, None, :], 3, axis=-1)
    h = rms_norm(x, norm_g) * (1.0 + scale) + shift
    proj = h @ w_in
    points = np.cumsum(IN_SPLIT_SIZES)[:-1].tolist()
    pool_u, pool_g, q, k, v, ret_g, rw, rw_g, gate_logits = jnp.split(proj, points, axis=-1)
    o_pool = causal_pool_mixer(pool_u, pool_w, pool_scale) * jax.nn.silu(pool_g)
    o_ret = retention(q, k, v, positions, ret_norm_g) * jax.nn.silu(ret_g)
    o_rwkv = rwkv7_time_mix(rw, shift_mu, w0, w2, a0, a2, k_k, k_a, r_k,
                            ln_w, ln_b) * jax.nn.silu(rw_g)
    branches = jnp.stack([o_pool, o_ret, o_rwkv], axis=2)
    y = jnp.einsum('btnw,nwd->btnd', branches, w_branch)
    gates = jax.nn.sigmoid(gate_logits.reshape(B, T, N_BRANCHES, D))
    merged = jnp.sum(gates * y, axis=2)
    return x + gate * (merged @ w_out)

def first_inputs(seed: int = 0) -> dict:
    key = jax.random.key(seed)
    ks = jax.random.split(key, 24)
    L, D, W = DEPTH, D_MODEL, BRANCH_W
    nrm = jax.random.normal
    f32 = jnp.float32
    return {
        "x": nrm(ks[0], (BATCH, SEQ, D), f32),
        "c": nrm(ks[1], (BATCH, D), f32),
        "positions": jnp.broadcast_to(jnp.arange(SEQ, dtype=jnp.int32), (BATCH, SEQ)),
        "norm_g": 1.0 + 0.05 * nrm(ks[2], (L, D), f32),
        "w_ada": 0.5 * D ** -0.5 * nrm(ks[3], (L, D, 3 * D), f32),
        "b_ada": 0.01 * nrm(ks[4], (L, 3 * D), f32),
        "w_in": D ** -0.5 * nrm(ks[5], (L, D, D_IN), f32),
        "pool_w": POOL_GROUP_W ** -0.5 * nrm(ks[6], (L, POOL_GROUPS, POOL_GROUP_W, POOL_GROUP_W), f32),
        "pool_scale": 1.0 + 0.1 * nrm(ks[7], (L, W), f32),
        "ret_norm_g": 1.0 + 0.05 * nrm(ks[8], (L, W), f32),
        "rwkv_shift_mu": jax.random.uniform(ks[9], (L, RWKV_SHIFT_W), f32),
        "rwkv_w0": jax.random.uniform(ks[10], (L, W), f32, -6.0, 1.0),
        "rwkv_w2": 0.5 * RWKV_W_LORA ** -0.5 * nrm(ks[11], (L, RWKV_W_LORA, W), f32),
        "rwkv_a0": 0.1 * nrm(ks[12], (L, W), f32),
        "rwkv_a2": 0.5 * RWKV_A_LORA ** -0.5 * nrm(ks[13], (L, RWKV_A_LORA, W), f32),
        "rwkv_k_k": 0.85 + 0.05 * nrm(ks[14], (L, W), f32),
        "rwkv_k_a": 1.0 + 0.05 * nrm(ks[15], (L, W), f32),
        "rwkv_r_k": 0.1 * nrm(ks[16], (L, RWKV_HEADS, RWKV_HEAD_DIM), f32),
        "rwkv_ln_w": 1.0 + 0.05 * nrm(ks[17], (L, W), f32),
        "rwkv_ln_b": 0.01 * nrm(ks[18], (L, W), f32),
        "w_branch": W ** -0.5 * nrm(ks[19], (L, N_BRANCHES, W, D), f32),
        "w_out": D ** -0.5 * nrm(ks[20], (L, D, D), f32),
        "final_g": 1.0 + 0.05 * nrm(ks[21], (D,), f32),
    }

def first_block(x, c, positions, norm_g, w_ada, b_ada, w_in, pool_w, pool_scale, ret_norm_g,
              rwkv_shift_mu, rwkv_w0, rwkv_w2, rwkv_a0, rwkv_a2, rwkv_k_k, rwkv_k_a,
              rwkv_r_k, rwkv_ln_w, rwkv_ln_b, w_branch, w_out, final_g):
    c_act = jax.nn.silu(c)
    for l in range(DEPTH):
        x = hybrid_layer(x, c_act, positions, norm_g[l], w_ada[l], b_ada[l], w_in[l],
                         pool_w[l], pool_scale[l], ret_norm_g[l], rwkv_shift_mu[l],
                         rwkv_w0[l], rwkv_w2[l], rwkv_a0[l], rwkv_a2[l], rwkv_k_k[l],
                         rwkv_k_a[l], rwkv_r_k[l], rwkv_ln_w[l], rwkv_ln_b[l],
                         w_branch[l], w_out[l])
    return rms_norm(x, final_g)


DEPTH_2 = 1

HEAD_DIM = 64
N_HEADS_DIL = 8
N_HEADS_FOX = 8
D_DIL = N_HEADS_DIL * HEAD_DIM
D_FOX = N_HEADS_FOX * HEAD_DIM
D_MIX = D_DIL + D_FOX
D_IN_2 = 3 * D_DIL + 3 * D_FOX + N_HEADS_FOX
DILATED_BRANCHES = ((128, 1), (512, 4), (2048, 16))
SEG = 128
BLOCK_Q = 128
N_BUCKETS = 32
MAX_DISTANCE = 2048
N_GROUPS = 4
EXPERTS_PER_GROUP = 8
N_EXPERTS = N_GROUPS * EXPERTS_PER_GROUP
TOP_K_IN_GROUP = 2
D_EXPERT = 256
EPS = 1e-6
SCALE = HEAD_DIM ** -0.5
NEG_INF = -1e30


def _rmsnorm(x, g):
    x32 = x.astype(jnp.float32)
    y = x32 * lax.rsqrt(jnp.mean(x32 * x32, axis=-1, keepdims=True) + EPS)
    return (y * g.astype(jnp.float32)).astype(x.dtype)

def _t5_bucket(dist):
    max_exact = N_BUCKETS // 2
    d32 = jnp.maximum(dist, 1).astype(jnp.float32)
    large = max_exact + (jnp.log(d32 / max_exact) / math.log(MAX_DISTANCE / max_exact)
                         * (N_BUCKETS - max_exact)).astype(jnp.int32)
    large = jnp.minimum(large, N_BUCKETS - 1)
    return jnp.where(dist < max_exact, dist, large)

def _dilated_branch(q, k, v, rel_bias, dilation):
    B, T, H, Dh = q.shape
    L = T // dilation
    nb = -(-L // SEG)
    L_pad = nb * SEG

    def to_sub(a):
        a = a.reshape(B, L, dilation, H, Dh).transpose(0, 2, 1, 3, 4)
        a = jnp.pad(a, ((0, 0), (0, 0), (0, L_pad - L), (0, 0), (0, 0)))
        return a.reshape(B, dilation, nb, SEG, H, Dh)

    qs, ks, vs = to_sub(q), to_sub(k), to_sub(v)

    def with_prev(a):
        prev = jnp.pad(a, ((0, 0), (0, 0), (1, 0), (0, 0), (0, 0), (0, 0)))[:, :, :-1]
        return jnp.concatenate([prev, a], axis=3)

    kk, vv = with_prev(ks), with_prev(vs)

    i = jnp.arange(SEG)[:, None]
    j = jnp.arange(2 * SEG)[None, :]
    m = i - j + SEG
    band = (m >= 0) & (m <= SEG)
    bias = rel_bias[_t5_bucket(jnp.clip(m, 0, SEG) * dilation)]
    bias = bias.transpose(2, 0, 1).astype(jnp.float32)
    blk = jnp.arange(nb)[:, None, None]
    valid = band[None] & (blk * SEG - SEG + j[None] >= 0)

    s = jnp.einsum('brnqhd,brnkhd->brnhqk', qs, kk,
                   preferred_element_type=jnp.float32) * SCALE + bias
    s = jnp.where(valid[:, None], s, NEG_INF)
    mx = jnp.max(s, axis=-1, keepdims=True)
    p = jnp.exp(s - mx)
    den = jnp.sum(p, axis=-1, keepdims=True)
    o = jnp.einsum('brnhqk,brnkhd->brnqhd', (p / den).astype(v.dtype), vv)
    lse = (mx + jnp.log(den))[..., 0].transpose(0, 1, 2, 4, 3)

    def from_sub(a):
        a = a.reshape(B, dilation, L_pad, *a.shape[4:])[:, :, :L]
        a = jnp.moveaxis(a, 1, 2)
        return a.reshape(B, T, *a.shape[3:])

    return from_sub(o), from_sub(lse)

def _dilated_attention(q, k, v, rel_bias):
    outs, lses = [], []
    for _, dilation in DILATED_BRANCHES:
        o, l = _dilated_branch(q, k, v, rel_bias, dilation)
        outs.append(o)
        lses.append(l)
    w = jax.nn.softmax(jnp.stack(lses), axis=0)
    return jnp.einsum('gbth,gbthd->bthd', w.astype(q.dtype), jnp.stack(outs))

def _forgetting_attention(q, k, v, log_f):
    B, T, H, Dh = q.shape
    nq = T // BLOCK_Q
    c = jnp.cumsum(log_f, axis=1)
    c_k = c.transpose(0, 2, 1)
    k_pos = jnp.arange(T)
    qb = q.reshape(B, nq, BLOCK_Q, H, Dh).transpose(1, 0, 2, 3, 4)
    cb = c.reshape(B, nq, BLOCK_Q, H).transpose(1, 0, 3, 2)
    starts = jnp.arange(nq) * BLOCK_Q

    def block(args):
        qi, ci, t0 = args
        s = jnp.einsum('bqhd,bkhd->bhqk', qi, k, preferred_element_type=jnp.float32) * SCALE
        s = s + ci[..., None] - c_k[:, :, None, :]
        q_pos = t0 + jnp.arange(BLOCK_Q)
        s = jnp.where(k_pos[None, :] <= q_pos[:, None], s, NEG_INF)
        p = jax.nn.softmax(s, axis=-1)
        return jnp.einsum('bhqk,bkhd->bqhd', p.astype(v.dtype), v)

    o = lax.map(block, (qb, cb, starts))
    return o.transpose(1, 0, 2, 3, 4).reshape(B, T, H, Dh)

def _hierarchical_moe(xt, w_rg, b_rg, w_re, b_re, w_gate, w_up, w_down):
    N = xt.shape[0]
    group_logits = (xt @ w_rg + b_rg).astype(jnp.float32)
    group_probs = jax.nn.softmax(group_logits, axis=-1)
    g1, g_idx = lax.top_k(group_probs, 1)
    expert_logits = (xt @ w_re + b_re).astype(jnp.float32).reshape(N, N_GROUPS, EXPERTS_PER_GROUP)
    sel = jnp.take_along_axis(expert_logits, g_idx[:, :, None], axis=1)[:, 0]
    top_v, top_i = lax.top_k(sel, TOP_K_IN_GROUP)
    g2 = jax.nn.softmax(top_v, axis=-1)
    expert_id = g_idx * EXPERTS_PER_GROUP + top_i
    combine = jnp.sum(jax.nn.one_hot(expert_id, N_EXPERTS, dtype=jnp.float32)
                      * (g1 * g2)[..., None], axis=1).astype(xt.dtype)
    y = jnp.zeros_like(xt)
    for e in range(N_EXPERTS):
        he = jax.nn.silu(xt @ w_gate[e]) * (xt @ w_up[e])
        y = y + combine[:, e:e + 1] * (he @ w_down[e])
    return y

def second_inputs(seed: int = 0) -> dict:
    key = jax.random.key(seed)
    ks = jax.random.split(key, 20)
    f32 = jnp.float32
    nrm = lambda k, shape, s: jax.random.normal(k, shape, f32) * s
    return {
        "x": nrm(ks[0], (BATCH, SEQ, D_MODEL), 1.0),
        "w_in": nrm(ks[1], (DEPTH_2, D_MODEL, D_IN_2), D_MODEL ** -0.5),
        "b_forget": 2.0 + nrm(ks[2], (DEPTH_2, N_HEADS_FOX), 0.5),
        "attn_norm": 1.0 + nrm(ks[3], (DEPTH_2, D_MODEL), 0.02),
        "out_norm_dil": 1.0 + nrm(ks[4], (DEPTH_2, D_DIL), 0.02),
        "out_norm_fox": 1.0 + nrm(ks[5], (DEPTH_2, D_FOX), 0.02),
        "w_out": nrm(ks[6], (DEPTH_2, D_MIX, D_MODEL), D_MIX ** -0.5),
        "ffn_norm": 1.0 + nrm(ks[7], (DEPTH_2, D_MODEL), 0.02),
        "w_router_group": nrm(ks[8], (DEPTH_2, D_MODEL, N_GROUPS), D_MODEL ** -0.5),
        "b_router_group": nrm(ks[9], (DEPTH_2, N_GROUPS), 0.01),
        "w_router_expert": nrm(ks[10], (DEPTH_2, D_MODEL, N_EXPERTS), D_MODEL ** -0.5),
        "b_router_expert": nrm(ks[11], (DEPTH_2, N_EXPERTS), 0.01),
        "w_expert_gate": nrm(ks[12], (DEPTH_2, N_EXPERTS, D_MODEL, D_EXPERT), D_MODEL ** -0.5),
        "w_expert_up": nrm(ks[13], (DEPTH_2, N_EXPERTS, D_MODEL, D_EXPERT), D_MODEL ** -0.5),
        "w_expert_down": nrm(ks[14], (DEPTH_2, N_EXPERTS, D_EXPERT, D_MODEL), D_EXPERT ** -0.5),
        "rel_bias": nrm(ks[15], (N_BUCKETS, N_HEADS_DIL), 0.5),
        "final_norm": 1.0 + nrm(ks[16], (D_MODEL,), 0.02),
    }

def second_block(x, w_in, b_forget, attn_norm, out_norm_dil, out_norm_fox, w_out, ffn_norm,
              w_router_group, b_router_group, w_router_expert, b_router_expert,
              w_expert_gate, w_expert_up, w_expert_down, rel_bias, final_norm):
    B, T, D = x.shape
    splits = [D_DIL, 2 * D_DIL, 3 * D_DIL, 3 * D_DIL + D_FOX, 3 * D_DIL + 2 * D_FOX,
              3 * D_DIL + 3 * D_FOX]
    for layer in range(DEPTH_2):
        h = _rmsnorm(x, attn_norm[layer])
        proj = h @ w_in[layer]
        qa, ka, va, qf, kf, vf, f_pre = jnp.split(proj, splits, axis=-1)
        heads = lambda a, n: a.reshape(B, T, n, HEAD_DIM)
        o_dil = _dilated_attention(heads(qa, N_HEADS_DIL), heads(ka, N_HEADS_DIL),
                                   heads(va, N_HEADS_DIL), rel_bias)
        log_f = jax.nn.log_sigmoid((f_pre + b_forget[layer]).astype(jnp.float32))
        o_fox = _forgetting_attention(heads(qf, N_HEADS_FOX), heads(kf, N_HEADS_FOX),
                                      heads(vf, N_HEADS_FOX), log_f)
        o_dil = _rmsnorm(o_dil.reshape(B, T, D_DIL), out_norm_dil[layer])
        o_fox = _rmsnorm(o_fox.reshape(B, T, D_FOX), out_norm_fox[layer])
        x = x + jnp.concatenate([o_dil, o_fox], axis=-1) @ w_out[layer]
        h2 = _rmsnorm(x, ffn_norm[layer]).reshape(B * T, D)
        y = _hierarchical_moe(h2, w_router_group[layer], b_router_group[layer],
                              w_router_expert[layer], b_router_expert[layer],
                              w_expert_gate[layer], w_expert_up[layer], w_expert_down[layer])
        x = x + y.reshape(B, T, D)
    return _rmsnorm(x, final_norm)


def setup_inputs(seed=0):
    out = dict(first_inputs(seed))
    for name, value in second_inputs(seed + 1).items():
        if name != "x":
            out[name + "_2"] = value
    return out


def reference(
    x, c, positions, norm_g, w_ada, b_ada, w_in, pool_w, pool_scale, ret_norm_g, rwkv_shift_mu,
    rwkv_w0, rwkv_w2, rwkv_a0, rwkv_a2, rwkv_k_k, rwkv_k_a, rwkv_r_k, rwkv_ln_w, rwkv_ln_b,
    w_branch, w_out, final_g, w_in_2, b_forget_2, attn_norm_2, out_norm_dil_2, out_norm_fox_2,
    w_out_2, ffn_norm_2, w_router_group_2, b_router_group_2, w_router_expert_2,
    b_router_expert_2, w_expert_gate_2, w_expert_up_2, w_expert_down_2, rel_bias_2,
    final_norm_2,
):
    x = first_block(
        x, c, positions, norm_g, w_ada, b_ada, w_in, pool_w, pool_scale, ret_norm_g,
        rwkv_shift_mu, rwkv_w0, rwkv_w2, rwkv_a0, rwkv_a2, rwkv_k_k, rwkv_k_a, rwkv_r_k,
        rwkv_ln_w, rwkv_ln_b, w_branch, w_out, final_g,
    )
    return second_block(
        x, w_in_2, b_forget_2, attn_norm_2, out_norm_dil_2, out_norm_fox_2, w_out_2, ffn_norm_2,
        w_router_group_2, b_router_group_2, w_router_expert_2, b_router_expert_2,
        w_expert_gate_2, w_expert_up_2, w_expert_down_2, rel_bias_2, final_norm_2,
    )


_drawn_inputs = setup_inputs


def setup_inputs(seed=0):
    import zlib

    import numpy as np

    out = dict(_drawn_inputs(seed))
    spreads = {}
    factors = {'ret_norm_g': 3.015,
     'rwkv_w2': 4.266,
     'rwkv_a0': 3.454,
     'rwkv_ln_w': 3.297,
     'rwkv_ln_b': 8.0,
     'out_norm_dil_2': 3.667,
     'out_norm_fox_2': 2.961,
     'ffn_norm_2': 3.028,
     'b_router_group_2': 4.818,
     'b_router_expert_2': 8.0,
     'final_norm_2': 2.722}
    for name, (base, spread) in spreads.items():
        noise = np.random.default_rng([zlib.crc32(name.encode()), seed]).standard_normal(out[name].shape)
        drawn = base * np.exp(spread * noise) if base else spread * noise
        out[name] = __import__('jax').numpy.asarray(drawn.astype(out[name].dtype))
    for name, factor in factors.items():
        out[name] = (out[name] * factor).astype(out[name].dtype)
    return out
```

```python
import math
from contextlib import ExitStack

import numpy as np

import concourse.bass as bass
from concourse import mybir

F32 = mybir.dt.float32
I32 = mybir.dt.int32
ALU = mybir.AluOpType
ACT = mybir.ActivationFunctionType
AX_X = mybir.AxisListType.X

P = 128
T = 512
NT = T // P
D = 1024
KD = D // P
W = 512
CW = W // P
LAYERS = 2
RET_H, RET_D = 4, 128
RW_H, RW_D = 8, 64
WINDOWS = (2, 4, 8, 16)
RMS_EPS = 1e-6
RET_EPS = 1e-5
RW_EPS = 64e-5
DECAY = -math.exp(-0.5)
OFF = -DECAY * P / 2
LEVELS = tuple(2 ** i for i in range(1, 7))
FOX_H = DIL_H = 8
HD = 64
ATT_SCALE = HD ** -0.5
NEG = -1e30
DIL_ROW = T + P
BUCKETS, MAX_DISTANCE = 32, 2048
DILATIONS, SEG = (1, 4, 16), 128

GROUPS, PER_GROUP, TOP_K, FF = 4, 8, 2, 256
EXPERTS = GROUPS * PER_GROUP
ROUTE = GROUPS + EXPERTS
SLOT = 128
UNROLL = 3
TILES = (T * TOP_K + EXPERTS * (SLOT - 1)) // SLOT
TILES = -(-TILES // UNROLL) * UNROLL
W_EXP = KD * 2 * FF + 2 * D

BLK = KD * 2 * P
RING = 4
ADA_B, PROJ_B, MERGE_B, OUT_B = 12, 20, 20, 4
LAYER_B = ADA_B + PROJ_B + MERGE_B + OUT_B
ATT_B = 12 + 4

_names = [("norm_g", 8), ("b_ada", 24), ("pool_scale", 4), ("ret_norm_g", 4), ("mu", 13), ("w0", 4), ("a0", 4),
          ("k_k", 4), ("k_a", 4), ("r_k", 4), ("ln_w", 4), ("ln_b", 4), ("pool_w", 4 * P), ("lora", W),
          ("w_lora", KD * P)]
PCOL, NPAR = {}, 0
for _n, _w in _names:
    PCOL[_n] = (NPAR, NPAR + _w)
    NPAR += _w

_names = [("c", 8), ("final_g", 8), ("attn_norm", 8), ("out_norm", 8), ("ffn_norm", 8), ("w_f", KD * 8), ("w_route", KD * 36), ("b_route", 36),
          ("b_forget", 1), ("rel", 8)]
GCOL, NGLOB = {}, 0
for _n, _w in _names:
    GCOL[_n] = (NGLOB, NGLOB + _w)
    NGLOB += _w

_names = [("ident", P), ("blk64", P), ("mean", P), ("ones", P), ("gram", W), ("lvl", 6 * P), ("lvl1", 2 * P),
          ("ret_mask", W), ("ret_q", W), ("ret_k", 4), ("freq", 64), ("inv_count", 64), ("off", 2), ("causal", P),
          ("iota", 64), ("rev", 8)]
CCOL, NCONST = {}, 0
for _n, _w in _names:
    CCOL[_n] = (NCONST, NCONST + _w)
    NCONST += _w


def constants():
    i = np.arange(P)
    row, col = i[:, None], i[None, :]
    out = np.zeros((P, NCONST), np.float32)

    def put(name, a):
        out[:, CCOL[name][0]:CCOL[name][1]] = a

    put("ident", np.eye(P))
    put("blk64", row // RW_D == col // RW_D)
    put("mean", np.full((P, P), 1.0 / D))
    put("ones", np.ones((P, P)))
    strict, incl = row < col, row <= col
    put("gram", np.concatenate([strict, incl, strict, incl], 1))
    put("lvl", np.concatenate([((row // b) % 2 == 1) & (col // b == row // b - 1) for b in LEVELS], 1))
    pair = (row % 2 == 0) & (col == row + 1)
    put("lvl1", np.concatenate([pair, pair.T], 1))
    log_gamma = np.log1p(-(2.0 ** (-5.0 - np.arange(RET_H))))
    scale = RET_D ** -0.5
    put("ret_mask", np.concatenate([np.where(incl, np.exp(g * np.maximum(col - row, 0)), 0) * scale
                                    for g in log_gamma], 1))
    put("ret_q", np.concatenate([np.exp(g * (col + 1.0)) + 0 * row for g in log_gamma], 1))
    put("ret_k", np.stack([np.exp(g * (P - 1 - i)) * scale for g in log_gamma], 1))
    put("freq", (np.float32(10000.0) ** (-np.arange(64, dtype=np.float32) / np.float32(64)))[None, :])
    t = np.arange(16)
    put("inv_count", np.concatenate([1.0 / np.minimum(t + 1, w) for w in WINDOWS])[None, :])
    put("off", np.array([OFF, -OFF])[None, :])
    put("causal", np.where(col <= row, 0.0, NEG))
    put("iota", np.arange(64)[None, :])
    put("rev", 8.0 - np.arange(8)[None, :])
    return out


def distance_table():
    dist = T - 1 - np.arange(DIL_ROW)
    d = np.maximum(dist, 0)
    exact = BUCKETS // 2
    log = np.log(np.maximum(d, 1).astype(np.float32) / np.float32(exact)) / np.float32(math.log(MAX_DISTANCE / exact))
    large = np.minimum(exact + (log * np.float32(BUCKETS - exact)).astype(np.int32), BUCKETS - 1)
    bucket = np.where(d < exact, d, large)
    count = sum(((dist >= 0) & (dist % r == 0) & (dist // r <= SEG)).astype(np.int32) for r in DILATIONS)
    out = np.zeros((BUCKETS + 1, DIL_ROW), np.float32)
    out[bucket, np.arange(DIL_ROW)] = dist >= 0
    out[BUCKETS] = np.where(count > 0, np.log(np.maximum(count, 1)), NEG)
    return out


def program(nc, wstream, lparams, gparams, consts, distances, experts, last_norm, x_in, pos_in, out):
    with ExitStack() as ctx:
        def sb(name, shape, dt=F32):
            return ctx.enter_context(nc.sbuf_tensor(name, shape, dt))

        SEM, PER, given = {}, {}, {}

        def sem(name, per=1):
            SEM[name] = ctx.enter_context(nc.semaphore(name))
            PER[name] = per

        def inc(ins, name, by=1):
            given[name] = given.get(name, 0) + by
            ins.then_inc(SEM[name], by)

        wring = sb("wring", [P, RING, KD, 2 * P])
        xT = sb("xT", [P, KD, T])
        hT = sb("hT", [P, KD, T])
        lpar = sb("lpar", [P, NPAR])
        gpar = sb("gpar", [P, NGLOB])
        cst = sb("cst", [P, NCONST])
        slots = sb("slots", [P, 9, CW, T])
        br_pool = sb("br_pool", [P, CW, T])
        gm_mem = sb("gm_mem", [P, 4096])
        ztp = sb("ztp", [P, 3, 8, P])
        w_sb = sb("w_sb", [P, T])
        u_sb = sb("u_sb", [P, T])
        state = sb("state", [P, CW, P])
        rstd = sb("rstd", [P, T])
        mod = sb("mod", [P, 24])
        gs = sb("gs", [P, KD])
        omm = sb("omm", [P, 13 + CW])
        e_end = sb("e_end", [P, CW, NT])
        c_act = sb("c_act", [P, KD])
        posi = sb("posi", [P, NT], I32)
        posf = sb("posf", [P, NT])
        cosT = sb("cosT", [P, NT, 64])
        sinT = sb("sinT", [P, NT, 64])
        hsum = sb("hsum", [P, 32])
        hvar = sb("hvar", [P, 32])
        slot_idx = sb("slot_idx", [P, TOP_K, NT], I32)
        tile_exp = sb("tile_exp", [P, TILES], I32)
        dram = lambda name, shape: nc.dram_tensor(name, shape, F32).ap()
        dil_rows = dram("dil_rows", (DIL_H, P * DIL_ROW))
        x_slots = dram("x_slots", (TILES * SLOT, D))
        y_slots = dram("y_slots", (TILES * SLOT, D))
        banks = ctx.enter_context(nc.psum_tensor("banks", [P, 8, T], F32))

        def par(name, c=None):
            a, b = PCOL[name]
            return lpar[:, a:b] if c is None else lpar[:, a + c:a + c + 1]

        def glob(name, c=None):
            a, b = GCOL[name]
            return gpar[:, a:b] if c is None else gpar[:, a + c:a + c + 1]

        def con(name, c=None):
            a, b = CCOL[name]
            return cst[:, a:b] if c is None else cst[:, a + c:a + c + 1]

        ident = con("ident")
        SL = [slots[:, i] for i in range(9)]
        R_, K_, X1, X2, X3, G_, V_, A_, KK = SL
        gm = gm_mem[:, :].rearrange("p (u k t) -> p u k t", u=8, k=4)
        zt, tt, pt = ztp[:, 0], ztp[:, 1], ztp[:, 2]
        b_tok, v_tok, k_tok, y_tok = (s.rearrange("p n f -> p n f") for s in (X1, G_, V_, X2))
        pool_u = gm_mem[:, 0:2048].rearrange("p (c t) -> p c t", c=CW)
        pool_gate = gm_mem[:, 2048:4096].rearrange("p (c t) -> p c t", c=CW)
        br_rwkv = R_
        rq_raw, rk_raw, rv_tok, ret_gate = X1, V_, KK, K_
        rq_rot, rk_rot, qT, qdT = X2, G_, X3, A_
        kT = gm_mem[:, 0:2048].rearrange("p (h t) -> p h t", h=RET_H)
        rot_tmp = [gm_mem[:, 2048 + 1024 * i:3072 + 1024 * i] for i in range(2)]
        k_tail, o_tok, br_ret, o_sq = X1, V_, X2, G_
        p_ret = [tt.rearrange("p (b h) t -> p b (h t)", b=2)[:, i] for i in range(2)]
        sig_gate = slots[:, 6:9].rearrange("p s c t -> p (s c) t")
        mT = gm_mem[:, :].rearrange("p (c t) -> p c t", c=KD)

        jobs = []

        def job(name, drained, k):
            jobs.append((name, drained, k))

        job("mod", "mod_ready", 1)
        job("ss", "rms_ready", 1)
        for c in range(CW):
            job(f"r{c}", "mixed", 1 + c)
        job("wl", "mixed", 5)
        for c in range(CW):
            job(f"z{c}", "g_ready", 1 + c)
        for c in range(CW):
            job(f"a{c}", "a_ready", 1 + c)
        for c in range(CW):
            job(f"k{c}", "mixed", 6 + c)
        for c in range(CW):
            job(f"v{c}", "mixed", 10 + c)
        for c in range(CW):
            job(f"pu{c}", "pu_ready", 1 + c)
        for c in range(CW):
            job(f"kss{c}", "kss_ready", 1 + c)
        for c in range(CW):
            job(f"pg{c}", "pg_ready", 1 + c)
        for c in range(CW):
            job(f"py{c}", "pool_done", 1 + c)
        for c in range(CW):
            job(f"bs{c}", "bonus_ready", 1 + c)
        for i, what in enumerate("vbk"):
            for n in range(NT):
                job(f"t{what}{n}", "tok_ready", 1 + NT * i + n)
        for n in range(NT):
            for h in range(RW_H):
                job(f"gram{n}{h}", "gram_ready", 1 + 8 * n + h)
            for g in range(2):
                job(f"ti{n}{g}", "tinit_ready", 1 + 2 * n + g)
            for l in range(6):
                for g in range(2):
                    job(f"p{n}{l}{g}", "p_ready", 1 + 12 * n + 2 * l + g)
                for g in range(2):
                    if l < 5:
                        job(f"tn{n}{l}{g}", "t_ready", 1 + 10 * n + 2 * l + g)
                    job(f"zn{n}{l}{g}", "z_ready", 3 + 14 * n + 2 * l + g)
            job(f"w{n}", "w_ready", 1 + n)
            job(f"u{n}", "u_ready", 1 + n)
            job(f"y{n}", "y_ready", 1 + n)
            if n < NT - 1:
                job(f"s{n}", "s_added", 1 + n)
        for c in range(CW):
            job(f"rg{c}", "rg_ready", 1 + c)
        for i, what in enumerate("qkv"):
            for b in range(2):
                for tp in range(2):
                    job(f"ret{what}{b}{tp}", "ret_tok", 1 + 4 * i + 2 * b + tp)
        for c in range(CW):
            job(f"tg{c}", "retg_ready", 1 + c)
        for c in range(CW):
            job(f"ty{c}", "y_scaled", 1 + c)
        for h in range(RET_H):
            job(f"tq{h}", "qd_ready", 1 + h)
        for h in range(RET_H):
            job(f"tkr{h}", "kT_ready", 1 + h)
        for n in range(NT):
            job(f"sc{n}", "pret_ready", 1 + n)
            job(f"o{n}", "o_ready", 1 + n)
            if n < NT - 1:
                job(f"kv{n}", "R_ready", 1 + n)
        for h in range(RET_H):
            job(f"to{h}", "ret_done", 1 + h)
        for cp in range(KD // 2):
            for n in range(3):
                for cc in range(2):
                    job(f"g{cp}{n}{cc}", "gate_sig", 1 + 6 * cp + 2 * n + cc)
            for cc in range(2):
                for n in range(3):
                    job(f"b{cp}{cc}{n}", "merged", 1 + 5 * (2 * cp + cc) + (0, 1, 3)[n])
        for c in range(KD):
            job(f"wo{c}", "x_done", 1 + c)
        NJ = len(jobs)
        JOB = {name: j for j, (name, _, _) in enumerate(jobs)}
        block_end = (["mod"] * ADA_B + ["r1", "r3", "k1", "k3", "v1", "v3", "pu1", "pu3", "pg1", "pg3", "rg1", "rg3"]
                     + [f"ret{w}{b}1" for w in "qkv" for b in range(2)] + ["tg1", "tg3"])
        for cp in range(KD // 2):
            block_end += [f"g{cp}{n}1" for n in range(3)] + [f"b{cp}{cc}2" for cc in range(2)]
        block_end += [f"wo{c}" for c in range(1, KD, 2)]
        assert len(block_end) == LAYER_B
        FIRST = {"r": ADA_B, "k": ADA_B + 2, "v": ADA_B + 4, "pu": ADA_B + 6, "pg": ADA_B + 8, "rg": ADA_B + 10,
                 "retq": ADA_B + 12, "retk": ADA_B + 14, "retv": ADA_B + 16, "tg": ADA_B + 18,
                 "merge": ADA_B + PROJ_B, "wo": ADA_B + PROJ_B + MERGE_B}

        for s in range(RING):
            sem(f"wload{s}", 16 * LAYER_B // RING)
        for name in ("x_loaded", "const_loaded", "glob_loaded", "pos_loaded", "stored"):
            sem(name)
        sem("c_ready")
        sem("rope_step")
        sem("rope_arg")
        sem("rope_ready")
        LAYER_SEMS = []
        for name, per in (("bank_full", NJ), ("params_loaded", 16), ("x_done", 8), ("ada_used", 11), ("mod_ready", 1), ("gs_ready", 3), ("xsq_ready", 8), ("rms_ready", 2), ("rms_sqrt", 1),
                          ("h_scaled", 8), ("h_ready", 8), ("mix_scaled", 13), ("mixed", 13), ("wl_tanh", 1),
                          ("g_ready", 4), ("a_ready", 4), ("kk_ready", 2), ("kss_ready", 4), ("kss_sqrt", 1),
                          ("k_mod", 2), ("rk_ready", 1), ("kk_unit", 2), ("bonus_ready", 4),
                          ("pu_ready", 4), ("pg_ready", 4), ("pool_step", 10 * 2 + 4 * 4), ("pool_d", 4),
                          ("pool_done", 4), ("g_sum", 1), ("g_prev", 1), ("exp_prev", 1), ("exp_plus", 1),
                          ("exp_minus", 1), ("ar_ready", 2), ("bk_ready", 2), ("tok_ready", 12),
                          ("gram_ready", 32), ("z_masked", 8), ("tinit_ready", 8), ("p_ready", 48),
                          ("t_ready", 40), ("z_ready", 56), ("w_ready", 4), ("u_ready", 4), ("y_ready", 4),
                          ("s_added", 3), ("s_ready", 3), ("y_norm", 7), ("y_sqrt", 1), ("y_scaled", 4),
                          ("y_bonus", 4), ("rwkv_done", 4), ("rg_ready", 4), ("ret_tok", 12), ("retg_ready", 4),
                          ("rot_step", 6), ("rot_ready", 2), ("qT_ready", 4), ("qd_ready", 4), ("kT_ready", 4),
                          ("ktail_ready", 1), ("pret_ready", 4), ("o_ready", 4), ("R_ready", 3), ("o_norm", 7),
                          ("o_sqrt", 1), ("ret_done", 4), ("gate_sig", 24), ("merged", 40)):
            sem(name, per)
            LAYER_SEMS.append(name)

        with nc.Block() as block:
            @block.sync
            def _(sp):
                def load_block(slot, index):
                    inc(sp.dma_start(wring[:, slot].rearrange("p k n -> p (k n)"),
                                     wstream[index].rearrange("a p n -> (a p) n")), f"wload{slot}", 16)

                sp.dma_start(cst[:, :], consts).then_inc(SEM["const_loaded"], 16)
                sp.dma_start(xT[:, :, :].rearrange("p k t -> p (k t)"), x_in).then_inc(SEM["x_loaded"], 16)
                sp.dma_start(gpar[:, :], gparams).then_inc(SEM["glob_loaded"], 16)
                sp.dma_start(posi[:, :], pos_in).then_inc(SEM["pos_loaded"], 16)
                for b in range(RING):
                    load_block(b, slice(b, b + 1))

            @block.scalar
            def _(act):
                act.wait_ge(SEM["const_loaded"], 16)
                act.wait_ge(SEM["glob_loaded"], 16)
                inc(nc.scalar.activation(c_act[:, :], glob("c"), ACT.Silu), "c_ready")
                act.wait_ge(SEM["rope_arg"], 1)
                nc.scalar.activation(sinT[:, :, :], sinT[:, :, :], ACT.Sin)
                inc(nc.scalar.activation(cosT[:, :, :], cosT[:, :, :], ACT.Sin), "rope_ready")
                act.wait_ge(SEM["x_loaded"], 16)

            @block.vector
            def _(dve):
                v = nc.vector
                dve.wait_ge(SEM["const_loaded"], 16)
                dve.wait_ge(SEM["pos_loaded"], 16)
                n_rope = [0]

                def rope(ins):
                    n_rope[0] += 1
                    ins.then_inc(SEM["rope_step"], 1)
                    dve.wait_ge(SEM["rope_step"], n_rope[0])

                ang, turns = cosT[:, :, :], sinT[:, :, :]
                rope(v.tensor_copy(posf[:, :], posi[:, :]))
                for n in range(NT):
                    last = v.tensor_scalar(cosT[:, n, :], con("freq"), posf[:, n:n + 1], None, ALU.mult)
                rope(last)
                MAGIC = 1.5 * 2.0 ** 23
                rope(v.tensor_scalar(turns, ang, 1.0 / (2 * math.pi), None, ALU.mult))
                rope(v.tensor_scalar(turns, turns, MAGIC, None, ALU.add))
                rope(v.tensor_scalar(turns, turns, MAGIC, None, ALU.subtract))
                c1 = 6.28125
                c2 = math.floor((2 * math.pi - c1) * 2 ** 20) / 2 ** 20
                for part in (c1, c2, 2 * math.pi - c1 - c2):
                    rope(v.scalar_tensor_tensor(ang, turns, -part, ang, ALU.mult, ALU.add))
                rope(v.tensor_scalar(turns, ang, math.pi - 1e-6, -(math.pi - 1e-6), ALU.min, ALU.max))
                rope(v.scalar_tensor_tensor(ang, turns, -1.0, turns, ALU.mult, ALU.max))
                v.tensor_scalar(ang, ang, -1.0, math.pi / 2, ALU.mult, ALU.add).then_inc(SEM["rope_arg"], 1)
                dve.wait_ge(SEM["x_loaded"], 16)
                dve.wait_ge(SEM["rope_ready"], 1)

        with nc.Fori(0, LAYERS) as L:
          with nc.Block() as block:
            @block.sync
            def _(sp):
                def load_block(slot, index):
                    inc(sp.dma_start(wring[:, slot].rearrange("p k n -> p (k n)"),
                                     wstream[index].rearrange("a p n -> (a p) n")), f"wload{slot}", 16)

                for b in range(LAYER_B):
                    if b < ADA_B - 1:
                        sp.wait_ge(SEM["ada_used"], b + 1)
                    else:
                        sp.wait_ge(SEM["bank_full"], JOB[block_end[b]] + 1)
                    load_block(b % RING, bass.ds(L * LAYER_B + (b + RING), 1))

            @block.tensor
            def _(pe):
                state_ = {"job": 0}

                def after(name, k=None):
                    pe.wait_ge(SEM[name], PER[name] if k is None else k)

                def open_bank(name):
                    j = state_["job"]
                    assert jobs[j][0] == name, (name, jobs[j])
                    if j >= 8:
                        after(*jobs[j - 8][1:])
                    state_["job"] = j + 1
                    return banks[:, j % 8]

                def full(mm):
                    inc(mm, "bank_full")

                def weights(b):
                    pe.wait_ge(SEM[f"wload{b % RING}"], L * PER[f"wload{b % RING}"] + 16 * (b // RING + 1))
                    return wring[:, b % RING]

                def project(prefix, first):
                    for c in range(CW):
                        if c % 2 == 0:
                            wb = weights(first + c // 2)
                        o = open_bank(f"{prefix}{c}")
                        for k in range(KD):
                            mm = nc.tensor.matmul(o, wb[:, k, (c % 2) * P:(c % 2 + 1) * P], hT[:, k, :],
                                                  start=(k == 0), stop=(k == KD - 1))
                        full(mm)

                def project_tok(prefix, first):
                    for b in range(2):
                        wb = weights(first + b)
                        for tp in range(2):
                            o = open_bank(f"{prefix}{b}{tp}")
                            for ti in range(2):
                                n = 2 * tp + ti
                                for k in range(KD):
                                    mm = nc.tensor.matmul(o[:, ti * 256:ti * 256 + 256], hT[:, k, n * P:n * P + P],
                                                          wb[:, k, :], start=(k == 0), stop=(k == KD - 1))
                            full(mm)

                def transposes(name, tiles):
                    o = open_bank(name)
                    for i, s in enumerate(tiles):
                        mm = nc.tensor.transpose(o[:, i * P:i * P + P], s, ident)
                    full(mm)

                o = open_bank("mod")
                for m in range(24):
                    if m % 2 == 0:
                        wb = weights(m // 2)
                    for k in range(KD):
                        mm = nc.tensor.matmul(o[:, m:m + 1], wb[:, k, (m % 2) * P:(m % 2 + 1) * P], c_act[:, k:k + 1],
                                              start=(k == 0), stop=(k == KD - 1))
                    if m % 2 == 1 and m < 23:
                        inc(mm, "ada_used")
                full(mm)
                o = open_bank("ss")
                for k in range(KD):
                    after("xsq_ready", k + 1)
                    mm = nc.tensor.matmul(o, con("mean"), hT[:, k, :], start=(k == 0), stop=(k == KD - 1))
                full(mm)
                after("h_ready")
                project("r", FIRST["r"])
                o = open_bank("wl")
                wl = par("w_lora").rearrange("p (k n) -> p k n", k=KD)
                for k in range(KD):
                    mm = nc.tensor.matmul(o, wl[:, k, :], hT[:, k, :], start=(k == 0), stop=(k == KD - 1))
                full(mm)
                after("wl_tanh")
                for name, p0 in (("z", 0), ("a", 64)):
                    for c in range(CW):
                        o = open_bank(f"{name}{c}")
                        full(nc.tensor.matmul(o, par("lora")[p0:p0 + 64, c * P:c * P + P], w_sb[p0:p0 + 64, :],
                                              start=True, stop=True))
                project("k", FIRST["k"])
                project("v", FIRST["v"])
                project("pu", FIRST["pu"])
                after("kk_ready")
                for c in range(CW):
                    o = open_bank(f"kss{c}")
                    full(nc.tensor.matmul(o, con("blk64"), X1[:, c, :], start=True, stop=True))
                project("pg", FIRST["pg"])
                for c in range(CW):
                    after("pool_d", c + 1)
                    o = open_bank(f"py{c}")
                    full(nc.tensor.matmul(o, par("pool_w")[:, c * P:c * P + P], pool_u[:, c, :], start=True, stop=True))
                after("rk_ready")
                for c in range(CW):
                    o = open_bank(f"bs{c}")
                    full(nc.tensor.matmul(o, con("blk64"), X3[:, c, :], start=True, stop=True))
                after("mixed")
                for n in range(NT):
                    transposes(f"tv{n}", [V_[:, c, n * P:n * P + P] for c in range(CW)])
                after("bk_ready", 1)
                for n in range(NT):
                    transposes(f"tb{n}", [A_[:, c, n * P:n * P + P] for c in range(CW)])
                after("bk_ready", 2)
                for n in range(NT):
                    transposes(f"tk{n}", [K_[:, c, n * P:n * P + P] for c in range(CW)])
                after("ar_ready")
                for n in range(NT):
                    t0 = n * P
                    for h in range(RW_H):
                        o = open_bank(f"gram{n}{h}")
                        p0, c = 64 * (h % 2), h // 2
                        for i, (lhs, rhs) in enumerate(((A_, KK), (A_, R_), (K_, KK), (K_, R_))):
                            mm = nc.tensor.matmul(o[:, i * P:i * P + P], lhs[p0:p0 + 64, c, t0:t0 + P],
                                                  rhs[p0:p0 + 64, c, t0:t0 + P], start=True, stop=True)
                        full(mm)
                    for g in range(2):
                        after("z_ready", 14 * n + 1 + g)
                        transposes(f"ti{n}{g}", [zt[:, u, :] for u in range(4 * g, 4 * g + 4)])
                    for l in range(6):
                        for g in range(2):
                            if l == 0:
                                after("tinit_ready", 2 * n + 1 + g)
                            else:
                                after("t_ready", 10 * n + 2 * (l - 1) + 1 + g)
                            o = open_bank(f"p{n}{l}{g}")
                            for i in range(4):
                                u = 4 * g + i
                                mm = nc.tensor.matmul(o[:, i * P:i * P + P], gm[:, u, 0, :], tt[:, u, :],
                                                      start=True, stop=True)
                            full(mm)
                        for g in range(2):
                            after("p_ready", 12 * n + 2 * l + 1 + g)
                            if l > 0:
                                after("z_ready", 14 * n + 2 * l + 1 + g)
                            if l < 5:
                                o = open_bank(f"tn{n}{l}{g}")
                                for i in range(4):
                                    u = 4 * g + i
                                    mm = nc.tensor.matmul(o[:, i * P:i * P + P], zt[:, u, :], pt[:, u, :],
                                                          start=True, stop=True)
                                full(mm)
                            o = open_bank(f"zn{n}{l}{g}")
                            for i in range(4):
                                u = 4 * g + i
                                mm = nc.tensor.matmul(o[:, i * P:i * P + P], pt[:, u, :], zt[:, u, :],
                                                      start=True, stop=True)
                            full(mm)
                    if n == 0:
                        after("tok_ready")
                    else:
                        after("s_ready", n)
                    o = open_bank(f"w{n}")
                    if n > 0:
                        for c in range(CW):
                            nc.tensor.matmul(o[:, c * P:c * P + P], KK[:, c, t0:t0 + P], state[:, c, :],
                                             start=(c == 0), stop=False, skip_group_check=True)
                    for h in range(RW_H):
                        mm = nc.tensor.matmul(o[:, h * 64:h * 64 + 64], gm[:, h, 2, :], v_tok[:, n, h * 64:h * 64 + 64],
                                              start=(n == 0 and h == 0), stop=(h == RW_H - 1), skip_group_check=True)
                    full(mm)
                    after("w_ready", n + 1)
                    after("z_ready", 14 * n + 14)
                    o = open_bank(f"u{n}")
                    for h in range(RW_H):
                        mm = nc.tensor.matmul(o[:, h * 64:h * 64 + 64], zt[:, h, :], w_sb[:, h * 64:h * 64 + 64],
                                              start=True, stop=True)
                    full(mm)
                    after("u_ready", n + 1)
                    o = open_bank(f"y{n}")
                    if n > 0:
                        for c in range(CW):
                            nc.tensor.matmul(o[:, c * P:c * P + P], R_[:, c, t0:t0 + P], state[:, c, :],
                                             start=(c == 0), stop=False, skip_group_check=True)
                    for h in range(RW_H):
                        cols = slice(h * 64, h * 64 + 64)
                        nc.tensor.matmul(o[:, cols], gm[:, h, 1, :], u_sb[:, cols],
                                         start=(n == 0 and h == 0), stop=False, skip_group_check=True)
                        mm = nc.tensor.matmul(o[:, cols], gm[:, h, 3, :], v_tok[:, n, cols],
                                              start=False, stop=(h == RW_H - 1), skip_group_check=True)
                    full(mm)
                    if n < NT - 1:
                        o = open_bank(f"s{n}")
                        for c in range(CW):
                            cols = slice(c * P, c * P + P)
                            nc.tensor.matmul(o[:, cols], b_tok[:, n, cols], u_sb[:, cols], start=True, stop=False)
                            mm = nc.tensor.matmul(o[:, cols], k_tok[:, n, cols], v_tok[:, n, cols],
                                                  start=False, stop=True)
                        full(mm)
                project("rg", FIRST["rg"])
                for what in "qkv":
                    project_tok(f"ret{what}", FIRST[f"ret{what}"])
                project("tg", FIRST["tg"])
                after("y_norm")
                for c in range(CW):
                    transposes(f"ty{c}", [y_tok[:, n, c * P:c * P + P] for n in range(NT)])
                after("rot_ready", 1)
                for h in range(RET_H):
                    transposes(f"tq{h}", [rq_rot[:, n, h * P:h * P + P] for n in range(NT)])
                after("rot_ready", 2)
                for h in range(RET_H):
                    transposes(f"tkr{h}", [rk_rot[:, n, h * P:h * P + P] for n in range(NT)])
                after("qd_ready")
                after("kT_ready")
                after("ktail_ready")
                for n in range(NT):
                    t0 = n * P
                    o = open_bank(f"sc{n}")
                    for h in range(RET_H):
                        mm = nc.tensor.matmul(o[:, h * P:h * P + P], kT[:, h, t0:t0 + P], qT[:, h, t0:t0 + P],
                                              start=True, stop=True)
                    full(mm)
                    after("pret_ready", n + 1)
                    if n > 0:
                        after("R_ready", n)
                    o = open_bank(f"o{n}")
                    for h in range(RET_H):
                        cols = slice(h * P, h * P + P)
                        mm = nc.tensor.matmul(o[:, cols], p_ret[n % 2][:, cols], rv_tok[:, n, cols],
                                              start=True, stop=(n == 0))
                        if n > 0:
                            mm = nc.tensor.matmul(o[:, cols], qdT[:, h, t0:t0 + P], state[:, h, :],
                                                  start=False, stop=True)
                    full(mm)
                    if n < NT - 1:
                        o = open_bank(f"kv{n}")
                        for h in range(RET_H):
                            cols = slice(h * P, h * P + P)
                            mm = nc.tensor.matmul(o[:, cols], k_tail[:, n, cols], rv_tok[:, n, cols],
                                                  start=True, stop=True)
                        full(mm)
                after("o_norm")
                for h in range(RET_H):
                    transposes(f"to{h}", [o_tok[:, n, h * P:h * P + P] for n in range(NT)])
                after("ret_done")
                after("rwkv_done")
                for cp in range(KD // 2):
                    first = FIRST["merge"] + 5 * cp
                    for n in range(3):
                        wb = weights(first + n)
                        for cc in range(2):
                            o = open_bank(f"g{cp}{n}{cc}")
                            for k in range(KD):
                                mm = nc.tensor.matmul(o, wb[:, k, cc * P:cc * P + P], hT[:, k, :],
                                                      start=(k == 0), stop=(k == KD - 1))
                            full(mm)
                    for cc in range(2):
                        wb = weights(first + 3 + cc).rearrange("p k n -> p (k n)")
                        for n, br in enumerate((br_pool, br_ret, br_rwkv)):
                            o = open_bank(f"b{cp}{cc}{n}")
                            for k in range(CW):
                                at = (n * CW + k) * P
                                mm = nc.tensor.matmul(o, wb[:, at:at + P], br[:, k, :], start=(k == 0), stop=(k == CW - 1))
                            full(mm)
                after("merged")
                for c in range(KD):
                    if c % 2 == 0:
                        wb = weights(FIRST["wo"] + c // 2)
                    o = open_bank(f"wo{c}")
                    for k in range(KD):
                        mm = nc.tensor.matmul(o, wb[:, k, (c % 2) * P:(c % 2 + 1) * P], mT[:, k, :],
                                              start=(k == 0), stop=(k == KD - 1))
                    full(mm)
                assert state_["job"] == NJ

            @block.scalar
            def _(act):
                def after(name, k=None):
                    act.wait_ge(SEM[name], PER[name] if k is None else k)

                def bank(name):
                    act.wait_ge(SEM["bank_full"], JOB[name] + 1)
                    return banks[:, JOB[name] % 8]

                act.dma_start(lpar[:, :], lparams[bass.ds(L, 1)].rearrange("a p n -> (a p) n")) \
                   .then_inc(SEM["params_loaded"], 16)
                for k in range(KD):
                    inc(nc.scalar.activation(hT[:, k, :], xT[:, k, :], ACT.Square), "xsq_ready")
                after("rms_ready", 1)
                inc(nc.scalar.activation(rstd[:, :], rstd[:, :], ACT.Sqrt), "rms_sqrt")
                for k in range(KD):
                    after("h_scaled", k + 1)
                    inc(nc.scalar.activation(hT[:, k, :], hT[:, k, :], ACT.Identity, bias=mod[:, k:k + 1]), "h_ready")
                after("gs_ready")
                after("params_loaded")
                for c in range(CW):
                    inc(nc.scalar.activation(R_[:, c, :], bank(f"r{c}"), ACT.Copy, scale=omm[:, c:c + 1]), "mix_scaled")
                inc(nc.scalar.activation(w_sb[:, :], bank("wl"), ACT.Copy, scale=omm[:, 4:5]), "mix_scaled")
                after("mixed", 5)
                inc(nc.scalar.activation(w_sb[0:64, :], w_sb[0:64, :], ACT.Tanh), "wl_tanh")
                for c in range(CW):
                    inc(nc.scalar.activation(G_[:, c, :], bank(f"z{c}"), ACT.Sigmoid, bias=par("w0", c)), "g_ready")
                for c in range(CW):
                    inc(nc.scalar.activation(A_[:, c, :], bank(f"a{c}"), ACT.Sigmoid, bias=par("a0", c)), "a_ready")
                for i, (z, name) in enumerate(((K_, "k"), (V_, "v"))):
                    for c in range(CW):
                        m = 5 + 4 * i + c
                        inc(nc.scalar.activation(z[:, c, :], bank(f"{name}{c}"), ACT.Copy, scale=omm[:, m:m + 1]),
                            "mix_scaled")
                for c in range(CW):
                    inc(nc.scalar.activation(pool_u[:, c, :], bank(f"pu{c}"), ACT.Copy), "pu_ready")
                after("kss_ready")
                inc(nc.scalar.activation(X2[:, :, :], X2[:, :, :], ACT.Sqrt), "kss_sqrt")
                for c in range(CW):
                    inc(nc.scalar.activation(pool_gate[:, c, :], bank(f"pg{c}"), ACT.Silu), "pg_ready")
                after("g_sum")
                nc.scalar.activation(e_end[:, :, :], X2[:, :, P - 1:T:P], ACT.Exp, scale=DECAY)
                inc(nc.scalar.activation(X1[:, :, :], X2[:, :, :], ACT.Exp, scale=DECAY, bias=con("off", 0)), "exp_plus")
                after("g_prev")
                inc(nc.scalar.activation(G_[:, :, :], G_[:, :, :], ACT.Exp, scale=DECAY, bias=con("off", 0)), "exp_prev")
                after("exp_plus")
                inc(nc.scalar.activation(X2[:, :, :], X2[:, :, :], ACT.Exp, scale=-DECAY, bias=con("off", 1)), "exp_minus")
                after("ar_ready")
                for n in range(NT):
                    inc(nc.scalar.activation(v_tok[:, n, :], bank(f"tv{n}"), ACT.Copy), "tok_ready")
                for n in range(NT):
                    inc(nc.scalar.activation(b_tok[:, n, :], bank(f"tb{n}"), ACT.Copy), "tok_ready")
                after("bonus_ready")
                for n in range(NT):
                    inc(nc.scalar.activation(k_tok[:, n, :], bank(f"tk{n}"), ACT.Copy), "tok_ready")
                for n in range(NT):
                    for g in range(2):
                        inc(nc.scalar.activation(tt[:, 4 * g:4 * g + 4, :].rearrange("p u t -> p (u t)"),
                                                 bank(f"ti{n}{g}"), ACT.Copy), "tinit_ready")
                    inc(nc.scalar.activation(w_sb[:, :], bank(f"w{n}"), ACT.Copy), "w_ready")
                    if n == 0:
                        after("bk_ready")
                    inc(nc.scalar.activation(y_tok[:, n, :], bank(f"y{n}"), ACT.Copy), "y_ready")
                for c in range(CW):
                    inc(nc.scalar.activation(A_[:, c, :], bank(f"rg{c}"), ACT.Silu), "rg_ready")
                after("y_norm", 4)
                for z, what in ((rq_raw, "q"), (rk_raw, "k"), (rv_tok, "v")):
                    for b in range(2):
                        for tp in range(2):
                            o = bank(f"ret{what}{b}{tp}").rearrange("p (n f) -> p n f", n=2)
                            inc(nc.scalar.activation(z[:, 2 * tp:2 * tp + 2, b * 256:b * 256 + 256], o, ACT.Copy), "ret_tok")
                for c in range(CW):
                    inc(nc.scalar.activation(ret_gate[:, c, :], bank(f"tg{c}"), ACT.Silu), "retg_ready")
                after("y_norm", 5)
                inc(nc.scalar.activation(hvar[:, :], hvar[:, :], ACT.Sqrt), "y_sqrt")
                after("rwkv_done")
                for h in range(RET_H):
                    inc(nc.scalar.activation(qT[:, h, :], bank(f"tq{h}"), ACT.Copy), "qT_ready")
                for h in range(RET_H):
                    inc(nc.scalar.activation(kT[:, h, :], bank(f"tkr{h}"), ACT.Copy), "kT_ready")
                for n in range(NT):
                    inc(nc.scalar.activation(o_tok[:, n, :], bank(f"o{n}"), ACT.Copy), "o_ready")
                after("o_norm", 5)
                inc(nc.scalar.activation(hvar[:, 0:16], hvar[:, 0:16], ACT.Sqrt), "o_sqrt")
                for cp in range(KD // 2):
                    for n in range(3):
                        for cc in range(2):
                            if cp >= 2:
                                after("merged", 5 * (2 * cp - 4 + cc) + (1, 2, 4)[n])
                            elif cp == 0 and n == 0 and cc == 0:
                                after("ret_done")
                            i = 6 * (cp % 2) + 2 * n + cc
                            inc(nc.scalar.activation(sig_gate[:, i, :], bank(f"g{cp}{n}{cc}"), ACT.Sigmoid), "gate_sig")

            @block.vector
            def _(dve):
                v = nc.vector

                def after(name, k=None):
                    dve.wait_ge(SEM[name], PER[name] if k is None else k)

                def bank(name):
                    dve.wait_ge(SEM["bank_full"], JOB[name] + 1)
                    return banks[:, JOB[name] % 8]

                done = {}

                def step(ins, name):
                    inc(ins, name)
                    done[name] = done.get(name, 0) + 1
                    after(name, done[name])

                after("params_loaded")
                mu = par("mu")
                inc(v.tensor_scalar(omm[:, 0:13], mu, -1.0, 1.0, ALU.mult, ALU.add), "gs_ready")
                inc(v.tensor_scalar(omm[:, 13:17], par("k_a"), -1.0, 1.0, ALU.mult, ALU.add), "gs_ready")
                step(v.tensor_tensor(mod[:, :], bank("mod")[:, 0:24], par("b_ada"), ALU.add), "mod_ready")
                inc(v.scalar_tensor_tensor(gs[:, :], mod[:, 8:16], 1.0, par("norm_g"), ALU.add, ALU.mult), "gs_ready")
                step(v.tensor_scalar(rstd[:, :], bank("ss"), RMS_EPS, None, ALU.add), "rms_ready")
                after("rms_sqrt")
                step(v.reciprocal(rstd[:, :], rstd[:, :]), "rms_ready")
                after("gs_ready")
                for k in range(KD):
                    inc(v.scalar_tensor_tensor(hT[:, k, :], xT[:, k, :], gs[:, k:k + 1], rstd[:, :], ALU.mult, ALU.mult),
                        "h_scaled")

                def mix(z, m, name):
                    o = bank(name)
                    after("mix_scaled", m + 1)
                    inc(v.scalar_tensor_tensor(z[:, 1:T], o[:, 0:T - 1], mu[:, m:m + 1], z[:, 1:T], ALU.mult, ALU.add),
                        "mixed")

                for c in range(CW):
                    mix(R_[:, c, :], c, f"r{c}")
                mix(w_sb[:, :], 4, "wl")
                for c in range(CW):
                    mix(K_[:, c, :], 5 + c, f"k{c}")
                after("mixed", 9)
                for c in range(CW):
                    last = v.tensor_scalar(KK[:, c, :], K_[:, c, :], par("k_k", c), None, ALU.mult)
                inc(last, "kk_ready")
                after("kk_ready", 1)
                inc(v.tensor_tensor(X1[:, :, :], KK[:, :, :], KK[:, :, :], ALU.mult), "kk_ready")
                for c in range(CW):
                    mix(V_[:, c, :], 9 + c, f"v{c}")
                after("a_ready")
                for c in range(CW):
                    last = v.tensor_scalar(X3[:, c, :], A_[:, c, :], par("k_a", c), omm[:, 13 + c:14 + c], ALU.mult, ALU.add)
                step(last, "k_mod")
                step(v.tensor_tensor(K_[:, :, :], K_[:, :, :], X3[:, :, :], ALU.mult), "k_mod")
                for c in range(CW):
                    last = v.scalar_tensor_tensor(X3[:, c, :], R_[:, c, :], par("r_k", c), K_[:, c, :], ALU.mult, ALU.mult)
                inc(last, "rk_ready")
                for c in range(CW):
                    inc(v.tensor_scalar(X2[:, c, :], bank(f"kss{c}"), 1e-24, None, ALU.max), "kss_ready")
                after("kss_sqrt")
                step(v.reciprocal(X2[:, :, :], X2[:, :, :]), "kk_unit")
                step(v.tensor_tensor(KK[:, :, :], KK[:, :, :], X2[:, :, :], ALU.mult), "kk_unit")
                v.tensor_tensor(A_[:, :, :], A_[:, :, :], KK[:, :, :], ALU.mult)
                after("g_ready")
                for c in range(CW):
                    for n in range(NT):
                        t0 = n * P
                        last = v.tensor_tensor_scan(X2[:, c, t0:t0 + P], con("ones"), G_[:, c, t0:t0 + P], 0.0,
                                                    ALU.mult, ALU.add)
                step(last, "g_sum")
                inc(v.tensor_tensor(G_[:, :, :], X2[:, :, :], G_[:, :, :], ALU.subtract), "g_prev")
                for c in range(CW):
                    o = bank(f"py{c}")
                    after("pg_ready", c + 1)
                    inc(v.scalar_tensor_tensor(br_pool[:, c, :], o, par("pool_scale", c), pool_gate[:, c, :],
                                               ALU.mult, ALU.mult), "pool_done")
                after("mixed")
                for c in range(CW):
                    inc(v.tensor_tensor(X3[:, c, :], bank(f"bs{c}"), V_[:, c, :], ALU.mult), "bonus_ready")
                after("exp_plus")
                inc(v.tensor_tensor(R_[:, :, :], R_[:, :, :], X1[:, :, :], ALU.mult), "ar_ready")
                after("exp_prev")
                inc(v.scalar_tensor_tensor(KK[:, :, :], KK[:, :, :], -1.0, G_[:, :, :], ALU.mult, ALU.mult), "ar_ready")
                after("exp_minus")
                inc(v.tensor_tensor(A_[:, :, :], A_[:, :, :], X2[:, :, :], ALU.mult), "bk_ready")
                inc(v.tensor_tensor(K_[:, :, :], K_[:, :, :], X2[:, :, :], ALU.mult), "bk_ready")

                flat = lambda a, g: a[:, 4 * g:4 * g + 4, :]
                lvl1 = con("lvl1")
                for n in range(NT):
                    for h in range(RW_H):
                        inc(v.tensor_tensor(gm[:, h].rearrange("p k t -> p (k t)"), bank(f"gram{n}{h}"), con("gram"), ALU.mult),
                            "gram_ready")
                    for g in range(2):
                        after("gram_ready", 8 * n + 4 * g + 4)
                        step(v.tensor_tensor(flat(zt, g), gm[:, 4 * g:4 * g + 4, 0, :],
                                             lvl1[:, 0:P].unsqueeze(1).broadcast_to([P, 4, P]), ALU.mult), "z_masked")
                        inc(v.tensor_tensor(flat(zt, g), flat(zt, g), ident.unsqueeze(1).broadcast_to([P, 4, P]), ALU.add),
                            "z_ready")
                    for l in range(6):
                        mask = con("lvl")[:, l * P:l * P + P].unsqueeze(1).broadcast_to([P, 4, P])
                        for g in range(2):
                            o = bank(f"p{n}{l}{g}").rearrange("p (u t) -> p u t", u=4)
                            inc(v.tensor_tensor(flat(pt, g), o, mask, ALU.mult), "p_ready")
                        for g in range(2):
                            if l < 5:
                                o = bank(f"tn{n}{l}{g}").rearrange("p (u t) -> p u t", u=4)
                                if l == 0:
                                    after("tinit_ready", 2 * n + 1 + g)
                                else:
                                    after("t_ready", 10 * n + 2 * (l - 1) + 1 + g)
                                inc(v.tensor_tensor(flat(tt, g), o, flat(tt, g), ALU.add), "t_ready")
                            o = bank(f"zn{n}{l}{g}").rearrange("p (u t) -> p u t", u=4)
                            after("z_ready", 14 * n + 2 * l + 1 + g)
                            inc(v.tensor_tensor(flat(zt, g), o, flat(zt, g), ALU.add), "z_ready")
                    inc(v.tensor_copy(u_sb[:, :], bank(f"u{n}")), "u_ready")
                    if n < NT - 1:
                        flat_state = state[:, :, :].rearrange("p c f -> p (c f)")
                        o = bank(f"s{n}")
                        if n == 0:
                            step(v.tensor_copy(flat_state, o), "s_added")
                        else:
                            step(v.tensor_tensor(flat_state, o, flat_state, ALU.add), "s_added")
                        for c in range(CW):
                            last = v.scalar_tensor_tensor(state[:, c, :], state[:, c, :], e_end[:, c, n:n + 1], con("blk64"),
                                                          ALU.mult, ALU.mult)
                        inc(last, "s_ready")
                        after("s_ready", n + 1)

                def head_norm(z, squares, heads, width, eps, name, sqrt_name):
                    z3 = z.rearrange("p n (h d) -> p (n h) d", d=width)
                    q3 = squares.rearrange("p n (h d) -> p (n h) d", d=width)
                    mean, var = hsum[:, 0:heads], hvar[:, 0:heads]
                    wide = [a.unsqueeze(2).broadcast_to([P, heads, width]) for a in (mean, var)]
                    step(v.tensor_reduce(mean, z3, AX_X, ALU.add), name)
                    step(v.scalar_tensor_tensor(z3, wide[0], -1.0 / width, z3, ALU.mult, ALU.add), name)
                    step(v.tensor_tensor(q3, z3, z3, ALU.mult), name)
                    step(v.tensor_reduce(var, q3, AX_X, ALU.add), name)
                    step(v.tensor_scalar(var, var, 1.0 / width, eps, ALU.mult, ALU.add), name)
                    after(sqrt_name)
                    step(v.reciprocal(var, var), name)
                    step(v.tensor_tensor(z3, z3, wide[1], ALU.mult), name)

                after("y_ready")
                head_norm(y_tok, X1, 32, RW_D, RW_EPS, "y_norm", "y_sqrt")
                after("rg_ready")
                for c in range(CW):
                    step(v.tensor_scalar(br_rwkv[:, c, :], bank(f"ty{c}"), par("ln_w", c), par("ln_b", c), ALU.mult, ALU.add),
                         "y_scaled")
                    step(v.tensor_tensor(br_rwkv[:, c, :], br_rwkv[:, c, :], X3[:, c, :], ALU.add), "y_bonus")
                    inc(v.tensor_tensor(br_rwkv[:, c, :], br_rwkv[:, c, :], A_[:, c, :], ALU.mult), "rwkv_done")
                for i, (raw, rot) in enumerate(((rq_raw, rq_rot), (rk_raw, rk_rot))):
                    after("ret_tok", 4 * i + 4)
                    x = raw.rearrange("p n (h e d) -> p n h e d", h=RET_H, e=2)
                    y = rot.rearrange("p n (h e d) -> p n h e d", h=RET_H, e=2)
                    t1, t2 = (a.rearrange("p (n h d) -> p n h d", n=NT, h=RET_H) for a in rot_tmp)
                    cs, sn = (a[:, :, :].unsqueeze(2).broadcast_to([P, NT, RET_H, 64]) for a in (cosT, sinT))
                    if i == 1:
                        after("rot_ready", 1)
                    v.tensor_tensor(t1, x[:, :, :, 0, :], cs, ALU.mult)
                    step(v.tensor_tensor(t2, x[:, :, :, 1, :], sn, ALU.mult), "rot_step")
                    step(v.tensor_tensor(y[:, :, :, 0, :], t1, t2, ALU.subtract), "rot_step")
                    v.tensor_tensor(t1, x[:, :, :, 0, :], sn, ALU.mult)
                    step(v.tensor_tensor(t2, x[:, :, :, 1, :], cs, ALU.mult), "rot_step")
                    inc(v.tensor_tensor(y[:, :, :, 1, :], t1, t2, ALU.add), "rot_ready")
                after("rot_ready")
                for h in range(RET_H):
                    cols = slice(h * P, h * P + P)
                    last = v.tensor_scalar(k_tail[:, :, cols], rk_rot[:, :, cols], con("ret_k", h), None, ALU.mult)
                inc(last, "ktail_ready")
                for h in range(RET_H):
                    o = bank(f"tq{h}").rearrange("p (n t) -> p n t", n=NT)
                    after("qT_ready", h + 1)
                    decay = con("ret_q")[:, h * P:h * P + P].unsqueeze(1).broadcast_to([P, NT, P])
                    inc(v.tensor_tensor(qdT[:, h, :].rearrange("p (n t) -> p n t", n=NT), o, decay, ALU.mult), "qd_ready")
                for n in range(NT):
                    inc(v.tensor_tensor(p_ret[n % 2], bank(f"sc{n}"), con("ret_mask"), ALU.mult), "pret_ready")
                    if n < NT - 1:
                        o = bank(f"kv{n}")
                        if n == 0:
                            last = v.tensor_copy(state[:, :, :].rearrange("p h e -> p (h e)"), o)
                        else:
                            for h in range(RET_H):
                                decay = math.exp(math.log1p(-(2.0 ** (-5.0 - h))) * P)
                                last = v.scalar_tensor_tensor(state[:, h, :], state[:, h, :], decay, o[:, h * P:h * P + P],
                                                              ALU.mult, ALU.add)
                        inc(last, "R_ready")
                        after("R_ready", n + 1)
                after("o_ready")
                head_norm(o_tok, o_sq, 16, RET_D, RET_EPS, "o_norm", "o_sqrt")
                after("retg_ready")
                for h in range(RET_H):
                    inc(v.scalar_tensor_tensor(br_ret[:, h, :], bank(f"to{h}"), par("ret_norm_g", h), ret_gate[:, h, :],
                                               ALU.mult, ALU.mult), "ret_done")
                for cp in range(KD // 2):
                    for cc in range(2):
                        c = 2 * cp + cc
                        for n in range(3):
                            after("gate_sig", 6 * cp + 2 * n + cc + 1)
                            o = bank(f"b{cp}{cc}{n}")
                            sig = sig_gate[:, 6 * (cp % 2) + 2 * n + cc, :]
                            part = (mT[:, c, :], w_sb[:, :], u_sb[:, :])[n]
                            step(v.tensor_tensor(part, o, sig, ALU.mult), "merged")
                            if n > 0:
                                step(v.tensor_tensor(mT[:, c, :], mT[:, c, :], part, ALU.add), "merged")
                for c in range(KD):
                    inc(v.scalar_tensor_tensor(xT[:, c, :], bank(f"wo{c}"), mod[:, 16 + c:17 + c], xT[:, c, :],
                                               ALU.mult, ALU.add), "x_done")

            @block.gpsimd
            def _(pool):
                g = nc.gpsimd

                count = [0]

                def step(ins):
                    inc(ins, "pool_step")
                    count[0] += 1
                    pool.wait_ge(SEM["pool_step"], count[0])

                tmp = [zt.rearrange("p u t -> p (u t)")[:, i * T:i * T + T] for i in range(2)]
                fix = tt.rearrange("p u t -> p (u t)")[:, 0:16]
                for i, w in enumerate(WINDOWS):
                    u = pool_u[:, i, :]
                    pool.wait_ge(SEM["pu_ready"], i + 1)
                    src, lag = u, 1
                    while lag < w:
                        dst = tmp[0] if src is not tmp[0] else tmp[1]
                        inc(g.tensor_copy(dst[:, 0:lag], src[:, 0:lag]), "pool_step")
                        count[0] += 1
                        step(g.tensor_tensor(dst[:, lag:T], src[:, lag:T], src[:, 0:T - lag], ALU.add))
                        src, lag = dst, 2 * lag
                    step(g.tensor_tensor(fix, src[:, 0:16], con("inv_count")[:, 16 * i:16 * i + 16], ALU.mult))
                    step(g.tensor_tensor(fix, fix, u[:, 0:16], ALU.subtract))
                    step(g.tensor_scalar(src, src, 1.0 / w, None, ALU.mult))
                    step(g.tensor_tensor(u, src, u, ALU.subtract))
                    inc(g.tensor_copy(u[:, 0:16], fix), "pool_d")

          numbers = [SEM[name].num for name in LAYER_SEMS]
          assert numbers == list(range(numbers[0], numbers[-1] + 1))
          nc.sync.sem_clear(range(numbers[0], numbers[-1] + 1))
          nc.all_engine_barrier()
        jobs = []
        for h in range(DIL_H):
            for i in range(2):
                job(f"dr{h}{i}", "dr_drained", 2 * h + i + 1)
        job("ss0", "n_mean", 1)
        job("ss1", "n_mean", 3)
        job("f", "f_step", 1)
        for i, what in enumerate(("qd", "kd", "vd", "qf", "kf", "vf")):
            for c in range(CW):
                job(f"{what}{c}", "qkv_ready", 4 * i + c + 1)
        for h in range(FOX_H):
            job(f"nc{h}", "nc_ready", h + 1)
        heads = [(kind, tb, h) for kind in range(2) for tb in range(NT) for h in range(DIL_H)]
        for i in range(-2, len(heads)):
            if i + 2 < len(heads):
                job(f"s{i + 2}", "s_shifted", i + 3)
            if i >= 0:
                job(f"p{i}", "pt_ready", i + 1)
        for c in range(KD):
            job(f"ot{c}", "oT_ready", c + 1)
        for c in range(KD):
            job(f"ao{c}", "x_att", c + 1)
        job("ss2", "n_mean", 5)
        job("route", "route_step", 1)
        for n in range(NT):
            for i in range(2):
                job(f"hk{n}{i}", "h_tok", 2 * n + i + 1)
        for n in range(NT):
            for i in range(2):
                job(f"xk{n}{i}", "x_tok", 2 * n + i + 1)
        job("rank", "rank_read", 1)
        RB = 6
        JOB = {name: j for j, (name, _, _) in enumerate(jobs)}
        DRAIN = {name: (sem_name, k) for name, sem_name, k in jobs}
        att_jobs = list(jobs)
        att_block_end = [f"{w}{c}" for w in ("qd", "kd", "vd", "qf", "kf", "vf") for c in (1, 3)]
        att_block_end += [f"ao{c}" for c in range(1, KD, 2)]

        for name in ("att_full", "dist_loaded", "dr_drained", "dr_stored", "bias_loaded", "zero_set", "x_zeroed", "fnorm_loaded",
                     "n_sq", "n_mean", "n_root", "n_out", "f_step", "f_act", "negc_step", "qkv_ready", "nc_ready",
                     "s_shifted", "s_max", "s_exp", "pt_ready", "pv_step", "o_step", "o_sq", "o_root", "o_scaled",
                     "oT_ready", "x_att", "route_step", "route_exp", "m_ready", "rank_read", "h_tok", "x_tok", "idx_ready",
                     "scattered"):
            sem(name)

        qd, kd, vd, qf, kf, vf = SL[:6]
        o_tok = [SL[6], SL[7]]
        bias_d = [SL[8][:, h, :] for h in range(4)] + [br_pool[:, h, :] for h in range(4)]
        neg_c = gm_mem[:, :].rearrange("p (h t) -> p h t", h=FOX_H)
        fnorm = lpar[:, D:2 * D]
        att_stat = cosT[:, :, :].rearrange("p a b -> p (a b)")[:, 0:4 * DIL_H * NT].rearrange("p (s i) -> p s i", s=2)
        flat_ztp = ztp[:, :, :, :].rearrange("p a u t -> p (a u t)")
        rows_mem = slots[:, 6:8].rearrange("p s c t -> p (s c t)")
        dil_sb = [rows_mem[:, h * DIL_ROW:(h + 1) * DIL_ROW] for h in range(6)]
        dil_sb += [flat_ztp[:, h * DIL_ROW:(h + 1) * DIL_ROW] for h in range(2)]
        dist_sb = flat_ztp[0:BUCKETS + 1, 2048:2048 + DIL_ROW]
        s_buf = [flat_ztp[:, i * T:i * T + T] for i in range(4)]
        p_buf = [flat_ztp[:, i * T:i * T + T] for i in range(4, 6)]
        f_sb, f_tmp = w_sb[0:FOX_H, :], u_sb[0:FOX_H, :]
        oT = hT
        zeros = lpar[:, 0:D]
        h_rows = wring[:, 0:2].rearrange("p s k n -> p (s k n)").rearrange("p (n d) -> p n d", n=NT)
        x_rows = wring[:, 2:4].rearrange("p s k n -> p (s k n)").rearrange("p (n d) -> p n d", n=NT)
        flat_pool = br_pool[:, :, :].rearrange("p c t -> p (c t)")
        rt = flat_pool[:, 0:26 * EXPERTS].rearrange("p (i n g) -> p i n g", n=NT, g=PER_GROUP)
        route = flat_pool[:, 26 * EXPERTS:26 * EXPERTS + NT * ROUTE].rearrange("p (n e) -> p n e", n=NT)
        n_max, n_sum = att_stat[:, 0, :], att_stat[:, 1, :]

        with nc.Block() as block:
            @block.sync
            def _(sp):
                sp.dma_start(dist_sb, distances).then_inc(SEM["dist_loaded"], 16)
                sp.dma_start(fnorm, last_norm).then_inc(SEM["fnorm_loaded"], 16)
                for b in range(ATT_B - RING):
                    sp.wait_ge(SEM["att_full"], JOB[att_block_end[b]] + 1)
                    index = LAYERS * LAYER_B + b + RING
                    sp.dma_start(wring[:, b % RING].rearrange("p k n -> p (k n)"), wstream[index]) \
                      .then_inc(SEM[f"wload{b % RING}"], 16)

            @block.tensor
            def _(pe):
                at = [0]

                def after(name, k):
                    pe.wait_ge(SEM[name], k)

                def open_bank(name):
                    j = at[0]
                    assert att_jobs[j][0] == name, (name, att_jobs[j])
                    if j >= RB:
                        after(*att_jobs[j - RB][1:])
                    at[0] = j + 1
                    return banks[:, j % RB]

                def full(mm):
                    mm.then_inc(SEM["att_full"], 1)

                def weights(b):
                    pe.wait_ge(SEM[f"wload{b % RING}"], 16 * (LAYERS * LAYER_B // RING + b // RING + 1))
                    return wring[:, b % RING]

                after("dist_loaded", 16)
                for h in range(DIL_H):
                    for i in range(2):
                        o = open_bank(f"dr{h}{i}")
                        half = slice(i * DIL_ROW // 2, (i + 1) * DIL_ROW // 2)
                        a = GCOL["rel"][0] + h
                        full(nc.tensor.matmul(o[:, 0:DIL_ROW // 2], gpar[0:BUCKETS + 1, a:a + 1].broadcast_to([BUCKETS + 1, P]),
                                              dist_sb[:, half], start=True, stop=True))

                def mean_square(i):
                    o = open_bank(f"ss{i}")
                    for k in range(KD):
                        after("n_sq", 8 * i + k + 1)
                        mm = nc.tensor.matmul(o, con("mean"), hT[:, k, :], start=(k == 0), stop=(k == KD - 1))
                    full(mm)

                mean_square(0)
                mean_square(1)
                after("n_out", 16)
                o = open_bank("f")
                w_f = glob("w_f").rearrange("p (k h) -> p k h", k=KD)
                for k in range(KD):
                    mm = nc.tensor.matmul(o[0:FOX_H, :], w_f[:, k, :], hT[:, k, :], start=(k == 0), stop=(k == KD - 1))
                full(mm)
                for i, what in enumerate(("qd", "kd", "vd", "qf", "kf", "vf")):
                    for c in range(CW):
                        if c % 2 == 0:
                            wb = weights(2 * i + c // 2)
                        o = open_bank(f"{what}{c}")
                        if what[0] == "v":
                            for ti in range(2):
                                n = 2 * (c % 2) + ti
                                for k in range(KD):
                                    mm = nc.tensor.matmul(o[:, ti * 256:ti * 256 + 256], hT[:, k, n * P:n * P + P],
                                                          wb[:, k, :], start=(k == 0), stop=(k == KD - 1))
                        else:
                            for k in range(KD):
                                mm = nc.tensor.matmul(o, wb[:, k, (c % 2) * P:(c % 2 + 1) * P], hT[:, k, :],
                                                      start=(k == 0), stop=(k == KD - 1))
                        full(mm)
                after("negc_step", 4)
                for h in range(FOX_H):
                    o = open_bank(f"nc{h}")
                    full(nc.tensor.matmul(o, ident[0:FOX_H, h:h + 1].broadcast_to([FOX_H, P]), f_sb, start=True, stop=True))
                after("qkv_ready", 24)

                def scores(i):
                    kind, tb, h = heads[i]
                    q, k = ((qd, kd), (qf, kf))[kind]
                    p0, c, n = 64 * (h % 2), h // 2, (tb + 1) * P
                    o = open_bank(f"s{i}")
                    query, keys = q[p0:p0 + 64, c, tb * P:n], k[p0:p0 + 64, c, :]
                    if kind == 0:
                        mm = nc.tensor.matmul(o[:, 0:n], query, keys[:, 0:n], start=True, stop=True)
                    else:
                        if tb > 0:
                            nc.tensor.matmul(o[:, 0:tb * P], query, keys[:, 0:tb * P], start=True, stop=True)
                        nc.tensor.matmul(o[:, tb * P:n], query, keys[:, tb * P:n], start=True, stop=False)
                        mm = nc.tensor.matmul(o[:, tb * P:n], ident, con("causal"), start=False, stop=True)
                    full(mm)

                def turn(i):
                    kind, tb, h = heads[i]
                    after("s_exp", i + 1)
                    o = open_bank(f"p{i}")
                    for sb_ in range(tb + 1):
                        mm = nc.tensor.transpose(o[:, sb_ * P:sb_ * P + P], s_buf[i % 4][:, sb_ * P:sb_ * P + P], ident)
                    full(mm)

                def values(i):
                    kind, tb, h = heads[i]
                    v = (vd, vf)[kind]
                    after("pt_ready", i + 1)
                    group = 4 * kind + tb
                    if h == 0 and group >= 2:
                        after("o_step", 2 * (group - 1))
                    o = banks[:, 6 + group % 2]
                    for sb_ in range(tb + 1):
                        mm = nc.tensor.matmul(o[:, h * HD:h * HD + HD], p_buf[i % 2][:, sb_ * P:sb_ * P + P],
                                              v[:, sb_, h * HD:h * HD + HD], start=(sb_ == 0), stop=(sb_ == tb))
                    mm.then_inc(SEM["pv_step"], 1)

                for i in range(-2, len(heads) + 1):
                    if i + 2 < len(heads):
                        scores(i + 2)
                    if 0 <= i < len(heads):
                        turn(i)
                    if i >= 1:
                        values(i - 1)
                for c in range(KD):
                    after("o_scaled", 4 * (c // CW) + 4)
                    o = open_bank(f"ot{c}")
                    for n in range(NT):
                        f0 = (c % CW) * P
                        mm = nc.tensor.transpose(o[:, n * P:n * P + P], o_tok[c // CW][:, n, f0:f0 + P], ident)
                    full(mm)
                after("oT_ready", KD)
                for c in range(KD):
                    if c % 2 == 0:
                        wb = weights(12 + c // 2)
                    o = open_bank(f"ao{c}")
                    for k in range(KD):
                        mm = nc.tensor.matmul(o, wb[:, k, (c % 2) * P:(c % 2 + 1) * P], oT[:, k, :],
                                              start=(k == 0), stop=(k == KD - 1))
                    full(mm)
                mean_square(2)
                after("n_out", 24)
                o = open_bank("route")
                w_r = glob("w_route").rearrange("p (k e) -> p k e", k=KD)
                for n in range(NT):
                    for k in range(KD):
                        nc.tensor.matmul(o[:, n * ROUTE:(n + 1) * ROUTE], hT[:, k, n * P:n * P + P], w_r[:, k, :],
                                         start=(k == 0), stop=False)
                    mm = nc.tensor.matmul(o[:, n * ROUTE:(n + 1) * ROUTE], con("ones")[0:1, :], glob("b_route")[0:1, :],
                                          start=False, stop=True)
                full(mm)
                for name, z in (("hk", hT), ("xk", xT)):
                    for n in range(NT):
                        for i in range(2):
                            o = open_bank(f"{name}{n}{i}")
                            for k in range(4):
                                mm = nc.tensor.transpose(o[:, k * P:k * P + P], z[:, 4 * i + k, n * P:n * P + P], ident)
                            full(mm)
                after("m_ready", 1)
                o = open_bank("rank")
                chosen = rt[:, 8:12].rearrange("p e n g -> p (e n g)").rearrange("p (n e) -> p n e", n=NT)
                for n in range(NT + 1):
                    for m in range(min(n + 1, NT)):
                        lhs = con("gram")[:, 0:P] if m == n else con("ones")
                        mm = nc.tensor.matmul(o[:, n * EXPERTS:(n + 1) * EXPERTS], lhs, chosen[:, m, :],
                                              start=(m == 0), stop=(m == min(n, NT - 1)))
                full(mm)
                assert at[0] == len(att_jobs)

            @block.scalar
            def _(act):
                def after(name, k):
                    act.wait_ge(SEM[name], k)

                def bank(name):
                    act.wait_ge(SEM["att_full"], JOB[name] + 1)
                    return banks[:, JOB[name] % RB]

                def squares(i):
                    for k in range(KD):
                        nc.scalar.activation(hT[:, k, :], xT[:, k, :], ACT.Square).then_inc(SEM["n_sq"], 1)

                def root(i):
                    after("n_mean", 2 * i + 1)
                    nc.scalar.activation(rstd[:, :], rstd[:, :], ACT.Sqrt).then_inc(SEM["n_root"], 1)

                squares(0)
                for h in range(DIL_H):
                    for i in range(2):
                        half = slice(i * DIL_ROW // 2, (i + 1) * DIL_ROW // 2)
                        nc.scalar.activation(dil_sb[h][:, half], bank(f"dr{h}{i}")[:, 0:DIL_ROW // 2], ACT.Copy) \
                            .then_inc(SEM["dr_drained"], 1)
                    after("dr_drained", 2 * h + 2)
                    act.dma_start(dil_rows[h].rearrange("(p y) -> p y", y=DIL_ROW), dil_sb[h]).then_inc(SEM["dr_stored"], 16)
                root(0)
                after("n_out", 8)
                squares(1)
                root(1)
                after("f_step", 2)
                nc.scalar.activation(f_tmp, f_tmp, ACT.Exp).then_inc(SEM["f_act"], 1)
                after("f_act", 1)
                nc.scalar.activation(f_tmp, f_tmp, ACT.Ln, bias=1.0).then_inc(SEM["f_act"], 1)
                for z, what in ((qd, "qd"), (kd, "kd"), (vd, "vd"), (qf, "qf"), (kf, "kf"), (vf, "vf")):
                    for c in range(CW):
                        o = bank(f"{what}{c}")
                        dst = z[:, c, :]
                        if what[0] == "v":
                            o = o.rearrange("p (n f) -> p n f", n=2)
                            dst = z[:, 2 * (c % 2):2 * (c % 2) + 2, (c // 2) * 256:(c // 2) * 256 + 256]
                        nc.scalar.activation(dst, o, ACT.Copy).then_inc(SEM["qkv_ready"], 1)
                for h in range(FOX_H):
                    nc.scalar.activation(neg_c[:, h, :], bank(f"nc{h}"), ACT.Copy).then_inc(SEM["nc_ready"], 1)
                after("dr_stored", 16 * DIL_H)

                def norm(kind):
                    for tb in range(NT):
                        after("o_step", 2 * (4 * kind + tb) + 2)
                        if kind or tb:
                            after("o_sq", 4 * kind + tb)
                        nc.scalar.activation(u_sb[:, :], o_tok[kind][:, tb, :], ACT.Square,
                                             accum_out=hvar[:, 4 * kind + tb:4 * kind + tb + 1]).then_inc(SEM["o_sq"], 1)

                for i, (kind, tb, h) in enumerate(heads):
                    n = (tb + 1) * P
                    after("s_max", i + 1)
                    nc.scalar.activation(s_buf[i % 4][:, 0:n], s_buf[i % 4][:, 0:n], ACT.Exp, bias=n_max[:, i:i + 1],
                                         accum_out=n_sum[:, i:i + 1]).then_inc(SEM["s_exp"], 1)
                    if i >= 1:
                        j = i - 1
                        if j >= 2:
                            after("pv_step", j - 1)
                        m = (heads[j][1] + 1) * P
                        nc.scalar.activation(p_buf[j % 2][:, 0:m], bank(f"p{j}")[:, 0:m], ACT.Copy).then_inc(SEM["pt_ready"], 1)
                j = len(heads) - 1
                after("pv_step", j - 1)
                nc.scalar.activation(p_buf[j % 2], bank(f"p{j}"), ACT.Copy).then_inc(SEM["pt_ready"], 1)
                for kind in range(2):
                    norm(kind)
                after("o_step", 17)
                nc.scalar.activation(hvar[:, 0:8], hvar[:, 0:8], ACT.Sqrt).then_inc(SEM["o_root"], 1)
                after("o_step", 18)
                for kind in range(2):
                    for tb in range(NT):
                        j = 4 * kind + tb
                        nc.scalar.activation(o_tok[kind][:, tb, :], o_tok[kind][:, tb, :], ACT.Copy, scale=hvar[:, j:j + 1]) \
                            .then_inc(SEM["o_scaled"], 1)
                for c in range(KD):
                    nc.scalar.activation(oT[:, c, :], bank(f"ot{c}"), ACT.Copy, scale=glob("out_norm", c)).then_inc(SEM["oT_ready"], 1)
                after("x_att", KD)
                squares(2)
                root(2)
                for name, rows, done in (("hk", h_rows, "h_tok"), ("xk", x_rows, "x_tok")):
                    for n in range(NT):
                        for i in range(2):
                            nc.scalar.activation(rows[:, n, i * T:i * T + T], bank(f"{name}{n}{i}"), ACT.Copy) \
                                .then_inc(SEM[done], 1)
                    if name == "hk":
                        after("route_step", 5)
                        nc.scalar.activation(rt[:, 0, :, 0:4], rt[:, 0, :, 0:4], ACT.Exp).then_inc(SEM["route_exp"], 1)
                        after("route_step", 30)
                        nc.scalar.activation(rt[:, 4, :, 3:4], rt[:, 4, :, 2:3], ACT.Exp).then_inc(SEM["route_exp"], 1)

            @block.vector
            def _(dve):
                v = nc.vector
                count = {}

                def after(name, k):
                    dve.wait_ge(SEM[name], k)

                def bank(name):
                    dve.wait_ge(SEM["att_full"], JOB[name] + 1)
                    return banks[:, JOB[name] % RB]

                def step(ins, name):
                    ins.then_inc(SEM[name], 1)
                    count[name] = count.get(name, 0) + 1
                    after(name, count[name])

                def norm(i, out_, gain):
                    step(v.tensor_scalar(rstd[:, :], bank(f"ss{i}"), RMS_EPS, None, ALU.add), "n_mean")
                    after("n_root", i + 1)
                    step(v.reciprocal(rstd[:, :], rstd[:, :]), "n_mean")
                    for k in range(KD):
                        v.scalar_tensor_tensor(out_[:, k, :], xT[:, k, :], glob(gain, k), rstd[:, :], ALU.mult, ALU.mult) \
                            .then_inc(SEM["n_out"], 1)

                def gather(group):
                    kind, tb = group // NT, group % NT
                    after("pv_step", DIL_H * (group + 1))
                    after("s_exp", DIL_H * (group + 1))
                    inv = n_sum[:, DIL_H * group:DIL_H * (group + 1)]
                    step(v.reciprocal(inv, inv), "o_step")
                    o = banks[:, 6 + group % 2].rearrange("p (h d) -> p h d", h=DIL_H)
                    step(v.tensor_tensor(o_tok[kind][:, tb, :].rearrange("p (h d) -> p h d", h=DIL_H), o,
                                         inv.unsqueeze(2).broadcast_to([P, DIL_H, HD]), ALU.mult), "o_step")

                norm(0, xT, "final_g")
                norm(1, hT, "attn_norm")
                step(v.tensor_scalar(f_sb, bank("f")[0:FOX_H, :], glob("b_forget")[0:FOX_H, :], None, ALU.add), "f_step")
                step(v.scalar_tensor_tensor(f_tmp, f_sb, -1.0, f_sb, ALU.mult, ALU.min), "f_step")
                step(v.tensor_scalar(f_sb, f_sb, 0.0, None, ALU.min), "f_step")
                after("f_act", 2)
                step(v.tensor_tensor(f_tmp, f_tmp, f_sb, ALU.subtract), "f_step")
                for n in range(NT):
                    first = 0.0 if n == 0 else f_sb[:, n * P - 1:n * P]
                    step(v.tensor_tensor_scan(f_sb[:, n * P:n * P + P], con("ones")[0:FOX_H, :], f_tmp[:, n * P:n * P + P],
                                              first, ALU.mult, ALU.add), "negc_step")
                after("bias_loaded", 16 * DIL_H)
                after("dr_stored", 16 * DIL_H)
                for i, (kind, tb, h) in enumerate(heads):
                    n = (tb + 1) * P
                    if kind:
                        after("nc_ready", h + 1)
                        bias = neg_c[:, h, 0:n]
                    else:
                        bias = bias_d[h][:, T - n:T]
                    if i >= 4:
                        after("att_full", JOB[f"p{i - 4}"] + 1)
                    step(v.scalar_tensor_tensor(s_buf[i % 4][:, 0:n], bank(f"s{i}")[:, 0:n], ATT_SCALE, bias,
                                                ALU.mult, ALU.add), "s_shifted")
                    v.tensor_reduce(n_max[:, i:i + 1], s_buf[i % 4][:, 0:n], AX_X, ALU.max, negate=True) \
                        .then_inc(SEM["s_max"], 1)
                    if h == 3 and i > 8:
                        gather(i // 8 - 1)
                gather(2 * NT - 1)
                after("o_sq", 8)
                step(v.tensor_scalar(hvar[:, 0:8], hvar[:, 0:8], 1.0 / (DIL_H * HD), RMS_EPS, ALU.mult, ALU.add), "o_step")
                after("o_root", 1)
                step(v.reciprocal(hvar[:, 0:8], hvar[:, 0:8]), "o_step")
                for c in range(KD):
                    v.tensor_tensor(xT[:, c, :], bank(f"ao{c}"), xT[:, c, :], ALU.add).then_inc(SEM["x_att"], 1)
                after("x_att", KD)
                norm(2, hT, "ffn_norm")
                r = lambda ins: step(ins, "route_step")
                r(v.tensor_copy(route[:, :, :], bank("route")[:, 0:NT * ROUTE].rearrange("p (n e) -> p n e", n=NT)))
                groups, experts_ = route[:, :, 0:GROUPS], route[:, :, GROUPS:ROUTE]
                t4 = lambda i: rt[:, i, :, 0:4]
                col = lambda i, j: rt[:, i, :, j:j + 1]
                w4 = lambda a: a.broadcast_to([P, NT, 4])
                w8 = lambda a: a.broadcast_to([P, NT, 8])
                rowb = lambda name, a, b: con(name)[:, a:b].unsqueeze(1).broadcast_to([P, NT, b - a])
                gmax, gsum, gbest = col(2, 0), col(2, 1), col(2, 2)
                r(v.tensor_reduce(gmax, groups, AX_X, ALU.max))
                r(v.tensor_tensor(t4(1), groups, w4(gmax), ALU.is_equal))
                r(v.tensor_tensor(t4(1), t4(1), rowb("rev", 0, 4), ALU.mult))
                r(v.tensor_tensor(t4(0), groups, w4(gmax), ALU.subtract))
                r(v.tensor_reduce(gbest, t4(1), AX_X, ALU.max))
                r(v.tensor_scalar(gbest, gbest, -1.0, 8.0, ALU.mult, ALU.add))
                r(v.tensor_tensor(t4(1), rowb("iota", 0, 4), w4(gbest), ALU.is_equal))
                sel, part = rt[:, 3], rt[:, 5]
                r(v.tensor_tensor(sel, experts_[:, :, 0:8], w8(rt[:, 1, :, 0:1]), ALU.mult))
                for gi in range(1, GROUPS):
                    r(v.tensor_tensor(part, experts_[:, :, 8 * gi:8 * gi + 8], w8(rt[:, 1, :, gi:gi + 1]), ALU.mult))
                    r(v.tensor_tensor(sel, sel, part, ALU.add))
                for k in range(TOP_K):
                    best, val = col(6, k), col(4, k)
                    r(v.tensor_reduce(val, sel, AX_X, ALU.max))
                    r(v.tensor_tensor(part, sel, w8(val), ALU.is_equal))
                    r(v.tensor_tensor(part, part, rowb("rev", 0, 8), ALU.mult))
                    r(v.tensor_reduce(best, part, AX_X, ALU.max))
                    r(v.tensor_scalar(best, best, -1.0, 8.0, ALU.mult, ALU.add))
                    if k == 0:
                        r(v.tensor_tensor(part, rowb("iota", 0, 8), w8(best), ALU.is_equal))
                        r(v.scalar_tensor_tensor(sel, part, -3e38, sel, ALU.mult, ALU.add))
                    r(v.scalar_tensor_tensor(best, gbest, 8.0, best, ALU.mult, ALU.add))
                r(v.tensor_tensor(col(4, 2), col(4, 1), col(4, 0), ALU.subtract))
                after("route_exp", 2)
                r(v.tensor_reduce(gsum, t4(0), AX_X, ALU.add))
                r(v.tensor_scalar(col(4, 4), col(4, 3), 1.0, None, ALU.add))
                r(v.tensor_tensor(gsum, gsum, col(4, 4), ALU.mult))
                r(v.reciprocal(col(7, 0), gsum))
                r(v.tensor_tensor(col(7, 1), col(7, 0), col(4, 3), ALU.mult))
                lay = lambda i: rt[:, i:i + 4].rearrange("p e n g -> p (e n g)").rearrange("p (n e) -> p n e", n=NT)
                chosen, hot, where, prod = lay(8), (lay(12), lay(16)), lay(20), lay(8)
                for k in range(TOP_K):
                    r(v.tensor_tensor(hot[k], rowb("iota", 0, EXPERTS), col(6, k).broadcast_to([P, NT, EXPERTS]), ALU.is_equal))
                v.tensor_tensor(chosen, hot[0], hot[1], ALU.add).then_inc(SEM["m_ready"], 1)
                o = bank("rank")
                tiles, incl, base = (rt[:, i].rearrange("p n g -> p (n g)") for i in (24, 25, 0))
                cnt = o[:, NT * EXPERTS:(NT + 1) * EXPERTS]
                r(v.tensor_scalar(tiles, cnt, 0.0, None, ALU.is_gt))
                for k in range(1, T // SLOT):
                    r(v.scalar_tensor_tensor(tiles, cnt, float(k * SLOT), tiles, ALU.is_gt, ALU.add))
                r(v.tensor_tensor_scan(incl, con("ones")[:, 0:EXPERTS], tiles, 0.0, ALU.mult, ALU.add))
                r(v.tensor_tensor(base, incl, tiles, ALU.subtract))
                r(v.tensor_scalar(base, base, float(SLOT), None, ALU.mult))
                step(v.tensor_tensor(where, o[:, 0:NT * EXPERTS].rearrange("p (n e) -> p n e", n=NT),
                                     base.unsqueeze(1).broadcast_to([P, NT, EXPERTS]), ALU.add), "rank_read")
                for k in range(TOP_K):
                    r(v.tensor_tensor(prod, hot[k], where, ALU.mult))
                    r(v.tensor_reduce(col(6, 2 + k), prod, AX_X, ALU.add))
                    v.tensor_copy(slot_idx[:, k, :], rt[:, 6, :, 2 + k]).then_inc(SEM["idx_ready"], 1)
                ends = gm_mem[:, 0:TILES * EXPERTS].rearrange("p (i e) -> p i e", e=EXPERTS)
                r(v.tensor_tensor(ends, incl.unsqueeze(1).broadcast_to([P, TILES, EXPERTS]),
                                  con("iota")[:, 0:TILES].unsqueeze(2).broadcast_to([P, TILES, EXPERTS]), ALU.is_le))
                of_tile = w_sb[:, 0:TILES]
                r(v.tensor_reduce(of_tile, ends, AX_X, ALU.add))
                r(v.tensor_scalar(of_tile, of_tile, float(EXPERTS - 1), None, ALU.min))
                v.tensor_copy(tile_exp[:, :], of_tile).then_inc(SEM["idx_ready"], 1)

            @block.gpsimd
            def _(pool):
                nc.gpsimd.memset(zeros, 0.0).then_inc(SEM["zero_set"], 1)
                pool.wait_ge(SEM["zero_set"], 1)
                pool.dma_start(x_slots.rearrange("(i p) d -> p i d", p=P),
                               zeros.unsqueeze(1).broadcast_to([P, TILES * SLOT // P, D])).then_inc(SEM["x_zeroed"], 16)
                pool.wait_ge(SEM["dr_stored"], 16 * DIL_H)
                for h in range(DIL_H):
                    skew = dil_rows[h:h + 1, P - 1:P - 1 + P * (DIL_ROW - 1)].rearrange("a (p y) -> (a p) y", y=DIL_ROW - 1)
                    pool.dma_start(bias_d[h], skew[:, 0:T]).then_inc(SEM["bias_loaded"], 16)
                pool.wait_ge(SEM["x_zeroed"], 16)
                pool.wait_ge(SEM["h_tok"], 2 * NT)
                for k in range(TOP_K):
                    pool.wait_ge(SEM["idx_ready"], k + 1)
                    for n in range(NT):
                        pool.indirect_dma_start(out=x_slots, out_offset=bass.IndirectOffsetOnAxis(ap=slot_idx[:, k, n:n + 1], axis=0),
                                                in_=h_rows[:, n, :], in_offset=None).then_inc(SEM["scattered"], 16)
                pool.wait_ge(SEM["scattered"], 16 * NT * TOP_K)

        for name in ["turned", "xs_act", "xs_dve", "gu_done", "silu_done", "he_ready", "down_done", "y_act", "y_dve"] + \
                [f"{what}{b}" for what in ("xs_loaded", "we_loaded", "ys_stored") for b in range(UNROLL)]:
            sem(name)
        ROUNDS = TILES // UNROLL
        we = slots[:, :, :, :].rearrange("p s c t -> p (s c t)").rearrange("p (b w) -> p b w", b=UNROLL)
        w_gu = [we[:, b, 0:KD * 2 * FF].rearrange("p (k f) -> p k f", k=KD) for b in range(UNROLL)]
        w_dn = [we[:, b, KD * 2 * FF:W_EXP].rearrange("p (f d) -> p f d", f=2) for b in range(UNROLL)]
        rows = hT[:, :, :].rearrange("p k t -> p (k t)")
        xs = [rows[:, b * D:(b + 1) * D] for b in range(2)] + [ztp[:, 0].rearrange("p u t -> p (u t)")]
        ys = [rows[:, (2 + b) * D:(3 + b) * D] for b in range(2)] + [ztp[:, 1].rearrange("p u t -> p (u t)")]
        xsT = [gm_mem[:, b * D:(b + 1) * D].rearrange("p (k t) -> p k t", k=KD) for b in range(UNROLL)]
        sil = [gm_mem[:, 3 * D + b * FF:3 * D + (b + 1) * FF] for b in range(UNROLL)]
        heT = [w_sb[:, 0:FF], w_sb[:, FF:2 * FF], u_sb[:, 0:FF]]
        halves = [slice(0, T), slice(T, 2 * T)]

        def rounds(engine, body):
            body(0, True, False)
            with engine.Fori(1, ROUNDS - 1) as it:
                body(it, False, False)
            body(ROUNDS - 1, False, True)

        with nc.Block() as block:
            @block.sync
            def _(sp):
                def load_rows(b, tile):
                    sp.dma_start(xs[b], x_slots[bass.ds(tile * SLOT, SLOT)]).then_inc(SEM[f"xs_loaded{b}"], 16)

                def load_weights(b, tile):
                    e = sp.value_load(tile_exp[0:1, bass.ds(tile, 1)], min_val=0, max_val=EXPERTS - 1)
                    sp.dma_start(we[:, b, :], experts[bass.ds(e, 1)].rearrange("a p w -> (a p) w")) \
                      .then_inc(SEM[f"we_loaded{b}"], 16)

                for b in range(UNROLL):
                    load_rows(b, b)
                    load_weights(b, b)
                with sp.Fori(0, ROUNDS - 1) as it:
                    for b in range(UNROLL):
                        sp.wait_ge(SEM["turned"], 2 * UNROLL * it + 2 * b + 2)
                        load_rows(b, UNROLL * it + (UNROLL + b))
                        sp.wait_ge(SEM["down_done"], 2 * UNROLL * it + 2 * b + 2)
                        load_weights(b, UNROLL * it + (UNROLL + b))

            @block.tensor
            def _(pe):
                def turn(b, it):
                    pe.wait_ge(SEM[f"xs_loaded{b}"], 16 * it + 16)
                    for i in range(2):
                        for k in range(4):
                            mm = nc.tensor.transpose(banks[:, i, k * P:k * P + P], xs[b][:, (4 * i + k) * P:(4 * i + k + 1) * P], ident)
                        mm.then_inc(SEM["turned"], 1)

                def body(it, first, last):
                    for b in range(UNROLL):
                        tile = UNROLL * it + b
                        pe.wait_ge(SEM[f"we_loaded{b}"], 16 * it + 16)
                        pe.wait_ge(SEM["xs_act"], tile + 1)
                        pe.wait_ge(SEM["xs_dve"], tile + 1)
                        if not first:
                            pe.wait_ge(SEM["he_ready"], tile - 2)
                        for f in range(4):
                            for k in range(KD):
                                mm = nc.tensor.matmul(banks[:, 2 + b, f * P:f * P + P], w_gu[b][:, k, f * P:f * P + P],
                                                      xsT[b][:, k, :], start=(k == 0), stop=(k == KD - 1))
                        mm.then_inc(SEM["gu_done"], 1)
                        if not (last and b == UNROLL - 1):
                            turn((b + 1) % UNROLL, it + (b + 1) // UNROLL)
                        pe.wait_ge(SEM["he_ready"], tile + 1)
                        for i in range(2):
                            if i == 0 and not (first and b < 2):
                                pe.wait_ge(SEM["y_dve"], tile - 1)
                            if i == 1 and not (first and b < 1):
                                pe.wait_ge(SEM["y_act"], tile)
                            for f in range(2):
                                mm = nc.tensor.matmul(banks[:, 5 + (2 * b + i) % 3], heT[b][:, f * P:f * P + P],
                                                      w_dn[b][:, f, halves[i]], start=(f == 0), stop=(f == 1))
                            mm.then_inc(SEM["down_done"], 1)

                turn(0, 0)
                rounds(pe, body)

            @block.scalar
            def _(act):
                def copy_turned(b, tile, early):
                    act.wait_ge(SEM["turned"], 2 * tile + 1)
                    if not early:
                        act.wait_ge(SEM["gu_done"], tile - 2)
                    nc.scalar.activation(xsT[b][:, 0:4, :].rearrange("p k t -> p (k t)"), banks[:, 0], ACT.Copy) \
                        .then_inc(SEM["xs_act"], 1)

                def body(it, first, last):
                    for b in range(UNROLL):
                        tile = UNROLL * it + b
                        act.wait_ge(SEM["gu_done"], tile + 1)
                        if not first:
                            act.wait_ge(SEM["he_ready"], tile - 2)
                        nc.scalar.activation(sil[b], banks[:, 2 + b, 0:FF], ACT.Silu).then_inc(SEM["silu_done"], 1)
                        if not (last and b == UNROLL - 1):
                            copy_turned((b + 1) % UNROLL, tile + 1, first and b < UNROLL - 1)
                        act.wait_ge(SEM["down_done"], 2 * tile + 1)
                        if not first:
                            act.wait_ge(SEM[f"ys_stored{b}"], 16 * it)
                        nc.scalar.activation(ys[b][:, halves[0]], banks[:, 5 + (2 * b) % 3], ACT.Copy).then_inc(SEM["y_act"], 1)

                copy_turned(0, 0, True)
                rounds(act, body)

            @block.vector
            def _(dve):
                def copy_turned(b, tile, early):
                    dve.wait_ge(SEM["turned"], 2 * tile + 2)
                    if not early:
                        dve.wait_ge(SEM["gu_done"], tile - 2)
                    nc.vector.tensor_copy(xsT[b][:, 4:8, :].rearrange("p k t -> p (k t)"), banks[:, 1]) \
                        .then_inc(SEM["xs_dve"], 1)

                def body(it, first, last):
                    for b in range(UNROLL):
                        tile = UNROLL * it + b
                        dve.wait_ge(SEM["silu_done"], tile + 1)
                        if not first:
                            dve.wait_ge(SEM["down_done"], 2 * tile - 4)
                        nc.vector.tensor_tensor(heT[b], banks[:, 2 + b, FF:2 * FF], sil[b], ALU.mult).then_inc(SEM["he_ready"], 1)
                        if not (last and b == UNROLL - 1):
                            copy_turned((b + 1) % UNROLL, tile + 1, first and b < UNROLL - 1)
                        dve.wait_ge(SEM["down_done"], 2 * tile + 2)
                        if not first:
                            dve.wait_ge(SEM[f"ys_stored{b}"], 16 * it)
                        nc.vector.tensor_copy(ys[b][:, halves[1]], banks[:, 5 + (2 * b + 1) % 3]).then_inc(SEM["y_dve"], 1)

                copy_turned(0, 0, True)
                rounds(dve, body)

            @block.gpsimd
            def _(pool):
                with pool.Fori(0, ROUNDS) as it:
                    for b in range(UNROLL):
                        tile = UNROLL * it + b
                        pool.wait_ge(SEM["y_act"], tile + 1)
                        pool.wait_ge(SEM["y_dve"], tile + 1)
                        pool.dma_start(y_slots[bass.ds(tile * SLOT, SLOT)], ys[b]).then_inc(SEM[f"ys_stored{b}"], 16)
                for b in range(UNROLL):
                    pool.wait_ge(SEM[f"ys_stored{b}"], 16 * ROUNDS)

        for name in ["z_added", "z_sq", "z_mean", "z_root", "z_out", "out_stored"] + [f"gathered{n}" for n in range(NT)]:
            sem(name)
        flat_slots = slots[:, :, :, :].rearrange("p s c t -> p (s c t)")
        back = [[flat_slots[:, (2 * n + k) * D:(2 * n + k + 1) * D] for k in range(TOP_K)] for n in range(NT)]
        z_var = hvar[:, 0:NT]

        with nc.Block() as block:
            @block.gpsimd
            def _(pool):
                for n in range(NT):
                    for k in range(TOP_K):
                        pool.indirect_dma_start(out=back[n][k], out_offset=None, in_=y_slots,
                                                in_offset=bass.IndirectOffsetOnAxis(ap=slot_idx[:, k, n:n + 1], axis=0)) \
                            .then_inc(SEM[f"gathered{n}"], 16)

            @block.vector
            def _(dve):
                v = nc.vector
                for n in range(NT):
                    dve.wait_ge(SEM[f"gathered{n}"], 16 * TOP_K)
                    for k in range(TOP_K):
                        v.scalar_tensor_tensor(x_rows[:, n, :], back[n][k], rt[:, 7, n, k:k + 1], x_rows[:, n, :], ALU.mult, ALU.add) \
                            .then_inc(SEM["z_added"], 1)
                        dve.wait_ge(SEM["z_added"], TOP_K * n + k + 1)
                dve.wait_ge(SEM["z_sq"], NT)
                v.tensor_scalar(z_var, z_var, 1.0 / D, RMS_EPS, ALU.mult, ALU.add).then_inc(SEM["z_mean"], 1)
                dve.wait_ge(SEM["z_root"], 1)
                v.reciprocal(z_var, z_var).then_inc(SEM["z_mean"], 1)
                dve.wait_ge(SEM["z_mean"], 2)
                for n in range(NT):
                    v.scalar_tensor_tensor(x_rows[:, n, :], x_rows[:, n, :], z_var[:, n:n + 1], fnorm, ALU.mult, ALU.mult) \
                        .then_inc(SEM["z_out"], 1)

            @block.scalar
            def _(act):
                for n in range(NT):
                    act.wait_ge(SEM["z_added"], TOP_K * (n + 1))
                    nc.scalar.activation(back[n][0], x_rows[:, n, :], ACT.Square, accum_out=z_var[:, n:n + 1]).then_inc(SEM["z_sq"], 1)
                act.wait_ge(SEM["z_mean"], 1)
                nc.scalar.activation(z_var, z_var, ACT.Sqrt).then_inc(SEM["z_root"], 1)

            @block.sync
            def _(sp):
                for n in range(NT):
                    sp.wait_ge(SEM["z_out"], n + 1)
                    sp.dma_start(out[n * P:(n + 1) * P], x_rows[:, n, :]).then_inc(SEM["out_stored"], 16)
                sp.wait_ge(SEM["out_stored"], 16 * NT)
        for name, n in given.items():
            assert n == PER[name] or name.startswith("wload"), (name, n, PER[name])


def pack(i):
    f = lambda n: np.asarray(i[n])
    col = lambda a: a.reshape(-1, P).T
    kcols = lambda a: a.reshape(a.shape[0] // P, P, a.shape[1]).transpose(1, 0, 2)

    def blocks(a):
        return [kcols(a[:, j:j + 256]).reshape(P, BLK) for j in range(0, a.shape[1], 256)]

    stream, lpar = [], []
    for l in range(LAYERS):
        w_in = f("w_in")[l]
        o = dict(pu=0, pg=512, q=1024, k=1536, v=2048, tg=2560, r=3072, wl=3584, rk=3648, rv=4160, al=4672, rg=4736,
                 gates=5248)
        stream += blocks(f("w_ada")[l])
        for name in ("r", "rk", "rv", "pu", "pg", "rg", "q", "k", "v", "tg"):
            stream += blocks(w_in[:, o[name]:o[name] + 512])
        wb = f("w_branch")[l]
        for cp in range(KD // 2):
            for n in range(3):
                a = o["gates"] + n * D + cp * 256
                stream += blocks(w_in[:, a:a + 256])
            for c in (2 * cp, 2 * cp + 1):
                part = wb[:, :, c * P:c * P + P].reshape(3 * CW, P, P).transpose(1, 0, 2).reshape(P, 12 * P)
                stream.append(np.concatenate([part, np.zeros((P, BLK - 12 * P), np.float32)], 1))
        stream += blocks(f("w_out")[l])
        mu = f("rwkv_shift_mu")[l]
        mu13 = np.concatenate([col(mu[0:512]), col(np.concatenate([mu[512:576], mu[1600:1664]])), col(mu[576:1088]),
                               col(mu[1088:1600])], 1)
        lora = np.concatenate([f("rwkv_w2")[l], f("rwkv_a2")[l]], 0)
        w_lora = np.concatenate([w_in[:, o["wl"]:o["wl"] + 64], w_in[:, o["al"]:o["al"] + 64]], 1)
        vecs = [col(f("norm_g")[l]), col(f("b_ada")[l]), col(f("pool_scale")[l]), col(f("ret_norm_g")[l]), mu13]
        vecs += [col(f("rwkv_" + n)[l].reshape(-1)) for n in ("w0", "a0", "k_k", "k_a", "r_k", "ln_w", "ln_b")]
        vecs += [f("pool_w")[l].transpose(1, 0, 2).reshape(P, 512), lora, kcols(w_lora).reshape(P, KD * P)]
        lpar.append(np.concatenate(vecs, 1))
    w2 = f("w_in_2")[0]
    stream += blocks(w2[:, 0:3072]) + blocks(f("w_out_2")[0])
    norms = np.concatenate([f("out_norm_dil_2")[0], f("out_norm_fox_2")[0]])
    zeros = lambda shape: np.zeros(shape, np.float32)
    tall = lambda a: np.concatenate([a, zeros((P - a.shape[0], a.shape[1]))], 0)
    w_route = np.concatenate([f("w_router_group_2")[0], f("w_router_expert_2")[0]], 1)
    b_route = np.concatenate([f("b_router_group_2")[0], f("b_router_expert_2")[0]])[None, :]
    rel = np.concatenate([f("rel_bias_2"), np.ones((1, DIL_H), np.float32)], 0)
    gpar = [col(f("c")[0]), col(f("final_g")), col(f("attn_norm_2")[0]), col(norms), col(f("ffn_norm_2")[0]),
            kcols(w2[:, 3072:3080]).reshape(P, KD * FOX_H), kcols(w_route).reshape(P, KD * ROUTE), tall(b_route),
            tall(f("b_forget_2")[0][:, None]), tall(rel)]
    wide = lambda a: a.reshape(EXPERTS, -1, P, a.shape[-1]).transpose(0, 2, 1, 3)
    gate_up = np.concatenate([wide(f("w_expert_gate_2")[0]), wide(f("w_expert_up_2")[0])], 3)
    experts = np.concatenate([gate_up.reshape(EXPERTS, P, -1), wide(f("w_expert_down_2")[0]).reshape(EXPERTS, P, -1)], 2)
    return {
        "wstream": np.stack(stream), "lparams": np.stack(lpar), "gparams": np.concatenate(gpar, 1),
        "consts": constants(), "distances": distance_table(), "experts": experts,
        "last_norm": np.broadcast_to(f("final_norm_2")[None, :], (P, D)),
        "x_in": np.ascontiguousarray(f("x")[0].T.reshape(KD, P, T).transpose(1, 0, 2).reshape(P, KD * T)),
        "pos_in": np.ascontiguousarray(f("positions")[0].reshape(NT, P).T.astype(np.int32)),
    }


def kernel(**inputs):
    import concourse.bacc as bacc
    from concourse.bass_utils import run_bass_kernel_spmd

    nc = bacc.Bacc("TRN2", target_bir_lowering=False, num_devices=1)
    arrays = {k: np.ascontiguousarray(a) for k, a in pack(inputs).items()}
    args = {k: nc.dram_tensor(k, a.shape, mybir.dt.from_np(a.dtype), kind="ExternalInput").ap() for k, a in arrays.items()}
    out = nc.dram_tensor("out", (T, D), F32, kind="ExternalOutput").ap()
    program(nc, out=out, **args)
    r = run_bass_kernel_spmd(nc, [arrays], core_ids=[0])
    got = r.results[0]["out"]
    return got.reshape(1, T, D)
```

```python
import math
from contextlib import ExitStack

import numpy as np

import concourse.bass as bass
from concourse import mybir

F32 = mybir.dt.float32
I32 = mybir.dt.int32
ALU = mybir.AluOpType
ACT = mybir.ActivationFunctionType
AX_X = mybir.AxisListType.X

P = 128
T = 512
NT = T // P
D = 1024
KD = D // P
W = 512
CW = W // P
LAYERS = 2
RET_H, RET_D = 4, 128
RW_H, RW_D = 8, 64
WINDOWS = (2, 4, 8, 16)
RMS_EPS = 1e-6
RET_EPS = 1e-5
RW_EPS = 64e-5
DECAY = -math.exp(-0.5)
OFF = -DECAY * P / 2
LEVELS = tuple(2 ** i for i in range(1, 7))
FOX_H = DIL_H = 8
HD = 64
ATT_SCALE = HD ** -0.5
NEG = -1e30
DIL_ROW = T + P
BUCKETS, MAX_DISTANCE = 32, 2048
DILATIONS, SEG = (1, 4, 16), 128

GROUPS, PER_GROUP, TOP_K, FF = 4, 8, 2, 256
EXPERTS = GROUPS * PER_GROUP
ROUTE = GROUPS + EXPERTS
SLOT = 80
EXTRA = (T * TOP_K - TOP_K) // SLOT
TILES = EXPERTS + EXTRA
UNROLL = 4

BLK = KD * 2 * P
RING = 4
ADA_B, PROJ_B, MERGE_B, OUT_B = 12, 20, 20, 4
LAYER_B = PROJ_B + MERGE_B + OUT_B
SETUP_B = LAYERS * ADA_B
ATT_B = 12 + 4

_names = [("pool_scale", 4), ("ret_norm_g", 4), ("mu", 13), ("w0", 4), ("a0", 4),
          ("k_k", 4), ("k_a", 4), ("r_k", 4), ("ln_w", 4), ("ln_b", 4), ("pool_w", 4 * P), ("lora", W),
          ("w_lora", KD * P)]
PCOL, NPAR = {}, 0
for _n, _w in _names:
    PCOL[_n] = (NPAR, NPAR + _w)
    NPAR += _w

_names = [("c", 8), ("norm_g", LAYERS * 8), ("b_ada", LAYERS * 24), ("final_g", 8), ("attn_norm", 8), ("out_norm", 8), ("ffn_norm", 8), ("w_f", KD * 8), ("w_route", KD * 36), ("b_route", 36),
          ("b_forget", 1), ("rel", 8)]
GCOL, NGLOB = {}, 0
for _n, _w in _names:
    GCOL[_n] = (NGLOB, NGLOB + _w)
    NGLOB += _w

_names = [("ident", P), ("blk64", P), ("mean", P), ("ones", P), ("gram", W), ("lvl", 6 * P), ("lvl1", 2 * P),
          ("ret_mask", W), ("ret_q", W), ("ret_k", 4), ("freq", 64), ("inv_count", 64), ("off", 2), ("causal", P),
          ("iota", 64), ("rev", 8), ("eps", 1)]
CCOL, NCONST = {}, 0
for _n, _w in _names:
    CCOL[_n] = (NCONST, NCONST + _w)
    NCONST += _w


def constants():
    i = np.arange(P)
    row, col = i[:, None], i[None, :]
    out = np.zeros((P, NCONST), np.float32)

    def put(name, a):
        out[:, CCOL[name][0]:CCOL[name][1]] = a

    put("ident", np.eye(P))
    put("blk64", row // RW_D == col // RW_D)
    put("mean", np.full((P, P), 1.0 / D))
    put("ones", np.ones((P, P)))
    strict, incl = row < col, row <= col
    put("gram", np.concatenate([strict, incl, strict, incl], 1))
    put("lvl", np.concatenate([((row // b) % 2 == 1) & (col // b == row // b - 1) for b in LEVELS], 1))
    pair = (row % 2 == 0) & (col == row + 1)
    put("lvl1", np.concatenate([pair, pair.T], 1))
    log_gamma = np.log1p(-(2.0 ** (-5.0 - np.arange(RET_H))))
    scale = RET_D ** -0.5
    put("ret_mask", np.concatenate([np.where(incl, np.exp(g * np.maximum(col - row, 0)), 0) * scale
                                    for g in log_gamma], 1))
    put("ret_q", np.concatenate([np.exp(g * (col + 1.0)) + 0 * row for g in log_gamma], 1))
    put("ret_k", np.stack([np.exp(g * (P - 1 - i)) * scale for g in log_gamma], 1))
    put("freq", (np.float32(10000.0) ** (-np.arange(64, dtype=np.float32) / np.float32(64)))[None, :])
    t = np.arange(16)
    put("inv_count", np.concatenate([1.0 / np.minimum(t + 1, w) for w in WINDOWS])[None, :])
    put("off", np.array([OFF, -OFF])[None, :])
    put("causal", np.where(col <= row, 0.0, NEG))
    put("iota", np.arange(64)[None, :])
    put("rev", 8.0 - np.arange(8)[None, :])
    put("eps", RMS_EPS)
    return out


def distance_table():
    dist = T - 1 - np.arange(DIL_ROW)
    d = np.maximum(dist, 0)
    exact = BUCKETS // 2
    log = np.log(np.maximum(d, 1).astype(np.float32) / np.float32(exact)) / np.float32(math.log(MAX_DISTANCE / exact))
    large = np.minimum(exact + (log * np.float32(BUCKETS - exact)).astype(np.int32), BUCKETS - 1)
    bucket = np.where(d < exact, d, large)
    count = sum(((dist >= 0) & (dist % r == 0) & (dist // r <= SEG)).astype(np.int32) for r in DILATIONS)
    out = np.zeros((BUCKETS + 1, DIL_ROW), np.float32)
    out[bucket, np.arange(DIL_ROW)] = dist >= 0
    out[BUCKETS] = np.where(count > 0, np.log(np.maximum(count, 1)), NEG)
    return out


def program(nc, wstream, lparams, gparams, consts, distances, experts, last_norm, x_in, pos_in, out):
    with ExitStack() as ctx:
        def sb(name, shape, dt=F32):
            return ctx.enter_context(nc.sbuf_tensor(name, shape, dt))

        SEM, PER, given = {}, {}, {}

        layer_ctx = ExitStack()

        def sem(name, per=1, owner=ctx):
            SEM[name] = owner.enter_context(nc.semaphore(name))
            PER[name] = per

        def inc(ins, name, by=1):
            given[name] = given.get(name, 0) + by
            ins.then_inc(SEM[name], by)

        wring = sb("wring", [P, RING, KD, 2 * P])
        xT = sb("xT", [P, KD, T])
        hT = sb("hT", [P, KD, T])
        lpar = sb("lpar", [P, NPAR])
        gpar = sb("gpar", [P, NGLOB])
        cst = sb("cst", [P, NCONST])
        slots = sb("slots", [P, 9, CW, T])
        br_pool = sb("br_pool", [P, CW, T])
        gm_mem = sb("gm_mem", [P, 4096])
        ztp = sb("ztp", [P, 3, 8, P])
        w_sb = sb("w_sb", [P, T])
        u_sb = sb("u_sb", [P, T])
        state = sb("state", [P, CW, P])
        rstd = sb("rstd", [P, T])
        mods = sb("mods", [P, LAYERS, 32])
        mod = sb("mod", [P, 32])
        omm = sb("omm", [P, 13 + CW])
        e_end = sb("e_end", [P, CW, NT])
        c_act = sb("c_act", [P, KD])
        posi = sb("posi", [P, NT], I32)
        posf = sb("posf", [P, NT])
        cosT = sb("cosT", [P, NT, 64])
        sinT = sb("sinT", [P, NT, 64])
        hsum = sb("hsum", [P, 32])
        hvar = sb("hvar", [P, 32])
        slot_idx = sb("slot_idx", [P, TOP_K, NT], I32)
        tile_exp = sb("tile_exp", [P, EXTRA + 1], I32)
        dram = lambda name, shape: nc.dram_tensor(name, shape, F32).ap()
        dil_rows = dram("dil_rows", (DIL_H, P * DIL_ROW))
        x_slots = dram("x_slots", (TILES * SLOT, D))
        y_slots = dram("y_slots", (TILES * SLOT, D))
        banks = ctx.enter_context(nc.psum_tensor("banks", [P, 8, T], F32))

        def par(name, c=None):
            a, b = PCOL[name]
            return lpar[:, a:b] if c is None else lpar[:, a + c:a + c + 1]

        def glob(name, c=None):
            a, b = GCOL[name]
            return gpar[:, a:b] if c is None else gpar[:, a + c:a + c + 1]

        def con(name, c=None):
            a, b = CCOL[name]
            return cst[:, a:b] if c is None else cst[:, a + c:a + c + 1]

        ident = con("ident")
        SL = [slots[:, i] for i in range(9)]
        R_, K_, X1, X2, X3, G_, V_, A_, KK = SL
        gm = gm_mem[:, :].rearrange("p (u k t) -> p u k t", u=8, k=4)
        zt, tt, pt = ztp[:, 0], ztp[:, 1], ztp[:, 2]
        b_tok, v_tok, k_tok, y_tok = (s.rearrange("p n f -> p n f") for s in (X1, G_, V_, X2))
        pool_u = gm_mem[:, 0:2048].rearrange("p (c t) -> p c t", c=CW)
        pool_gate = gm_mem[:, 2048:4096].rearrange("p (c t) -> p c t", c=CW)
        br_rwkv = X3
        rq_raw, rk_raw, rv_tok, ret_gate = X1, V_, KK, K_
        flat_ztp = ztp[:, :, :, :].rearrange("p a u t -> p (a u t)")
        rq_rot = flat_ztp[:, 0:2048].rearrange("p (n f) -> p n f", n=NT)
        rk_rot, qT, qdT = G_, R_, K_
        kT = gm_mem[:, 0:2048].rearrange("p (h t) -> p h t", h=RET_H)
        rot_tmp = [gm_mem[:, 2048 + 1024 * i:3072 + 1024 * i] for i in range(2)]
        k_tail, o_tok, br_ret, o_sq = X1, V_, X2, G_
        p_ret = [w_sb[:, :], u_sb[:, :]]
        sig_gate = slots[:, 6:9].rearrange("p s c t -> p (s c) t")
        mT = gm_mem[:, :].rearrange("p (c t) -> p c t", c=KD)

        jobs = []

        def job(name, drained, k):
            jobs.append((name, drained, k))

        for c in range(CW):
            job(f"r{c}", "mixed", 1 + c)
        job("wl", "mixed", 5)
        for c in range(CW):
            job(f"z{c}", "g_ready", 1 + c)
        for c in range(CW):
            job(f"a{c}", "a_ready", 1 + c)
        for c in range(CW):
            job(f"k{c}", "mixed", 6 + c)
        for c in range(CW):
            job(f"v{c}", "mixed", 10 + c)
        for c in range(CW):
            job(f"pu{c}", "pu_ready", 1 + c)
        for c in range(CW):
            job(f"kss{c}", "kss_ready", 1 + c)
        for c in range(CW):
            job(f"pg{c}", "pg_ready", 1 + c)
        for c in range(CW):
            job(f"py{c}", "pool_done", 1 + c)
        for c in range(CW):
            job(f"bs{c}", "bonus_ready", 1 + c)
        for i, what in enumerate("vbk"):
            for n in range(NT):
                job(f"t{what}{n}", "tok_ready", 1 + NT * i + n)
        for n in range(NT):
            for h in range(RW_H):
                job(f"gram{n}{h}", "gram_ready", 1 + 8 * n + h)
            for g in range(2):
                job(f"ti{n}{g}", "tinit_ready", 1 + 2 * n + g)
            for l in range(6):
                for g in range(2):
                    job(f"p{n}{l}{g}", "p_ready", 1 + 12 * n + 2 * l + g)
                for g in range(2):
                    if l < 5:
                        job(f"tn{n}{l}{g}", "t_ready", 1 + 10 * n + 2 * l + g)
                    job(f"zn{n}{l}{g}", "z_ready", 3 + 14 * n + 2 * l + g)
            job(f"w{n}", "w_ready", 1 + n)
            job(f"u{n}", "u_ready", 1 + n)
            job(f"y{n}", "y_ready", 1 + n)
            if n < NT - 1:
                job(f"s{n}", "s_added", 1 + n)
        for i, what in enumerate("qkv"):
            for b in range(2):
                for tp in range(2):
                    job(f"ret{what}{b}{tp}", "ret_tok", 1 + 4 * i + 2 * b + tp)
        for c in range(CW):
            job(f"rg{c}", "rg_ready", 1 + c)
        for h in range(RET_H):
            job(f"tq{h}", "qd_ready", 1 + h)
        for h in range(RET_H):
            job(f"tkr{h}", "kT_ready", 1 + h)
        for n in range(NT):
            job(f"sc{n}", "pret_ready", 1 + n)
            job(f"o{n}", "o_ready", 1 + n)
            if n < NT - 1:
                job(f"kv{n}", "R_ready", 1 + n)
        for c in range(CW):
            job(f"tg{c}", "retg_ready", 1 + c)
        for c in range(CW):
            job(f"ty{c}", "y_scaled", 1 + c)
        for h in range(RET_H):
            job(f"to{h}", "ret_done", 1 + h)
        for cp in range(KD // 2):
            for n in range(3):
                for cc in range(2):
                    job(f"g{cp}{n}{cc}", "gate_sig", 1 + 6 * cp + 2 * n + cc)
            for cc in range(2):
                for n in range(3):
                    job(f"b{cp}{cc}{n}", "merged", 1 + 5 * (2 * cp + cc) + (0, 1, 3)[n])
        for c in range(KD):
            job(f"wo{c}", "x_done", 1 + c)
        job("ss", "rms_sqrt", 1)
        NJ = len(jobs)
        JOB = {name: j for j, (name, _, _) in enumerate(jobs)}
        block_end = ["r1", "r3", "k1", "k3", "v1", "v3", "pu1", "pu3", "pg1", "pg3"]
        block_end += [f"ret{w}{b}1" for w in "qkv" for b in range(2)] + ["rg1", "rg3", "tg1", "tg3"]
        for cp in range(KD // 2):
            block_end += [f"g{cp}{n}1" for n in range(3)] + [f"b{cp}{cc}2" for cc in range(2)]
        block_end += [f"wo{c}" for c in range(1, KD, 2)]
        assert len(block_end) == LAYER_B
        FIRST = {"r": 0, "k": 2, "v": 4, "pu": 6, "pg": 8, "retq": 10, "retk": 12, "retv": 14, "rg": 16, "tg": 18,
                 "merge": PROJ_B, "wo": PROJ_B + MERGE_B}

        for s in range(RING):
            sem(f"wload{s}", 16 * LAYER_B // RING)
        for name in ("x_loaded", "const_loaded", "glob_loaded", "pos_loaded", "dist_loaded", "dr_full", "dr_drained", "dr_stored",
                     "ada_step", "ada_summed", "mods_step", "first_sq", "first_sum", "first_root"):
            sem(name)
        sem("c_ready")
        sem("rope_step")
        sem("rope_arg")
        sem("rope_ready")
        LAYER_SEMS = []
        for name, per in (("bank_full", NJ), ("params_loaded", 16), ("x_done", 8), ("mod_ready", 1), ("omm_ready", 2), ("xsq_ready", 8), ("xsq_summed", 7),
                          ("rms_ready", 1), ("rms_sqrt", 1),
                          ("h_scaled", 8), ("h_ready", 8), ("mix_scaled", 13), ("mixed", 13), ("wl_tanh", 1),
                          ("g_ready", 4), ("a_ready", 4), ("kk_ready", 2), ("kss_ready", 4), ("kss_sqrt", 1),
                          ("k_mod", 2), ("rk_ready", 1), ("kk_unit", 2), ("bonus_ready", 4),
                          ("pu_ready", 4), ("pg_ready", 4), ("pool_step", 10 * 2 + 4 * 4), ("pool_d", 4),
                          ("pool_done", 4), ("g_sum", 1), ("g_prev", 1), ("exp_prev", 1), ("exp_plus", 1),
                          ("exp_minus", 1), ("ar_ready", 2), ("bk_ready", 2), ("tok_ready", 12),
                          ("gram_ready", 32), ("z_masked", 8), ("tinit_ready", 8), ("p_ready", 48),
                          ("t_ready", 40), ("z_ready", 56), ("w_ready", 4), ("u_ready", 4), ("y_ready", 4),
                          ("s_added", 3), ("s_ready", 3), ("y_norm", 7), ("y_sqrt", 1), ("y_scaled", 4),
                          ("rwkv_done", 4), ("rg_ready", 4), ("ret_tok", 12), ("retg_ready", 4),
                          ("rot_step", 6), ("rot_ready", 2), ("qT_ready", 4), ("qd_ready", 4), ("kT_ready", 4),
                          ("ktail_ready", 1), ("pret_ready", 4), ("o_ready", 4), ("R_ready", 3), ("o_norm", 7),
                          ("o_sqrt", 1), ("ret_done", 4), ("gate_sig", 24), ("merged", 40)):
            sem(name, per, layer_ctx)
            LAYER_SEMS.append(name)

        HALF_ROW = DIL_ROW // 2
        DIST_FROM, MEAN_FROM = 4, 6
        dil_mem = slots[:, 0:3].rearrange("p s c t -> p (s c t)")
        dil_sb = [dil_mem[:, h * DIL_ROW:(h + 1) * DIL_ROW] for h in range(DIL_H)]
        dist_sb = gm_mem[0:BUCKETS + 1, 0:DIL_ROW]
        ada_acc = [[flat_ztp[:, (2 * i + j) * 256:(2 * i + j + 1) * 256] for j in range(2)] for i in range(3)]

        with nc.Block() as block:
            @block.sync
            def _(sp):
                def load_block(slot, index):
                    inc(sp.dma_start(wring[:, slot].rearrange("p k n -> p (k n)"),
                                     wstream[index].rearrange("a p n -> (a p) n")), f"wload{slot}", 16)

                sp.dma_start(gpar[:, :], gparams).then_inc(SEM["glob_loaded"], 16)
                load_block(0, slice(0, 1))
                sp.dma_start(cst[:, :], consts).then_inc(SEM["const_loaded"], 16)
                for b in range(1, RING):
                    load_block(b, slice(b, b + 1))
                sp.dma_start(posi[:, :], pos_in).then_inc(SEM["pos_loaded"], 16)
                sp.dma_start(dist_sb, distances).then_inc(SEM["dist_loaded"], 16)
                sp.dma_start(xT[:, :, :].rearrange("p k t -> p (k t)"), x_in).then_inc(SEM["x_loaded"], 16)
                for b in range(RING, SETUP_B + RING):
                    sp.wait_ge(SEM["ada_step"], KD * (b - RING + 1))
                    load_block(b % RING, slice(b, b + 1))

            @block.tensor
            def _(pe):
                def distance_row(j):
                    if j == 0:
                        pe.wait_ge(SEM["dist_loaded"], 16)
                    if j >= 4:
                        pe.wait_ge(SEM["dr_drained"], j - 3)
                    a = GCOL["rel"][0] + j // 2
                    nc.tensor.matmul(banks[:, 4 + j % 4, 0:HALF_ROW], gpar[0:BUCKETS + 1, a:a + 1].broadcast_to([BUCKETS + 1, P]),
                                     dist_sb[:, j % 2 * HALF_ROW:(j % 2 + 1) * HALF_ROW], start=True, stop=True) \
                        .then_inc(SEM["dr_full"], 1)

                pe.wait_ge(SEM["const_loaded"], 16)
                for b in range(SETUP_B):
                    pe.wait_ge(SEM["ada_step"], KD * (b + 1))
                    for m in range(2):
                        column, cols = banks[:, 0, 2 * b + m:2 * b + m + 1], slice(m * P, m * P + P)
                        for chain in range(2):
                            mm = nc.tensor.matmul(column, ada_acc[b % 3][chain][:, cols], con("ones")[:, 0:1],
                                                  start=(chain == 0), stop=(chain == 1))
                    mm.then_inc(SEM["ada_summed"], 1)
                    if DIST_FROM <= b < DIST_FROM + 2 * DIL_H:
                        distance_row(b - DIST_FROM)
                    if b % 2 == 0 and MEAN_FROM <= b < MEAN_FROM + 2 * KD:
                        k = (b - MEAN_FROM) // 2
                        pe.wait_ge(SEM["first_sq"], k + 1)
                        mm = nc.tensor.matmul(banks[:, 1], con("mean"), hT[:, k, :], start=(k == 0), stop=(k == KD - 1))
                        if k == KD - 1:
                            mm.then_inc(SEM["first_sum"], 1)

            @block.scalar
            def _(act):
                act.wait_ge(SEM["glob_loaded"], 16)
                nc.scalar.activation(c_act[:, :], glob("c"), ACT.Silu).then_inc(SEM["c_ready"], 1)
                act.wait_ge(SEM["const_loaded"], 16)
                for j in range(2 * DIL_H):
                    if j == MEAN_FROM - DIST_FROM:
                        act.wait_ge(SEM["x_loaded"], 16)
                        for k in range(KD):
                            nc.scalar.activation(hT[:, k, :], xT[:, k, :], ACT.Square).then_inc(SEM["first_sq"], 1)
                    if j == 2 * DIL_H - 2:
                        act.wait_ge(SEM["first_sum"], 1)
                        nc.scalar.activation(rstd[:, :], banks[:, 1], ACT.Sqrt, bias=con("eps")).then_inc(SEM["first_root"], 1)
                    act.wait_ge(SEM["dr_full"], j + 1)
                    nc.scalar.activation(dil_sb[j // 2][:, j % 2 * HALF_ROW:(j % 2 + 1) * HALF_ROW], banks[:, 4 + j % 4, 0:HALF_ROW],
                                         ACT.Copy).then_inc(SEM["dr_drained"], 1)
                for h in range(DIL_H):
                    act.wait_ge(SEM["dr_drained"], 2 * h + 2)
                    act.dma_start(dil_rows[h].rearrange("(p y) -> p y", y=DIL_ROW), dil_sb[h]).then_inc(SEM["dr_stored"], 16)
                act.wait_ge(SEM["rope_arg"], 1)
                nc.scalar.activation(sinT[:, :, :], sinT[:, :, :], ACT.Sin)
                nc.scalar.activation(cosT[:, :, :], cosT[:, :, :], ACT.Sin).then_inc(SEM["rope_ready"], 1)
                act.wait_ge(SEM["dr_stored"], 16 * DIL_H)

            @block.vector
            def _(dve):
                v = nc.vector
                def rotary_angles():
                    dve.wait_ge(SEM["const_loaded"], 16)
                    dve.wait_ge(SEM["pos_loaded"], 16)
                    n_rope = [0]
                    def rope(ins):
                        n_rope[0] += 1
                        ins.then_inc(SEM["rope_step"], 1)
                        dve.wait_ge(SEM["rope_step"], n_rope[0])
                    ang, turns = cosT[:, :, :], sinT[:, :, :]
                    rope(v.tensor_copy(posf[:, :], posi[:, :]))
                    for n in range(NT):
                        last = v.tensor_scalar(cosT[:, n, :], con("freq"), posf[:, n:n + 1], None, ALU.mult)
                    rope(last)
                    MAGIC = 1.5 * 2.0 ** 23
                    rope(v.tensor_scalar(turns, ang, 1.0 / (2 * math.pi), None, ALU.mult))
                    rope(v.tensor_scalar(turns, turns, MAGIC, None, ALU.add))
                    rope(v.tensor_scalar(turns, turns, MAGIC, None, ALU.subtract))
                    c1 = 6.28125
                    c2 = math.floor((2 * math.pi - c1) * 2 ** 20) / 2 ** 20
                    for part in (c1, c2, 2 * math.pi - c1 - c2):
                        rope(v.scalar_tensor_tensor(ang, turns, -part, ang, ALU.mult, ALU.add))
                    rope(v.tensor_scalar(turns, ang, math.pi - 1e-6, -(math.pi - 1e-6), ALU.min, ALU.max))
                    rope(v.scalar_tensor_tensor(ang, turns, -1.0, turns, ALU.mult, ALU.max))
                    v.tensor_scalar(ang, ang, -1.0, math.pi / 2, ALU.mult, ALU.add).then_inc(SEM["rope_arg"], 1)

                dve.wait_ge(SEM["c_ready"], 1)
                for b in range(SETUP_B):
                    if b == RING:
                        rotary_angles()
                    if b == SETUP_B - 1:
                        dve.wait_ge(SEM["first_root"], 1)
                        v.reciprocal(rstd[:, :], rstd[:, :])
                    dve.wait_ge(SEM[f"wload{b % RING}"], 16 * (b // RING + 1))
                    if b >= 3:
                        dve.wait_ge(SEM["ada_summed"], b - 2)
                    for k in range(KD):
                        acc, w_k, c_k = ada_acc[b % 3][k % 2], wring[:, b % RING, k, :], c_act[:, k:k + 1]
                        if k < 2:
                            ins = v.tensor_scalar(acc, w_k, c_k, None, ALU.mult)
                        else:
                            dve.wait_ge(SEM["ada_step"], KD * b + k - 1)
                            ins = v.scalar_tensor_tensor(acc, w_k, c_k, acc, ALU.mult, ALU.add)
                        ins.then_inc(SEM["ada_step"], 1)
                dve.wait_ge(SEM["ada_summed"], SETUP_B)
                parts = banks[:, 0, 0:LAYERS * 24].rearrange("p (l m) -> p l m", l=LAYERS)
                v.tensor_tensor(mods[:, :, 0:24], parts, glob("b_ada").rearrange("p (l m) -> p l m", l=LAYERS), ALU.add) \
                    .then_inc(SEM["mods_step"], 1)
                dve.wait_ge(SEM["mods_step"], 1)
                v.scalar_tensor_tensor(mods[:, :, 24:32], mods[:, :, 8:16], 1.0, glob("norm_g").rearrange("p (l m) -> p l m", l=LAYERS),
                                       ALU.add, ALU.mult)

        with nc.Fori(0, LAYERS) as L:
          with nc.Block() as block:
            @block.sync
            def _(sp):
                def load_block(slot, index):
                    inc(sp.dma_start(wring[:, slot].rearrange("p k n -> p (k n)"),
                                     wstream[index].rearrange("a p n -> (a p) n")), f"wload{slot}", 16)

                for b in range(LAYER_B):
                    sp.wait_ge(SEM["bank_full"], JOB[block_end[b]] + 1)
                    load_block(b % RING, bass.ds(L * LAYER_B + (SETUP_B + b + RING), 1))

            @block.tensor
            def _(pe):
                state_ = {"job": 0}

                def after(name, k=None):
                    pe.wait_ge(SEM[name], PER[name] if k is None else k)

                def open_bank(name):
                    j = state_["job"]
                    assert jobs[j][0] == name, (name, jobs[j])
                    if j >= 8:
                        after(*jobs[j - 8][1:])
                    state_["job"] = j + 1
                    return banks[:, j % 8]

                def full(mm):
                    inc(mm, "bank_full")

                def weights(b):
                    pe.wait_ge(SEM[f"wload{b % RING}"], L * PER[f"wload{b % RING}"] + 16 * ((SETUP_B + b) // RING + 1))
                    return wring[:, b % RING]

                def project(prefix, first, fresh=False):
                    for c in range(CW):
                        if c % 2 == 0:
                            wb = weights(first + c // 2)
                        o = open_bank(f"{prefix}{c}")
                        for k in range(KD):
                            if fresh and c == 0:
                                after("h_ready", k + 1)
                            mm = nc.tensor.matmul(o, wb[:, k, (c % 2) * P:(c % 2 + 1) * P], hT[:, k, :],
                                                  start=(k == 0), stop=(k == KD - 1))
                        full(mm)

                def project_tok(prefix, first):
                    for b in range(2):
                        wb = weights(first + b)
                        for tp in range(2):
                            o = open_bank(f"{prefix}{b}{tp}")
                            for ti in range(2):
                                n = 2 * tp + ti
                                for k in range(KD):
                                    mm = nc.tensor.matmul(o[:, ti * 256:ti * 256 + 256], hT[:, k, n * P:n * P + P],
                                                          wb[:, k, :], start=(k == 0), stop=(k == KD - 1))
                            full(mm)

                def transposes(name, tiles):
                    o = open_bank(name)
                    for i, s in enumerate(tiles):
                        mm = nc.tensor.transpose(o[:, i * P:i * P + P], s, ident)
                    full(mm)

                project("r", FIRST["r"], fresh=True)
                after("params_loaded")
                o = open_bank("wl")
                wl = par("w_lora").rearrange("p (k n) -> p k n", k=KD)
                for k in range(KD):
                    mm = nc.tensor.matmul(o, wl[:, k, :], hT[:, k, :], start=(k == 0), stop=(k == KD - 1))
                full(mm)
                after("wl_tanh")
                for name, p0 in (("z", 0), ("a", 64)):
                    for c in range(CW):
                        o = open_bank(f"{name}{c}")
                        full(nc.tensor.matmul(o, par("lora")[p0:p0 + 64, c * P:c * P + P], w_sb[p0:p0 + 64, :],
                                              start=True, stop=True))
                project("k", FIRST["k"])
                project("v", FIRST["v"])
                project("pu", FIRST["pu"])
                after("kk_ready")
                for c in range(CW):
                    o = open_bank(f"kss{c}")
                    full(nc.tensor.matmul(o, con("blk64"), X1[:, c, :], start=True, stop=True))
                project("pg", FIRST["pg"])
                for c in range(CW):
                    after("pool_d", c + 1)
                    o = open_bank(f"py{c}")
                    full(nc.tensor.matmul(o, par("pool_w")[:, c * P:c * P + P], pool_u[:, c, :], start=True, stop=True))
                after("rk_ready")
                for c in range(CW):
                    o = open_bank(f"bs{c}")
                    full(nc.tensor.matmul(o, con("blk64"), X3[:, c, :], start=True, stop=True))
                after("mixed")
                for n in range(NT):
                    transposes(f"tv{n}", [V_[:, c, n * P:n * P + P] for c in range(CW)])
                after("bk_ready", 1)
                for n in range(NT):
                    transposes(f"tb{n}", [A_[:, c, n * P:n * P + P] for c in range(CW)])
                after("bk_ready", 2)
                for n in range(NT):
                    transposes(f"tk{n}", [K_[:, c, n * P:n * P + P] for c in range(CW)])
                after("ar_ready")
                for n in range(NT):
                    t0 = n * P
                    for h in range(RW_H):
                        o = open_bank(f"gram{n}{h}")
                        p0, c = 64 * (h % 2), h // 2
                        for i, (lhs, rhs) in enumerate(((A_, KK), (A_, R_), (K_, KK), (K_, R_))):
                            mm = nc.tensor.matmul(o[:, i * P:i * P + P], lhs[p0:p0 + 64, c, t0:t0 + P],
                                                  rhs[p0:p0 + 64, c, t0:t0 + P], start=True, stop=True)
                        full(mm)
                    for g in range(2):
                        after("z_ready", 14 * n + 1 + g)
                        transposes(f"ti{n}{g}", [zt[:, u, :] for u in range(4 * g, 4 * g + 4)])
                    for l in range(6):
                        for g in range(2):
                            if l == 0:
                                after("tinit_ready", 2 * n + 1 + g)
                            else:
                                after("t_ready", 10 * n + 2 * (l - 1) + 1 + g)
                            o = open_bank(f"p{n}{l}{g}")
                            for i in range(4):
                                u = 4 * g + i
                                mm = nc.tensor.matmul(o[:, i * P:i * P + P], gm[:, u, 0, :], tt[:, u, :],
                                                      start=True, stop=True)
                            full(mm)
                        for g in range(2):
                            after("p_ready", 12 * n + 2 * l + 1 + g)
                            if l > 0:
                                after("z_ready", 14 * n + 2 * l + 1 + g)
                            if l < 5:
                                o = open_bank(f"tn{n}{l}{g}")
                                for i in range(4):
                                    u = 4 * g + i
                                    mm = nc.tensor.matmul(o[:, i * P:i * P + P], zt[:, u, :], pt[:, u, :],
                                                          start=True, stop=True)
                                full(mm)
                            o = open_bank(f"zn{n}{l}{g}")
                            for i in range(4):
                                u = 4 * g + i
                                mm = nc.tensor.matmul(o[:, i * P:i * P + P], pt[:, u, :], zt[:, u, :],
                                                      start=True, stop=True)
                            full(mm)
                    if n == 0:
                        after("tok_ready")
                    else:
                        after("s_ready", n)
                    o = open_bank(f"w{n}")
                    if n > 0:
                        for c in range(CW):
                            nc.tensor.matmul(o[:, c * P:c * P + P], KK[:, c, t0:t0 + P], state[:, c, :],
                                             start=(c == 0), stop=False, skip_group_check=True)
                    for h in range(RW_H):
                        mm = nc.tensor.matmul(o[:, h * 64:h * 64 + 64], gm[:, h, 2, :], v_tok[:, n, h * 64:h * 64 + 64],
                                              start=(n == 0 and h == 0), stop=(h == RW_H - 1), skip_group_check=True)
                    full(mm)
                    o_u, o_y = open_bank(f"u{n}"), open_bank(f"y{n}")
                    if n > 0:
                        for c in range(CW):
                            nc.tensor.matmul(o_y[:, c * P:c * P + P], R_[:, c, t0:t0 + P], state[:, c, :],
                                             start=(c == 0), stop=False, skip_group_check=True)
                    for h in range(RW_H):
                        cols = slice(h * 64, h * 64 + 64)
                        nc.tensor.matmul(o_y[:, cols], gm[:, h, 3, :], v_tok[:, n, cols],
                                         start=(n == 0 and h == 0), stop=False, skip_group_check=True)
                    after("w_ready", n + 1)
                    after("z_ready", 14 * n + 14)
                    for h in range(RW_H):
                        mm = nc.tensor.matmul(o_u[:, h * 64:h * 64 + 64], zt[:, h, :], w_sb[:, h * 64:h * 64 + 64],
                                              start=True, stop=True)
                    full(mm)
                    if n < NT - 1:
                        o_s = open_bank(f"s{n}")
                        for c in range(CW):
                            cols = slice(c * P, c * P + P)
                            nc.tensor.matmul(o_s[:, cols], k_tok[:, n, cols], v_tok[:, n, cols],
                                             start=(c == 0), stop=False, skip_group_check=True)
                    after("u_ready", n + 1)
                    for h in range(RW_H):
                        cols = slice(h * 64, h * 64 + 64)
                        mm = nc.tensor.matmul(o_y[:, cols], gm[:, h, 1, :], u_sb[:, cols],
                                              start=False, stop=(h == RW_H - 1), skip_group_check=True)
                    full(mm)
                    if n < NT - 1:
                        for c in range(CW):
                            cols = slice(c * P, c * P + P)
                            mm = nc.tensor.matmul(o_s[:, cols], b_tok[:, n, cols], u_sb[:, cols],
                                                  start=False, stop=(c == CW - 1), skip_group_check=True)
                        full(mm)
                for what in "qkv":
                    project_tok(f"ret{what}", FIRST[f"ret{what}"])
                project("rg", FIRST["rg"])
                after("rot_ready", 1)
                for h in range(RET_H):
                    transposes(f"tq{h}", [rq_rot[:, n, h * P:h * P + P] for n in range(NT)])
                after("rot_ready", 2)
                for h in range(RET_H):
                    transposes(f"tkr{h}", [rk_rot[:, n, h * P:h * P + P] for n in range(NT)])
                after("qd_ready")
                after("kT_ready")
                after("ktail_ready")
                for n in range(NT):
                    t0 = n * P
                    o = open_bank(f"sc{n}")
                    for h in range(RET_H):
                        mm = nc.tensor.matmul(o[:, h * P:h * P + P], kT[:, h, t0:t0 + P], qT[:, h, t0:t0 + P],
                                              start=True, stop=True)
                    full(mm)
                    after("pret_ready", n + 1)
                    if n > 0:
                        after("R_ready", n)
                    o = open_bank(f"o{n}")
                    for h in range(RET_H):
                        cols = slice(h * P, h * P + P)
                        mm = nc.tensor.matmul(o[:, cols], p_ret[n % 2][:, cols], rv_tok[:, n, cols],
                                              start=True, stop=(n == 0))
                        if n > 0:
                            mm = nc.tensor.matmul(o[:, cols], qdT[:, h, t0:t0 + P], state[:, h, :],
                                                  start=False, stop=True)
                    full(mm)
                    if n < NT - 1:
                        o = open_bank(f"kv{n}")
                        for h in range(RET_H):
                            cols = slice(h * P, h * P + P)
                            mm = nc.tensor.matmul(o[:, cols], k_tail[:, n, cols], rv_tok[:, n, cols],
                                                  start=True, stop=True)
                        full(mm)
                project("tg", FIRST["tg"])
                after("y_norm")
                for c in range(CW):
                    transposes(f"ty{c}", [y_tok[:, n, c * P:c * P + P] for n in range(NT)])
                after("o_norm")
                for h in range(RET_H):
                    transposes(f"to{h}", [o_tok[:, n, h * P:h * P + P] for n in range(NT)])
                after("ret_done")
                after("rwkv_done")
                for cp in range(KD // 2):
                    first = FIRST["merge"] + 5 * cp
                    for n in range(3):
                        wb = weights(first + n)
                        for cc in range(2):
                            o = open_bank(f"g{cp}{n}{cc}")
                            for k in range(KD):
                                mm = nc.tensor.matmul(o, wb[:, k, cc * P:cc * P + P], hT[:, k, :],
                                                      start=(k == 0), stop=(k == KD - 1))
                            full(mm)
                    for cc in range(2):
                        wb = weights(first + 3 + cc).rearrange("p k n -> p (k n)")
                        for n, br in enumerate((br_pool, br_ret, br_rwkv)):
                            o = open_bank(f"b{cp}{cc}{n}")
                            for k in range(CW):
                                at = (n * CW + k) * P
                                mm = nc.tensor.matmul(o, wb[:, at:at + P], br[:, k, :], start=(k == 0), stop=(k == CW - 1))
                            full(mm)
                after("merged")
                for c in range(KD):
                    if c % 2 == 0:
                        wb = weights(FIRST["wo"] + c // 2)
                    o = open_bank(f"wo{c}")
                    for k in range(KD):
                        mm = nc.tensor.matmul(o, wb[:, k, (c % 2) * P:(c % 2 + 1) * P], mT[:, k, :],
                                              start=(k == 0), stop=(k == KD - 1))
                    full(mm)
                o = open_bank("ss")
                after("xsq_summed")
                full(nc.tensor.matmul(o, con("mean"), hT[:, 0, :], start=True, stop=True))
                assert state_["job"] == NJ

            @block.scalar
            def _(act):
                def after(name, k=None):
                    act.wait_ge(SEM[name], PER[name] if k is None else k)

                def bank(name):
                    act.wait_ge(SEM["bank_full"], JOB[name] + 1)
                    return banks[:, JOB[name] % 8]

                act.dma_start(lpar[:, :], lparams[bass.ds(L, 1)].rearrange("a p n -> (a p) n")) \
                   .then_inc(SEM["params_loaded"], 16)
                inc(nc.scalar.activation(mod[:, :], mods[:, bass.ds(L, 1), :].rearrange("p a m -> p (a m)"), ACT.Copy), "mod_ready")
                after("mod_ready")
                for k in range(KD):
                    after("h_scaled", k + 1)
                    inc(nc.scalar.activation(hT[:, k, :], hT[:, k, :], ACT.Identity, bias=mod[:, k:k + 1]), "h_ready")
                after("omm_ready")
                after("params_loaded")
                for c in range(CW):
                    inc(nc.scalar.activation(R_[:, c, :], bank(f"r{c}"), ACT.Copy, scale=omm[:, c:c + 1]), "mix_scaled")
                inc(nc.scalar.activation(w_sb[:, :], bank("wl"), ACT.Copy, scale=omm[:, 4:5]), "mix_scaled")
                after("mixed", 5)
                inc(nc.scalar.activation(w_sb[0:64, :], w_sb[0:64, :], ACT.Tanh), "wl_tanh")
                for c in range(CW):
                    inc(nc.scalar.activation(G_[:, c, :], bank(f"z{c}"), ACT.Sigmoid, bias=par("w0", c)), "g_ready")
                for c in range(CW):
                    inc(nc.scalar.activation(A_[:, c, :], bank(f"a{c}"), ACT.Sigmoid, bias=par("a0", c)), "a_ready")
                for i, (z, name) in enumerate(((K_, "k"), (V_, "v"))):
                    for c in range(CW):
                        m = 5 + 4 * i + c
                        inc(nc.scalar.activation(z[:, c, :], bank(f"{name}{c}"), ACT.Copy, scale=omm[:, m:m + 1]),
                            "mix_scaled")
                for c in range(CW):
                    inc(nc.scalar.activation(pool_u[:, c, :], bank(f"pu{c}"), ACT.Copy), "pu_ready")
                after("kss_ready")
                inc(nc.scalar.activation(X2[:, :, :], X2[:, :, :], ACT.Sqrt), "kss_sqrt")
                for c in range(CW):
                    inc(nc.scalar.activation(pool_gate[:, c, :], bank(f"pg{c}"), ACT.Silu), "pg_ready")
                after("g_sum")
                nc.scalar.activation(e_end[:, :, :], X2[:, :, P - 1:T:P], ACT.Exp, scale=DECAY)
                inc(nc.scalar.activation(X1[:, :, :], X2[:, :, :], ACT.Exp, scale=DECAY, bias=con("off", 0)), "exp_plus")
                after("g_prev")
                inc(nc.scalar.activation(G_[:, :, :], G_[:, :, :], ACT.Exp, scale=DECAY, bias=con("off", 0)), "exp_prev")
                after("exp_plus")
                inc(nc.scalar.activation(X2[:, :, :], X2[:, :, :], ACT.Exp, scale=-DECAY, bias=con("off", 1)), "exp_minus")
                after("ar_ready")
                for n in range(NT):
                    inc(nc.scalar.activation(v_tok[:, n, :], bank(f"tv{n}"), ACT.Copy), "tok_ready")
                for n in range(NT):
                    inc(nc.scalar.activation(b_tok[:, n, :], bank(f"tb{n}"), ACT.Copy), "tok_ready")
                after("bonus_ready")
                for n in range(NT):
                    inc(nc.scalar.activation(k_tok[:, n, :], bank(f"tk{n}"), ACT.Copy), "tok_ready")
                for n in range(NT):
                    for g in range(2):
                        inc(nc.scalar.activation(tt[:, 4 * g:4 * g + 4, :].rearrange("p u t -> p (u t)"),
                                                 bank(f"ti{n}{g}"), ACT.Copy), "tinit_ready")
                    inc(nc.scalar.activation(w_sb[:, :], bank(f"w{n}"), ACT.Copy), "w_ready")
                    if n == 0:
                        after("bk_ready")
                    inc(nc.scalar.activation(y_tok[:, n, :], bank(f"y{n}"), ACT.Copy), "y_ready")
                for z, what in ((rq_raw, "q"), (rk_raw, "k"), (rv_tok, "v")):
                    for b in range(2):
                        for tp in range(2):
                            o = bank(f"ret{what}{b}{tp}").rearrange("p (n f) -> p n f", n=2)
                            inc(nc.scalar.activation(z[:, 2 * tp:2 * tp + 2, b * 256:b * 256 + 256], o, ACT.Copy), "ret_tok")
                        if what == "q" and b == 0:
                            after("y_norm", 5)
                            inc(nc.scalar.activation(hvar[:, :], hvar[:, :], ACT.Sqrt), "y_sqrt")
                for c in range(CW):
                    inc(nc.scalar.activation(A_[:, c, :], bank(f"rg{c}"), ACT.Silu), "rg_ready")
                for h in range(RET_H):
                    inc(nc.scalar.activation(qT[:, h, :], bank(f"tq{h}"), ACT.Copy), "qT_ready")
                for h in range(RET_H):
                    inc(nc.scalar.activation(kT[:, h, :], bank(f"tkr{h}"), ACT.Copy), "kT_ready")
                for n in range(NT):
                    inc(nc.scalar.activation(o_tok[:, n, :], bank(f"o{n}"), ACT.Copy), "o_ready")
                for c in range(CW):
                    inc(nc.scalar.activation(ret_gate[:, c, :], bank(f"tg{c}"), ACT.Silu), "retg_ready")
                    if c == 0:
                        after("o_norm", 5)
                        inc(nc.scalar.activation(hvar[:, 0:16], hvar[:, 0:16], ACT.Sqrt), "o_sqrt")
                for cp in range(KD // 2):
                    for n in range(3):
                        for cc in range(2):
                            if cp >= 2:
                                after("merged", 5 * (2 * cp - 4 + cc) + (1, 2, 4)[n])
                            elif cp == 0 and n == 0 and cc == 0:
                                after("ret_done")
                            i = 6 * (cp % 2) + 2 * n + cc
                            inc(nc.scalar.activation(sig_gate[:, i, :], bank(f"g{cp}{n}{cc}"), ACT.Sigmoid), "gate_sig")
                for k in range(KD):
                    after("x_done", k + 1)
                    inc(nc.scalar.activation(hT[:, k, :], xT[:, k, :], ACT.Square), "xsq_ready")
                inc(nc.scalar.activation(rstd[:, :], bank("ss"), ACT.Sqrt, bias=con("eps")), "rms_sqrt")

            @block.vector
            def _(dve):
                v = nc.vector

                def after(name, k=None):
                    dve.wait_ge(SEM[name], PER[name] if k is None else k)

                def bank(name):
                    dve.wait_ge(SEM["bank_full"], JOB[name] + 1)
                    return banks[:, JOB[name] % 8]

                done = {}

                def step(ins, name):
                    inc(ins, name)
                    done[name] = done.get(name, 0) + 1
                    after(name, done[name])

                after("mod_ready")
                for k in range(KD):
                    inc(v.scalar_tensor_tensor(hT[:, k, :], xT[:, k, :], mod[:, 24 + k:25 + k], rstd[:, :], ALU.mult, ALU.mult),
                        "h_scaled")
                after("params_loaded")
                mu = par("mu")
                inc(v.tensor_scalar(omm[:, 0:13], mu, -1.0, 1.0, ALU.mult, ALU.add), "omm_ready")
                inc(v.tensor_scalar(omm[:, 13:17], par("k_a"), -1.0, 1.0, ALU.mult, ALU.add), "omm_ready")

                def mix(z, m, name):
                    o = bank(name)
                    after("mix_scaled", m + 1)
                    inc(v.scalar_tensor_tensor(z[:, 1:T], o[:, 0:T - 1], mu[:, m:m + 1], z[:, 1:T], ALU.mult, ALU.add),
                        "mixed")

                for c in range(CW):
                    mix(R_[:, c, :], c, f"r{c}")
                mix(w_sb[:, :], 4, "wl")
                for c in range(CW):
                    mix(K_[:, c, :], 5 + c, f"k{c}")
                after("mixed", 9)
                for c in range(CW):
                    last = v.tensor_scalar(KK[:, c, :], K_[:, c, :], par("k_k", c), None, ALU.mult)
                inc(last, "kk_ready")
                after("kk_ready", 1)
                inc(v.tensor_tensor(X1[:, :, :], KK[:, :, :], KK[:, :, :], ALU.mult), "kk_ready")
                for c in range(CW):
                    mix(V_[:, c, :], 9 + c, f"v{c}")
                after("a_ready")
                for c in range(CW):
                    last = v.tensor_scalar(X3[:, c, :], A_[:, c, :], par("k_a", c), omm[:, 13 + c:14 + c], ALU.mult, ALU.add)
                step(last, "k_mod")
                step(v.tensor_tensor(K_[:, :, :], K_[:, :, :], X3[:, :, :], ALU.mult), "k_mod")
                for c in range(CW):
                    last = v.scalar_tensor_tensor(X3[:, c, :], R_[:, c, :], par("r_k", c), K_[:, c, :], ALU.mult, ALU.mult)
                inc(last, "rk_ready")
                for c in range(CW):
                    inc(v.tensor_scalar(X2[:, c, :], bank(f"kss{c}"), 1e-24, None, ALU.max), "kss_ready")
                after("kss_sqrt")
                step(v.reciprocal(X2[:, :, :], X2[:, :, :]), "kk_unit")
                step(v.tensor_tensor(KK[:, :, :], KK[:, :, :], X2[:, :, :], ALU.mult), "kk_unit")
                v.tensor_tensor(A_[:, :, :], A_[:, :, :], KK[:, :, :], ALU.mult)
                after("g_ready")
                for c in range(CW):
                    for n in range(NT):
                        t0 = n * P
                        last = v.tensor_tensor_scan(X2[:, c, t0:t0 + P], con("ones"), G_[:, c, t0:t0 + P], 0.0,
                                                    ALU.mult, ALU.add)
                step(last, "g_sum")
                inc(v.tensor_tensor(G_[:, :, :], X2[:, :, :], G_[:, :, :], ALU.subtract), "g_prev")
                for c in range(CW):
                    o = bank(f"py{c}")
                    after("pg_ready", c + 1)
                    inc(v.scalar_tensor_tensor(br_pool[:, c, :], o, par("pool_scale", c), pool_gate[:, c, :],
                                               ALU.mult, ALU.mult), "pool_done")
                after("mixed")
                for c in range(CW):
                    inc(v.tensor_tensor(X3[:, c, :], bank(f"bs{c}"), V_[:, c, :], ALU.mult), "bonus_ready")
                after("exp_plus")
                inc(v.tensor_tensor(R_[:, :, :], R_[:, :, :], X1[:, :, :], ALU.mult), "ar_ready")
                after("exp_prev")
                inc(v.scalar_tensor_tensor(KK[:, :, :], KK[:, :, :], -1.0, G_[:, :, :], ALU.mult, ALU.mult), "ar_ready")
                after("exp_minus")
                inc(v.tensor_tensor(A_[:, :, :], A_[:, :, :], X2[:, :, :], ALU.mult), "bk_ready")
                inc(v.tensor_tensor(K_[:, :, :], K_[:, :, :], X2[:, :, :], ALU.mult), "bk_ready")

                flat = lambda a, g: a[:, 4 * g:4 * g + 4, :]
                lvl1 = con("lvl1")
                for n in range(NT):
                    for g in range(2):
                        for h in range(4 * g, 4 * g + 4):
                            inc(v.tensor_tensor(gm[:, h].rearrange("p k t -> p (k t)"), bank(f"gram{n}{h}"), con("gram"), ALU.mult),
                                "gram_ready")
                        after("gram_ready", 8 * n + 4 * g + 4)
                        step(v.tensor_tensor(flat(zt, g), gm[:, 4 * g:4 * g + 4, 0, :],
                                             lvl1[:, 0:P].unsqueeze(1).broadcast_to([P, 4, P]), ALU.mult), "z_masked")
                        inc(v.tensor_tensor(flat(zt, g), flat(zt, g), ident.unsqueeze(1).broadcast_to([P, 4, P]), ALU.add),
                            "z_ready")
                    for l in range(6):
                        mask = con("lvl")[:, l * P:l * P + P].unsqueeze(1).broadcast_to([P, 4, P])
                        for g in range(2):
                            o = bank(f"p{n}{l}{g}").rearrange("p (u t) -> p u t", u=4)
                            inc(v.tensor_tensor(flat(pt, g), o, mask, ALU.mult), "p_ready")
                        for g in range(2):
                            if l < 5:
                                o = bank(f"tn{n}{l}{g}").rearrange("p (u t) -> p u t", u=4)
                                if l == 0:
                                    after("tinit_ready", 2 * n + 1 + g)
                                else:
                                    after("t_ready", 10 * n + 2 * (l - 1) + 1 + g)
                                inc(v.tensor_tensor(flat(tt, g), o, flat(tt, g), ALU.add), "t_ready")
                            o = bank(f"zn{n}{l}{g}").rearrange("p (u t) -> p u t", u=4)
                            after("z_ready", 14 * n + 2 * l + 1 + g)
                            inc(v.tensor_tensor(flat(zt, g), o, flat(zt, g), ALU.add), "z_ready")
                    inc(v.tensor_copy(u_sb[:, :], bank(f"u{n}")), "u_ready")
                    if n < NT - 1:
                        flat_state = state[:, :, :].rearrange("p c f -> p (c f)")
                        o = bank(f"s{n}")
                        if n == 0:
                            step(v.tensor_copy(flat_state, o), "s_added")
                        else:
                            step(v.tensor_tensor(flat_state, o, flat_state, ALU.add), "s_added")
                        for c in range(CW):
                            last = v.scalar_tensor_tensor(state[:, c, :], state[:, c, :], e_end[:, c, n:n + 1], con("blk64"),
                                                          ALU.mult, ALU.mult)
                        inc(last, "s_ready")
                        after("s_ready", n + 1)

                def head_norm(z, squares, heads, width, eps, name, sqrt_name):
                    z3 = z.rearrange("p n (h d) -> p (n h) d", d=width)
                    q3 = squares.rearrange("p n (h d) -> p (n h) d", d=width)
                    mean, var = hsum[:, 0:heads], hvar[:, 0:heads]
                    wide = [a.unsqueeze(2).broadcast_to([P, heads, width]) for a in (mean, var)]
                    step(v.tensor_reduce(mean, z3, AX_X, ALU.add), name)
                    step(v.scalar_tensor_tensor(z3, wide[0], -1.0 / width, z3, ALU.mult, ALU.add), name)
                    step(v.tensor_tensor(q3, z3, z3, ALU.mult), name)
                    step(v.tensor_reduce(var, q3, AX_X, ALU.add), name)
                    step(v.tensor_scalar(var, var, 1.0 / width, eps, ALU.mult, ALU.add), name)
                    after(sqrt_name)
                    step(v.reciprocal(var, var), name)
                    step(v.tensor_tensor(z3, z3, wide[1], ALU.mult), name)

                after("y_ready")
                head_norm(y_tok, G_, 32, RW_D, RW_EPS, "y_norm", "y_sqrt")
                for i, (raw, rot) in enumerate(((rq_raw, rq_rot), (rk_raw, rk_rot))):
                    after("ret_tok", 4 * i + 4)
                    x = raw.rearrange("p n (h e d) -> p n h e d", h=RET_H, e=2)
                    y = rot.rearrange("p n (h e d) -> p n h e d", h=RET_H, e=2)
                    t1, t2 = (a.rearrange("p (n h d) -> p n h d", n=NT, h=RET_H) for a in rot_tmp)
                    cs, sn = (a[:, :, :].unsqueeze(2).broadcast_to([P, NT, RET_H, 64]) for a in (cosT, sinT))
                    if i == 1:
                        after("rot_ready", 1)
                    v.tensor_tensor(t1, x[:, :, :, 0, :], cs, ALU.mult)
                    step(v.tensor_tensor(t2, x[:, :, :, 1, :], sn, ALU.mult), "rot_step")
                    step(v.tensor_tensor(y[:, :, :, 0, :], t1, t2, ALU.subtract), "rot_step")
                    v.tensor_tensor(t1, x[:, :, :, 0, :], sn, ALU.mult)
                    step(v.tensor_tensor(t2, x[:, :, :, 1, :], cs, ALU.mult), "rot_step")
                    inc(v.tensor_tensor(y[:, :, :, 1, :], t1, t2, ALU.add), "rot_ready")
                after("rot_ready")
                for h in range(RET_H):
                    cols = slice(h * P, h * P + P)
                    last = v.tensor_scalar(k_tail[:, :, cols], rk_rot[:, :, cols], con("ret_k", h), None, ALU.mult)
                inc(last, "ktail_ready")
                for h in range(RET_H):
                    o = bank(f"tq{h}").rearrange("p (n t) -> p n t", n=NT)
                    after("qT_ready", h + 1)
                    decay = con("ret_q")[:, h * P:h * P + P].unsqueeze(1).broadcast_to([P, NT, P])
                    inc(v.tensor_tensor(qdT[:, h, :].rearrange("p (n t) -> p n t", n=NT), o, decay, ALU.mult), "qd_ready")
                for n in range(NT):
                    inc(v.tensor_tensor(p_ret[n % 2], bank(f"sc{n}"), con("ret_mask"), ALU.mult), "pret_ready")
                    if n < NT - 1:
                        o = bank(f"kv{n}")
                        if n == 0:
                            last = v.tensor_copy(state[:, :, :].rearrange("p h e -> p (h e)"), o)
                        else:
                            for h in range(RET_H):
                                decay = math.exp(math.log1p(-(2.0 ** (-5.0 - h))) * P)
                                last = v.scalar_tensor_tensor(state[:, h, :], state[:, h, :], decay, o[:, h * P:h * P + P],
                                                              ALU.mult, ALU.add)
                        inc(last, "R_ready")
                        after("R_ready", n + 1)
                after("o_ready")
                head_norm(o_tok, o_sq, 16, RET_D, RET_EPS, "o_norm", "o_sqrt")
                after("rg_ready")
                for c in range(CW):
                    step(v.scalar_tensor_tensor(br_rwkv[:, c, :], bank(f"ty{c}"), par("ln_w", c), br_rwkv[:, c, :], ALU.mult, ALU.add),
                         "y_scaled")
                    inc(v.scalar_tensor_tensor(br_rwkv[:, c, :], br_rwkv[:, c, :], par("ln_b", c), A_[:, c, :], ALU.add, ALU.mult),
                        "rwkv_done")
                after("retg_ready")
                for h in range(RET_H):
                    inc(v.scalar_tensor_tensor(br_ret[:, h, :], bank(f"to{h}"), par("ret_norm_g", h), ret_gate[:, h, :],
                                               ALU.mult, ALU.mult), "ret_done")
                for cp in range(KD // 2):
                    for cc in range(2):
                        c = 2 * cp + cc
                        for n in range(3):
                            after("gate_sig", 6 * cp + 2 * n + cc + 1)
                            o = bank(f"b{cp}{cc}{n}")
                            sig = sig_gate[:, 6 * (cp % 2) + 2 * n + cc, :]
                            part = (mT[:, c, :], w_sb[:, :], u_sb[:, :])[n]
                            step(v.tensor_tensor(part, o, sig, ALU.mult), "merged")
                            if n > 0:
                                step(v.tensor_tensor(mT[:, c, :], mT[:, c, :], part, ALU.add), "merged")
                def add_square(k):
                    after("xsq_ready", k + 1)
                    step(v.tensor_tensor(hT[:, 0, :], hT[:, 0, :], hT[:, k, :], ALU.add), "xsq_summed")

                for c in range(KD):
                    inc(v.scalar_tensor_tensor(xT[:, c, :], bank(f"wo{c}"), mod[:, 16 + c:17 + c], xT[:, c, :],
                                               ALU.mult, ALU.add), "x_done")
                    if c >= 2:
                        add_square(c - 1)
                add_square(KD - 1)
                after("rms_sqrt")
                inc(v.reciprocal(rstd[:, :], rstd[:, :]), "rms_ready")

            @block.gpsimd
            def _(pool):
                g = nc.gpsimd

                count = [0]

                def step(ins):
                    inc(ins, "pool_step")
                    count[0] += 1
                    pool.wait_ge(SEM["pool_step"], count[0])

                tmp = [zt.rearrange("p u t -> p (u t)")[:, i * T:i * T + T] for i in range(2)]
                fix = tt.rearrange("p u t -> p (u t)")[:, 0:16]
                for i, w in enumerate(WINDOWS):
                    u = pool_u[:, i, :]
                    pool.wait_ge(SEM["pu_ready"], i + 1)
                    src, lag = u, 1
                    while lag < w:
                        dst = tmp[0] if src is not tmp[0] else tmp[1]
                        inc(g.tensor_copy(dst[:, 0:lag], src[:, 0:lag]), "pool_step")
                        count[0] += 1
                        step(g.tensor_tensor(dst[:, lag:T], src[:, lag:T], src[:, 0:T - lag], ALU.add))
                        src, lag = dst, 2 * lag
                    step(g.tensor_tensor(fix, src[:, 0:16], con("inv_count")[:, 16 * i:16 * i + 16], ALU.mult))
                    step(g.tensor_tensor(fix, fix, u[:, 0:16], ALU.subtract))
                    step(g.tensor_scalar(src, src, 1.0 / w, None, ALU.mult))
                    step(g.tensor_tensor(u, src, u, ALU.subtract))
                    inc(g.tensor_copy(u[:, 0:16], fix), "pool_d")

          numbers = [SEM[name].num for name in LAYER_SEMS]
          assert numbers == list(range(numbers[0], numbers[-1] + 1))
          nc.sync.sem_clear(range(numbers[0], numbers[-1] + 1))
          nc.all_engine_barrier()
        layer_ctx.close()
        jobs = []
        job("ss1", "n_root", 1)
        job("f", "f_step", 1)
        for i, what in enumerate(("qd", "kd", "vd", "qf", "kf", "vf")):
            for c in range(CW):
                job(f"{what}{c}", "qkv_ready", 4 * i + c + 1)
        for h in range(FOX_H):
            job(f"nc{h}", "nc_ready", h + 1)
        heads = [(kind, tb, h) for kind in range(2) for tb in range(NT) for h in range(DIL_H)]
        for i in range(-2, len(heads)):
            if i + 2 < len(heads):
                job(f"s{i + 2}", "s_shifted", i + 3)
            if i >= 0:
                job(f"p{i}", "pt_ready", i + 1)
        for c in range(KD):
            job(f"ot{c}", "oT_ready", c + 1)
        for c in range(KD):
            job(f"ao{c}", "x_att", c + 1)
        job("ss2", "n_root", 2)
        job("route", "route_step", 1)
        for n in range(NT):
            for i in range(2):
                job(f"hk{n}{i}", "h_tok", 2 * n + i + 1)
        job("rank", "rank_read", 1)
        for n in range(NT):
            for i in range(2):
                job(f"xk{n}{i}", "x_tok", 2 * n + i + 1)
        RB = 6
        JOB = {name: j for j, (name, _, _) in enumerate(jobs)}
        DRAIN = {name: (sem_name, k) for name, sem_name, k in jobs}
        att_jobs = list(jobs)
        att_block_end = [f"{w}{c}" for w in ("qd", "kd", "vd", "qf", "kf", "vf") for c in (1, 3)]
        att_block_end += [f"ao{c}" for c in range(1, KD, 2)]

        for name in ("att_full", "bias_loaded", "zero_set", "x_zeroed", "fnorm_loaded",
                     "n_sq", "sq_summed", "n_mean", "n_root", "n_out", "f_step", "f_act", "negc_step", "qkv_ready", "nc_ready",
                     "s_shifted", "s_max", "s_exp", "pt_ready", "pv_step", "o_step", "o_sq", "o_root", "o_scaled",
                     "oT_ready", "x_att", "route_step", "route_exp", "m_ready", "rank_read", "h_tok", "x_tok", "idx_ready",
                     "scattered"):
            sem(name)

        qd, kd, vd, qf, kf, vf = SL[:6]
        o_tok = [SL[6], SL[7]]
        bias_d = [SL[8][:, h, :] for h in range(4)] + [br_pool[:, h, :] for h in range(4)]
        neg_c = gm_mem[:, :].rearrange("p (h t) -> p h t", h=FOX_H)
        fnorm = lpar[:, D:2 * D]
        att_stat = cosT[:, :, :].rearrange("p a b -> p (a b)")[:, 0:4 * DIL_H * NT].rearrange("p (s i) -> p s i", s=2)
        squares_mem = slots[:, 6:8].rearrange("p s c t -> p (s c) t")
        s_buf = [flat_ztp[:, i * T:i * T + T] for i in range(4)]
        p_buf = [flat_ztp[:, i * T:i * T + T] for i in range(4, 6)]
        f_sb, f_tmp = w_sb[0:FOX_H, :], u_sb[0:FOX_H, :]
        oT = hT
        zeros = lpar[:, 0:D]
        h_rows = wring[:, 0:2].rearrange("p s k n -> p (s k n)").rearrange("p (n d) -> p n d", n=NT)
        x_rows = wring[:, 2:4].rearrange("p s k n -> p (s k n)").rearrange("p (n d) -> p n d", n=NT)
        flat_pool = br_pool[:, :, :].rearrange("p c t -> p (c t)")
        rt = flat_pool[:, 0:26 * EXPERTS].rearrange("p (i n g) -> p i n g", n=NT, g=PER_GROUP)
        route = flat_pool[:, 26 * EXPERTS:26 * EXPERTS + NT * ROUTE].rearrange("p (n e) -> p n e", n=NT)
        n_max, n_sum = att_stat[:, 0, :], att_stat[:, 1, :]

        for name in ["turned", "xs_act", "xs_dve", "gu_done", "silu_done", "he_ready", "down_done", "y_act", "y_dve"] + \
                [f"{what}{b}" for what in ("xs_loaded", "gu_loaded", "dn_loaded", "ys_stored") for b in range(UNROLL)]:
            sem(name)
        ROUNDS = EXPERTS // UNROLL
        EARLY = 3
        GU, DN = KD * 2 * FF, 2 * D
        flat_slots = slots[:, 0:8].rearrange("p s c t -> p (s c t)")
        flat_x = xT[:, :, :].rearrange("p k t -> p (k t)")
        gu_mem = [flat_slots[:, b * GU:(b + 1) * GU] for b in range(UNROLL)]
        dn_mem = [flat_x[:, 0:DN], flat_x[:, DN:2 * DN], SL[8].rearrange("p c t -> p (c t)"), wring[:, 0].rearrange("p k n -> p (k n)")]
        w_gu = [m.rearrange("p (k f) -> p k f", k=KD) for m in gu_mem]
        w_dn = [m.rearrange("p (f d) -> p f d", f=2) for m in dn_mem]

        with nc.Block() as block:
            @block.sync
            def _(sp):
                sp.dma_start(fnorm, last_norm).then_inc(SEM["fnorm_loaded"], 16)
                for b in range(ATT_B - RING):
                    sp.wait_ge(SEM["att_full"], JOB[att_block_end[b]] + 1)
                    index = SETUP_B + LAYERS * LAYER_B + b + RING
                    sp.dma_start(wring[:, b % RING].rearrange("p k n -> p (k n)"), wstream[index]) \
                      .then_inc(SEM[f"wload{b % RING}"], 16)
                sp.wait_ge(SEM["pv_step"], len(heads))
                sp.dma_start(dn_mem[2], experts[2, :, GU:GU + DN]).then_inc(SEM["dn_loaded2"], 16)
                for b in range(EARLY):
                    sp.dma_start(gu_mem[b], experts[b, :, 0:GU]).then_inc(SEM[f"gu_loaded{b}"], 16)

            @block.tensor
            def _(pe):
                at = [0]

                def after(name, k):
                    pe.wait_ge(SEM[name], k)

                def open_bank(name):
                    j = at[0]
                    assert att_jobs[j][0] == name, (name, att_jobs[j])
                    if j >= RB:
                        after(*att_jobs[j - RB][1:])
                    at[0] = j + 1
                    return banks[:, j % RB]

                def full(mm):
                    mm.then_inc(SEM["att_full"], 1)

                def weights(b):
                    pe.wait_ge(SEM[f"wload{b % RING}"], 16 * ((SETUP_B + LAYERS * LAYER_B + b) // RING + 1))
                    return wring[:, b % RING]

                o = open_bank("ss1")
                for k in range(KD):
                    after("n_sq", k + 1)
                    mm = nc.tensor.matmul(o, con("mean"), squares_mem[:, k, :], start=(k == 0), stop=(k == KD - 1))
                full(mm)
                o = open_bank("f")
                w_f = glob("w_f").rearrange("p (k h) -> p k h", k=KD)
                for k in range(KD):
                    after("n_out", 8 + k + 1)
                    mm = nc.tensor.matmul(o[0:FOX_H, :], w_f[:, k, :], hT[:, k, :], start=(k == 0), stop=(k == KD - 1))
                full(mm)
                for i, what in enumerate(("qd", "kd", "vd", "qf", "kf", "vf")):
                    for c in range(CW):
                        if c % 2 == 0:
                            wb = weights(2 * i + c // 2)
                        o = open_bank(f"{what}{c}")
                        if what[0] == "v":
                            for ti in range(2):
                                n = 2 * (c % 2) + ti
                                for k in range(KD):
                                    mm = nc.tensor.matmul(o[:, ti * 256:ti * 256 + 256], hT[:, k, n * P:n * P + P],
                                                          wb[:, k, :], start=(k == 0), stop=(k == KD - 1))
                        else:
                            for k in range(KD):
                                mm = nc.tensor.matmul(o, wb[:, k, (c % 2) * P:(c % 2 + 1) * P], hT[:, k, :],
                                                      start=(k == 0), stop=(k == KD - 1))
                        full(mm)
                after("negc_step", 4)
                for h in range(FOX_H):
                    o = open_bank(f"nc{h}")
                    full(nc.tensor.matmul(o, ident[0:FOX_H, h:h + 1].broadcast_to([FOX_H, P]), f_sb, start=True, stop=True))
                after("qkv_ready", 24)

                def scores(i):
                    kind, tb, h = heads[i]
                    q, k = ((qd, kd), (qf, kf))[kind]
                    p0, c, n = 64 * (h % 2), h // 2, (tb + 1) * P
                    o = open_bank(f"s{i}")
                    query, keys = q[p0:p0 + 64, c, tb * P:n], k[p0:p0 + 64, c, :]
                    if kind == 0:
                        mm = nc.tensor.matmul(o[:, 0:n], query, keys[:, 0:n], start=True, stop=True)
                    else:
                        if tb > 0:
                            nc.tensor.matmul(o[:, 0:tb * P], query, keys[:, 0:tb * P], start=True, stop=True)
                        nc.tensor.matmul(o[:, tb * P:n], query, keys[:, tb * P:n], start=True, stop=False)
                        mm = nc.tensor.matmul(o[:, tb * P:n], ident, con("causal"), start=False, stop=True)
                    full(mm)

                def turn(i):
                    kind, tb, h = heads[i]
                    after("s_exp", i + 1)
                    o = open_bank(f"p{i}")
                    for sb_ in range(tb + 1):
                        mm = nc.tensor.transpose(o[:, sb_ * P:sb_ * P + P], s_buf[i % 4][:, sb_ * P:sb_ * P + P], ident)
                    full(mm)

                def values(i):
                    kind, tb, h = heads[i]
                    v = (vd, vf)[kind]
                    after("pt_ready", i + 1)
                    group = 4 * kind + tb
                    if h == 0 and group >= 2:
                        after("o_step", 2 * (group - 1))
                    o = banks[:, 6 + group % 2]
                    for sb_ in range(tb + 1):
                        mm = nc.tensor.matmul(o[:, h * HD:h * HD + HD], p_buf[i % 2][:, sb_ * P:sb_ * P + P],
                                              v[:, sb_, h * HD:h * HD + HD], start=(sb_ == 0), stop=(sb_ == tb))
                    mm.then_inc(SEM["pv_step"], 1)

                for i in range(-2, len(heads) + 1):
                    if i + 2 < len(heads):
                        scores(i + 2)
                    if 0 <= i < len(heads):
                        turn(i)
                    if i >= 1:
                        values(i - 1)
                for c in range(KD):
                    after("o_scaled", 4 * (c // CW) + 4)
                    o = open_bank(f"ot{c}")
                    for n in range(NT):
                        f0 = (c % CW) * P
                        mm = nc.tensor.transpose(o[:, n * P:n * P + P], o_tok[c // CW][:, n, f0:f0 + P], ident)
                    full(mm)
                after("oT_ready", KD)
                for c in range(KD):
                    if c % 2 == 0:
                        wb = weights(12 + c // 2)
                    o = open_bank(f"ao{c}")
                    for k in range(KD):
                        mm = nc.tensor.matmul(o, wb[:, k, (c % 2) * P:(c % 2 + 1) * P], oT[:, k, :],
                                              start=(k == 0), stop=(k == KD - 1))
                    full(mm)
                after("sq_summed", KD - 1)
                full(nc.tensor.matmul(open_bank("ss2"), con("mean"), squares_mem[:, 0, :], start=True, stop=True))
                after("n_out", 24)
                o = open_bank("route")
                w_r = glob("w_route").rearrange("p (k e) -> p k e", k=KD)
                for n in range(NT):
                    for k in range(KD):
                        nc.tensor.matmul(o[:, n * ROUTE:(n + 1) * ROUTE], hT[:, k, n * P:n * P + P], w_r[:, k, :],
                                         start=(k == 0), stop=False)
                    mm = nc.tensor.matmul(o[:, n * ROUTE:(n + 1) * ROUTE], con("ones")[0:1, :], glob("b_route")[0:1, :],
                                          start=False, stop=True)
                full(mm)
                def rows_of(name, z):
                    for n in range(NT):
                        for i in range(2):
                            o = open_bank(f"{name}{n}{i}")
                            for k in range(4):
                                mm = nc.tensor.transpose(o[:, k * P:k * P + P], z[:, 4 * i + k, n * P:n * P + P], ident)
                            full(mm)

                rows_of("hk", hT)
                after("m_ready", 1)
                o = open_bank("rank")
                chosen = rt[:, 8:12].rearrange("p e n g -> p (e n g)").rearrange("p (n e) -> p n e", n=NT)
                for n in range(NT + 1):
                    for m in range(min(n + 1, NT)):
                        lhs = con("gram")[:, 0:P] if m == n else con("ones")
                        mm = nc.tensor.matmul(o[:, n * EXPERTS:(n + 1) * EXPERTS], lhs, chosen[:, m, :],
                                              start=(m == 0), stop=(m == min(n, NT - 1)))
                full(mm)
                rows_of("xk", xT)
                assert at[0] == len(att_jobs)

            @block.scalar
            def _(act):
                def after(name, k):
                    act.wait_ge(SEM[name], k)

                def bank(name):
                    act.wait_ge(SEM["att_full"], JOB[name] + 1)
                    return banks[:, JOB[name] % RB]

                def mean_root(i, name, k0):
                    for k in range(KD):
                        after(name, k0 + k + 1)
                        nc.scalar.activation(squares_mem[:, k, :], xT[:, k, :], ACT.Square).then_inc(SEM["n_sq"], 1)
                    nc.scalar.activation(rstd[:, :], bank(f"ss{i}"), ACT.Sqrt, bias=con("eps")).then_inc(SEM["n_root"], 1)

                mean_root(1, "n_out", 0)
                after("f_step", 2)
                nc.scalar.activation(f_tmp, f_tmp, ACT.Exp).then_inc(SEM["f_act"], 1)
                after("f_act", 1)
                nc.scalar.activation(f_tmp, f_tmp, ACT.Ln, bias=1.0).then_inc(SEM["f_act"], 1)
                for z, what in ((qd, "qd"), (kd, "kd"), (vd, "vd"), (qf, "qf"), (kf, "kf"), (vf, "vf")):
                    for c in range(CW):
                        o = bank(f"{what}{c}")
                        dst = z[:, c, :]
                        if what[0] == "v":
                            o = o.rearrange("p (n f) -> p n f", n=2)
                            dst = z[:, 2 * (c % 2):2 * (c % 2) + 2, (c // 2) * 256:(c // 2) * 256 + 256]
                        nc.scalar.activation(dst, o, ACT.Copy).then_inc(SEM["qkv_ready"], 1)
                for h in range(FOX_H):
                    nc.scalar.activation(neg_c[:, h, :], bank(f"nc{h}"), ACT.Copy).then_inc(SEM["nc_ready"], 1)

                def token_squares(group):
                    after("o_step", 2 * group + 2)
                    if group:
                        after("o_sq", group)
                    nc.scalar.activation(u_sb[:, :], o_tok[group // NT][:, group % NT, :], ACT.Square,
                                         accum_out=hvar[:, group:group + 1]).then_inc(SEM["o_sq"], 1)

                for i, (kind, tb, h) in enumerate(heads):
                    n = (tb + 1) * P
                    after("s_max", i + 1)
                    nc.scalar.activation(s_buf[i % 4][:, 0:n], s_buf[i % 4][:, 0:n], ACT.Exp, bias=n_max[:, i:i + 1],
                                         accum_out=n_sum[:, i:i + 1]).then_inc(SEM["s_exp"], 1)
                    if i >= 1:
                        j = i - 1
                        if j >= 2:
                            after("pv_step", j - 1)
                        m = (heads[j][1] + 1) * P
                        nc.scalar.activation(p_buf[j % 2][:, 0:m], bank(f"p{j}")[:, 0:m], ACT.Copy).then_inc(SEM["pt_ready"], 1)
                    if h == 5 and i > 8:
                        token_squares(i // 8 - 1)
                j = len(heads) - 1
                after("pv_step", j - 1)
                nc.scalar.activation(p_buf[j % 2], bank(f"p{j}"), ACT.Copy).then_inc(SEM["pt_ready"], 1)
                token_squares(2 * NT - 1)
                after("o_step", 17)
                nc.scalar.activation(hvar[:, 0:8], hvar[:, 0:8], ACT.Sqrt).then_inc(SEM["o_root"], 1)
                after("o_step", 18)
                for kind in range(2):
                    for tb in range(NT):
                        j = 4 * kind + tb
                        nc.scalar.activation(o_tok[kind][:, tb, :], o_tok[kind][:, tb, :], ACT.Copy, scale=hvar[:, j:j + 1]) \
                            .then_inc(SEM["o_scaled"], 1)
                for c in range(KD):
                    nc.scalar.activation(oT[:, c, :], bank(f"ot{c}"), ACT.Copy, scale=glob("out_norm", c)).then_inc(SEM["oT_ready"], 1)
                mean_root(2, "x_att", 0)
                for name, rows, done in (("hk", h_rows, "h_tok"), ("xk", x_rows, "x_tok")):
                    for n in range(NT):
                        for i in range(2):
                            nc.scalar.activation(rows[:, n, i * T:i * T + T], bank(f"{name}{n}{i}"), ACT.Copy) \
                                .then_inc(SEM[done], 1)
                    if name == "hk":
                        after("route_step", 5)
                        nc.scalar.activation(rt[:, 0, :, 0:4], rt[:, 0, :, 0:4], ACT.Exp).then_inc(SEM["route_exp"], 1)
                        after("route_step", 30)
                        nc.scalar.activation(rt[:, 4, :, 3:4], rt[:, 4, :, 2:3], ACT.Exp).then_inc(SEM["route_exp"], 1)

            @block.vector
            def _(dve):
                v = nc.vector
                count = {}

                def after(name, k):
                    dve.wait_ge(SEM[name], k)

                def bank(name):
                    dve.wait_ge(SEM["att_full"], JOB[name] + 1)
                    return banks[:, JOB[name] % RB]

                def step(ins, name):
                    ins.then_inc(SEM[name], 1)
                    count[name] = count.get(name, 0) + 1
                    after(name, count[name])

                def scale(out_, gain):
                    for k in range(KD):
                        v.scalar_tensor_tensor(out_[:, k, :], xT[:, k, :], glob(gain, k), rstd[:, :], ALU.mult, ALU.mult) \
                            .then_inc(SEM["n_out"], 1)

                def norm(i, out_, gain):
                    after("n_root", i)
                    step(v.reciprocal(rstd[:, :], rstd[:, :]), "n_mean")
                    scale(out_, gain)

                def add_square(k):
                    after("n_sq", KD + k + 1)
                    step(v.tensor_tensor(squares_mem[:, 0, :], squares_mem[:, 0, :], squares_mem[:, k, :], ALU.add), "sq_summed")

                def gather(group):
                    kind, tb = group // NT, group % NT
                    after("pv_step", DIL_H * (group + 1))
                    after("s_exp", DIL_H * (group + 1))
                    inv = n_sum[:, DIL_H * group:DIL_H * (group + 1)]
                    step(v.reciprocal(inv, inv), "o_step")
                    o = banks[:, 6 + group % 2].rearrange("p (h d) -> p h d", h=DIL_H)
                    step(v.tensor_tensor(o_tok[kind][:, tb, :].rearrange("p (h d) -> p h d", h=DIL_H), o,
                                         inv.unsqueeze(2).broadcast_to([P, DIL_H, HD]), ALU.mult), "o_step")

                scale(xT, "final_g")
                norm(1, hT, "attn_norm")
                step(v.tensor_scalar(f_sb, bank("f")[0:FOX_H, :], glob("b_forget")[0:FOX_H, :], None, ALU.add), "f_step")
                step(v.scalar_tensor_tensor(f_tmp, f_sb, -1.0, f_sb, ALU.mult, ALU.min), "f_step")
                step(v.tensor_scalar(f_sb, f_sb, 0.0, None, ALU.min), "f_step")
                after("f_act", 2)
                step(v.tensor_tensor(f_tmp, f_tmp, f_sb, ALU.subtract), "f_step")
                for n in range(NT):
                    first = 0.0 if n == 0 else f_sb[:, n * P - 1:n * P]
                    step(v.tensor_tensor_scan(f_sb[:, n * P:n * P + P], con("ones")[0:FOX_H, :], f_tmp[:, n * P:n * P + P],
                                              first, ALU.mult, ALU.add), "negc_step")
                after("bias_loaded", 16 * DIL_H)
                for i, (kind, tb, h) in enumerate(heads):
                    n = (tb + 1) * P
                    if kind:
                        after("nc_ready", h + 1)
                        bias = neg_c[:, h, 0:n]
                    else:
                        bias = bias_d[h][:, T - n:T]
                    if i >= 4:
                        after("att_full", JOB[f"p{i - 4}"] + 1)
                    step(v.scalar_tensor_tensor(s_buf[i % 4][:, 0:n], bank(f"s{i}")[:, 0:n], ATT_SCALE, bias,
                                                ALU.mult, ALU.add), "s_shifted")
                    v.tensor_reduce(n_max[:, i:i + 1], s_buf[i % 4][:, 0:n], AX_X, ALU.max, negate=True) \
                        .then_inc(SEM["s_max"], 1)
                    if h == 3 and i > 8:
                        gather(i // 8 - 1)
                gather(2 * NT - 1)
                after("o_sq", 8)
                step(v.tensor_scalar(hvar[:, 0:8], hvar[:, 0:8], 1.0 / (DIL_H * HD), RMS_EPS, ALU.mult, ALU.add), "o_step")
                after("o_root", 1)
                step(v.reciprocal(hvar[:, 0:8], hvar[:, 0:8]), "o_step")
                for c in range(KD):
                    v.tensor_tensor(xT[:, c, :], bank(f"ao{c}"), xT[:, c, :], ALU.add).then_inc(SEM["x_att"], 1)
                    if c >= 2:
                        add_square(c - 1)
                add_square(KD - 1)
                norm(2, hT, "ffn_norm")
                r = lambda ins: step(ins, "route_step")
                r(v.tensor_copy(route[:, :, :], bank("route")[:, 0:NT * ROUTE].rearrange("p (n e) -> p n e", n=NT)))
                groups, experts_ = route[:, :, 0:GROUPS], route[:, :, GROUPS:ROUTE]
                t4 = lambda i: rt[:, i, :, 0:4]
                col = lambda i, j: rt[:, i, :, j:j + 1]
                w4 = lambda a: a.broadcast_to([P, NT, 4])
                w8 = lambda a: a.broadcast_to([P, NT, 8])
                rowb = lambda name, a, b: con(name)[:, a:b].unsqueeze(1).broadcast_to([P, NT, b - a])
                gmax, gsum, gbest = col(2, 0), col(2, 1), col(2, 2)
                r(v.tensor_reduce(gmax, groups, AX_X, ALU.max))
                r(v.tensor_tensor(t4(1), groups, w4(gmax), ALU.is_equal))
                r(v.tensor_tensor(t4(1), t4(1), rowb("rev", 0, 4), ALU.mult))
                r(v.tensor_tensor(t4(0), groups, w4(gmax), ALU.subtract))
                r(v.tensor_reduce(gbest, t4(1), AX_X, ALU.max))
                r(v.tensor_scalar(gbest, gbest, -1.0, 8.0, ALU.mult, ALU.add))
                r(v.tensor_tensor(t4(1), rowb("iota", 0, 4), w4(gbest), ALU.is_equal))
                sel, part = rt[:, 3], rt[:, 5]
                r(v.tensor_tensor(sel, experts_[:, :, 0:8], w8(rt[:, 1, :, 0:1]), ALU.mult))
                for gi in range(1, GROUPS):
                    r(v.tensor_tensor(part, experts_[:, :, 8 * gi:8 * gi + 8], w8(rt[:, 1, :, gi:gi + 1]), ALU.mult))
                    r(v.tensor_tensor(sel, sel, part, ALU.add))
                for k in range(TOP_K):
                    best, val = col(6, k), col(4, k)
                    r(v.tensor_reduce(val, sel, AX_X, ALU.max))
                    r(v.tensor_tensor(part, sel, w8(val), ALU.is_equal))
                    r(v.tensor_tensor(part, part, rowb("rev", 0, 8), ALU.mult))
                    r(v.tensor_reduce(best, part, AX_X, ALU.max))
                    r(v.tensor_scalar(best, best, -1.0, 8.0, ALU.mult, ALU.add))
                    if k == 0:
                        r(v.tensor_tensor(part, rowb("iota", 0, 8), w8(best), ALU.is_equal))
                        r(v.scalar_tensor_tensor(sel, part, -3e38, sel, ALU.mult, ALU.add))
                    r(v.scalar_tensor_tensor(best, gbest, 8.0, best, ALU.mult, ALU.add))
                r(v.tensor_tensor(col(4, 2), col(4, 1), col(4, 0), ALU.subtract))
                after("route_exp", 2)
                r(v.tensor_reduce(gsum, t4(0), AX_X, ALU.add))
                r(v.tensor_scalar(col(4, 4), col(4, 3), 1.0, None, ALU.add))
                r(v.tensor_tensor(gsum, gsum, col(4, 4), ALU.mult))
                r(v.reciprocal(col(7, 0), gsum))
                r(v.tensor_tensor(col(7, 1), col(7, 0), col(4, 3), ALU.mult))
                lay = lambda i: rt[:, i:i + 4].rearrange("p e n g -> p (e n g)").rearrange("p (n e) -> p n e", n=NT)
                chosen, hot, where, prod = lay(8), (lay(12), lay(16)), lay(20), lay(8)
                for k in range(TOP_K):
                    r(v.tensor_tensor(hot[k], rowb("iota", 0, EXPERTS), col(6, k).broadcast_to([P, NT, EXPERTS]), ALU.is_equal))
                v.tensor_tensor(chosen, hot[0], hot[1], ALU.add).then_inc(SEM["m_ready"], 1)
                o = bank("rank")
                extra, incl, jump = (rt[:, i].rearrange("p n g -> p (n g)") for i in (24, 25, 0))
                cnt = o[:, NT * EXPERTS:(NT + 1) * EXPERTS]
                r(v.tensor_scalar(extra, cnt, float(SLOT), None, ALU.is_gt))
                for k in range(2, -(-T // SLOT)):
                    r(v.scalar_tensor_tensor(extra, cnt, float(k * SLOT), extra, ALU.is_gt, ALU.add))
                r(v.tensor_tensor_scan(incl, con("ones")[:, 0:EXPERTS], extra, 0.0, ALU.mult, ALU.add))
                numbers = con("iota")[:, 0:EXPERTS]
                r(v.tensor_tensor(jump, incl, extra, ALU.subtract))
                r(v.scalar_tensor_tensor(jump, jump, EXPERTS - 1.0, numbers, ALU.add, ALU.subtract))
                r(v.tensor_scalar(jump, jump, float(SLOT), None, ALU.mult))
                rank = o[:, 0:NT * EXPERTS].rearrange("p (n e) -> p n e", n=NT)
                r(v.scalar_tensor_tensor(where, rank, float(SLOT), jump.unsqueeze(1).broadcast_to([P, NT, EXPERTS]),
                                         ALU.is_ge, ALU.mult))
                step(v.scalar_tensor_tensor(prod, rowb("iota", 0, EXPERTS), float(SLOT), rank, ALU.mult, ALU.add), "rank_read")
                r(v.tensor_tensor(where, where, prod, ALU.add))
                for k in range(TOP_K):
                    r(v.tensor_tensor(prod, hot[k], where, ALU.mult))
                    r(v.tensor_reduce(col(6, 2 + k), prod, AX_X, ALU.add))
                    v.tensor_copy(slot_idx[:, k, :], rt[:, 6, :, 2 + k]).then_inc(SEM["idx_ready"], 1)
                ends = gm_mem[:, 0:EXTRA * EXPERTS].rearrange("p (i e) -> p i e", e=EXPERTS)
                r(v.tensor_tensor(ends, incl.unsqueeze(1).broadcast_to([P, EXTRA, EXPERTS]),
                                  con("iota")[:, 0:EXTRA].unsqueeze(2).broadcast_to([P, EXTRA, EXPERTS]), ALU.is_le))
                of_tile = w_sb[:, 0:EXTRA + 1]
                r(v.tensor_reduce(of_tile[:, 0:EXTRA], ends, AX_X, ALU.add))
                r(v.tensor_scalar(of_tile[:, 0:EXTRA], of_tile[:, 0:EXTRA], float(EXPERTS - 1), None, ALU.min))
                r(v.tensor_copy(of_tile[:, EXTRA:EXTRA + 1], incl[:, EXPERTS - 1:EXPERTS]))
                v.tensor_copy(tile_exp[:, :], of_tile).then_inc(SEM["idx_ready"], 1)

            @block.gpsimd
            def _(pool):
                nc.gpsimd.memset(zeros, 0.0).then_inc(SEM["zero_set"], 1)
                pool.wait_ge(SEM["zero_set"], 1)
                pool.dma_start(x_slots.rearrange("(i p) d -> p i d", p=SLOT),
                               zeros[0:SLOT].unsqueeze(1).broadcast_to([SLOT, TILES, D])).then_inc(SEM["x_zeroed"], 16)
                pool.dma_start(y_slots[EXPERTS * SLOT:TILES * SLOT].rearrange("(i p) d -> p i d", p=SLOT),
                               zeros[0:SLOT].unsqueeze(1).broadcast_to([SLOT, EXTRA, D])).then_inc(SEM["x_zeroed"], 16)
                for h in range(DIL_H):
                    skew = dil_rows[h:h + 1, P - 1:P - 1 + P * (DIL_ROW - 1)].rearrange("a (p y) -> (a p) y", y=DIL_ROW - 1)
                    pool.dma_start(bias_d[h], skew[:, 0:T]).then_inc(SEM["bias_loaded"], 16)
                pool.wait_ge(SEM["x_zeroed"], 32)
                pool.wait_ge(SEM["h_tok"], 2 * NT)
                for k in range(TOP_K):
                    pool.wait_ge(SEM["idx_ready"], k + 1)
                    for n in range(NT):
                        pool.indirect_dma_start(out=x_slots, out_offset=bass.IndirectOffsetOnAxis(ap=slot_idx[:, k, n:n + 1], axis=0),
                                                in_=h_rows[:, n, :], in_offset=None).then_inc(SEM["scattered"], 16)
                pool.wait_ge(SEM["scattered"], 16 * NT * TOP_K)

        rows = hT[:, :, :].rearrange("p k t -> p (k t)")
        ys_mem = [flat_ztp[:, 0:D], flat_ztp[:, D:2 * D]] + [wring[:, 1, 4 * i:4 * i + 4].rearrange("p k n -> p (k n)") for i in range(2)]
        xs = [rows[0:SLOT, b * D:(b + 1) * D] for b in range(UNROLL)]
        ys = [m[0:SLOT, :] for m in ys_mem]
        XT, HE = KD * SLOT, 2 * SLOT
        xsT = [gm_mem[:, b * XT:(b + 1) * XT] for b in range(UNROLL)]
        sil = [gm_mem[:, UNROLL * XT + b * HE:UNROLL * XT + (b + 1) * HE] for b in range(UNROLL)]
        heT = [flat_ztp[:, 2 * D + b * HE:2 * D + (b + 1) * HE] for b in range(UNROLL)]
        halves = [slice(0, T), slice(T, 2 * T)]

        def turn_rows(b, i, bank):
            for k in range(4):
                mm = nc.tensor.transpose(bank[:, k * SLOT:(k + 1) * SLOT], xs[b][:, (4 * i + k) * P:(4 * i + k + 1) * P],
                                         ident[0:SLOT, 0:SLOT])
            return mm

        def gate_up(b, bank):
            for f in range(4):
                for k in range(KD):
                    mm = nc.tensor.matmul(bank[:, f * SLOT:(f + 1) * SLOT], w_gu[b][:, k, f * P:f * P + P],
                                          xsT[b][:, k * SLOT:(k + 1) * SLOT], start=(k == 0), stop=(k == KD - 1))
            return mm

        def down(b, i, bank):
            for f in range(2):
                mm = nc.tensor.matmul(bank[0:SLOT, :], heT[b][:, f * SLOT:(f + 1) * SLOT], w_dn[b][:, f, halves[i]],
                                      start=(f == 0), stop=(f == 1))
            return mm

        def rounds(engine, body):
            body(0, True, False)
            with engine.Fori(1, ROUNDS - 1) as it:
                body(it, False, False)
            body(ROUNDS - 1, False, True)

        with nc.Block() as block:
            @block.sync
            def _(sp):
                def load_rows(b, tile):
                    sp.dma_start(xs[b], x_slots[bass.ds(tile * SLOT, SLOT)]).then_inc(SEM[f"xs_loaded{b}"], 16)

                def load_gate_up(b, tile):
                    sp.dma_start(gu_mem[b], experts[bass.ds(tile, 1), :, 0:GU].rearrange("a p w -> (a p) w")) \
                      .then_inc(SEM[f"gu_loaded{b}"], 16)

                def load_down(b, tile):
                    sp.dma_start(dn_mem[b], experts[bass.ds(tile, 1), :, GU:GU + DN].rearrange("a p w -> (a p) w")) \
                      .then_inc(SEM[f"dn_loaded{b}"], 16)

                for b in range(UNROLL):
                    load_rows(b, b)
                    if b >= EARLY:
                        load_gate_up(b, b)
                    if b != 2:
                        load_down(b, b)
                with sp.Fori(0, ROUNDS - 1) as it:
                    for b in range(UNROLL):
                        tile = UNROLL * it + b
                        sp.wait_ge(SEM["turned"], 2 * tile + 2)
                        load_rows(b, tile + UNROLL)
                        sp.wait_ge(SEM["gu_done"], tile + 1)
                        load_gate_up(b, tile + UNROLL)
                        sp.wait_ge(SEM["down_done"], 2 * tile + 2)
                        load_down(b, tile + UNROLL)

            @block.tensor
            def _(pe):
                def turn(b, it):
                    pe.wait_ge(SEM[f"xs_loaded{b}"], 16 * it + 16)
                    for i in range(2):
                        turn_rows(b, i, banks[:, i]).then_inc(SEM["turned"], 1)

                def body(it, first, last):
                    for b in range(UNROLL):
                        tile = UNROLL * it + b
                        pe.wait_ge(SEM[f"gu_loaded{b}"], 16 * it + 16)
                        pe.wait_ge(SEM["xs_act"], tile + 1)
                        pe.wait_ge(SEM["xs_dve"], tile + 1)
                        if not (first and b < 2):
                            pe.wait_ge(SEM["he_ready"], tile - 1)
                        gate_up(b, banks[:, 2 + b % 2]).then_inc(SEM["gu_done"], 1)
                        if not (last and b == UNROLL - 1):
                            turn((b + 1) % UNROLL, it + (b + 1) // UNROLL)
                        pe.wait_ge(SEM[f"dn_loaded{b}"], 16 * it + 16)
                        pe.wait_ge(SEM["he_ready"], tile + 1)
                        for i in range(2):
                            if not (first and b < 2):
                                pe.wait_ge(SEM[("y_act", "y_dve")[i]], tile - 1)
                            down(b, i, banks[:, 4 + (2 * b + i) % 4]).then_inc(SEM["down_done"], 1)

                turn(0, 0)
                rounds(pe, body)

            @block.scalar
            def _(act):
                def copy_turned(b, tile, early):
                    act.wait_ge(SEM["turned"], 2 * tile + 1)
                    if not early:
                        act.wait_ge(SEM["gu_done"], tile - (UNROLL - 1))
                    nc.scalar.activation(xsT[b][:, 0:4 * SLOT], banks[:, 0, 0:4 * SLOT], ACT.Copy).then_inc(SEM["xs_act"], 1)

                def body(it, first, last):
                    for b in range(UNROLL):
                        tile = UNROLL * it + b
                        act.wait_ge(SEM["gu_done"], tile + 1)
                        if not first:
                            act.wait_ge(SEM["he_ready"], tile - (UNROLL - 1))
                        nc.scalar.activation(sil[b], banks[:, 2 + b % 2, 0:HE], ACT.Silu).then_inc(SEM["silu_done"], 1)
                        if not (last and b == UNROLL - 1):
                            copy_turned((b + 1) % UNROLL, tile + 1, first and b < UNROLL - 1)
                        act.wait_ge(SEM["down_done"], 2 * tile + 1)
                        if not first:
                            act.wait_ge(SEM[f"ys_stored{b}"], 16 * it)
                        nc.scalar.activation(ys[b][:, halves[0]], banks[0:SLOT, 4 + (2 * b) % 4], ACT.Copy).then_inc(SEM["y_act"], 1)

                copy_turned(0, 0, True)
                rounds(act, body)

            @block.vector
            def _(dve):
                def copy_turned(b, tile, early):
                    dve.wait_ge(SEM["turned"], 2 * tile + 2)
                    if not early:
                        dve.wait_ge(SEM["gu_done"], tile - (UNROLL - 1))
                    nc.vector.tensor_copy(xsT[b][:, 4 * SLOT:8 * SLOT], banks[:, 1, 0:4 * SLOT]).then_inc(SEM["xs_dve"], 1)

                def body(it, first, last):
                    for b in range(UNROLL):
                        tile = UNROLL * it + b
                        dve.wait_ge(SEM["silu_done"], tile + 1)
                        if not first:
                            dve.wait_ge(SEM["down_done"], 2 * tile - 2 * (UNROLL - 1))
                        nc.vector.tensor_tensor(heT[b], banks[:, 2 + b % 2, HE:2 * HE], sil[b], ALU.mult).then_inc(SEM["he_ready"], 1)
                        if not (last and b == UNROLL - 1):
                            copy_turned((b + 1) % UNROLL, tile + 1, first and b < UNROLL - 1)
                        dve.wait_ge(SEM["down_done"], 2 * tile + 2)
                        if not first:
                            dve.wait_ge(SEM[f"ys_stored{b}"], 16 * it)
                        nc.vector.tensor_copy(ys[b][:, halves[1]], banks[0:SLOT, 4 + (2 * b + 1) % 4]).then_inc(SEM["y_dve"], 1)

                copy_turned(0, 0, True)
                rounds(dve, body)

            @block.gpsimd
            def _(pool):
                with pool.Fori(0, ROUNDS) as it:
                    for b in range(UNROLL):
                        tile = UNROLL * it + b
                        pool.wait_ge(SEM["y_act"], tile + 1)
                        pool.wait_ge(SEM["y_dve"], tile + 1)
                        pool.dma_start(y_slots[bass.ds(tile * SLOT, SLOT)], ys[b]).then_inc(SEM[f"ys_stored{b}"], 16)
                for b in range(UNROLL):
                    pool.wait_ge(SEM[f"ys_stored{b}"], 16 * ROUNDS)

        for name in ("e_loaded", "e_turned", "e_xs", "e_gu", "e_silu", "e_he", "e_down", "e_y", "e_stored"):
            sem(name)

        def further(engine, body):
            needed = engine.value_load(tile_exp[0:1, EXTRA:EXTRA + 1], min_val=0, max_val=EXTRA)
            with engine.If(needed > 0):
                body(0, True)
                with engine.Fori(1, EXTRA) as i:
                    with engine.If(needed > i):
                        body(i, False)

        with nc.Block() as block:
            @block.sync
            def _(sp):
                def body(i, first):
                    if not first:
                        sp.wait_ge(SEM["e_stored"], 16 * i)
                    e = sp.value_load(tile_exp[0:1, bass.ds(i, 1)], min_val=0, max_val=EXPERTS - 1)
                    sp.dma_start(xs[0], x_slots[bass.ds((i + EXPERTS) * SLOT, SLOT)]).then_inc(SEM["e_loaded"], 16)
                    sp.dma_start(gu_mem[0], experts[bass.ds(e, 1), :, 0:GU].rearrange("a p w -> (a p) w")).then_inc(SEM["e_loaded"], 16)
                    sp.dma_start(dn_mem[0], experts[bass.ds(e, 1), :, GU:GU + DN].rearrange("a p w -> (a p) w")) \
                      .then_inc(SEM["e_loaded"], 16)
                further(sp, body)

            @block.gpsimd
            def _(pool):
                def body(i, first):
                    pool.wait_ge(SEM["e_y"], i + 1)
                    pool.dma_start(y_slots[bass.ds((i + EXPERTS) * SLOT, SLOT)], ys[0]).then_inc(SEM["e_stored"], 16)
                    pool.wait_ge(SEM["e_stored"], 16 * i + 16)
                further(pool, body)

            @block.tensor
            def _(pe):
                def body(i, first):
                    pe.wait_ge(SEM["e_loaded"], 48 * i + 48)
                    turn_rows(0, 0, banks[:, 0])
                    turn_rows(0, 1, banks[:, 1]).then_inc(SEM["e_turned"], 1)
                    pe.wait_ge(SEM["e_xs"], i + 1)
                    gate_up(0, banks[:, 2]).then_inc(SEM["e_gu"], 1)
                    pe.wait_ge(SEM["e_he"], i + 1)
                    down(0, 0, banks[:, 4])
                    down(0, 1, banks[:, 5]).then_inc(SEM["e_down"], 1)
                further(pe, body)

            @block.scalar
            def _(act):
                def body(i, first):
                    act.wait_ge(SEM["e_turned"], i + 1)
                    nc.scalar.activation(xsT[0].rearrange("p (i w) -> p i w", i=2), banks[:, 0:2, 0:4 * SLOT], ACT.Copy) \
                        .then_inc(SEM["e_xs"], 1)
                    act.wait_ge(SEM["e_gu"], i + 1)
                    nc.scalar.activation(sil[0], banks[:, 2, 0:HE], ACT.Silu).then_inc(SEM["e_silu"], 1)
                    act.wait_ge(SEM["e_down"], i + 1)
                    nc.scalar.activation(ys[0].rearrange("p (i w) -> p i w", i=2), banks[0:SLOT, 4:6], ACT.Copy).then_inc(SEM["e_y"], 1)
                further(act, body)

            @block.vector
            def _(dve):
                def body(i, first):
                    dve.wait_ge(SEM["e_silu"], i + 1)
                    nc.vector.tensor_tensor(heT[0], banks[:, 2, HE:2 * HE], sil[0], ALU.mult).then_inc(SEM["e_he"], 1)
                further(dve, body)

        for name in ["z_added", "z_sq", "z_mean", "z_root", "z_out", "out_stored"] + [f"gathered{n}" for n in range(NT)]:
            sem(name)
        back = [[flat_slots[:, (2 * n + k) * D:(2 * n + k + 1) * D] for k in range(TOP_K)] for n in range(NT)]
        z_var = hvar[:, 0:NT]

        with nc.Block() as block:
            @block.gpsimd
            def _(pool):
                for n in range(NT):
                    for k in range(TOP_K):
                        pool.indirect_dma_start(out=back[n][k], out_offset=None, in_=y_slots,
                                                in_offset=bass.IndirectOffsetOnAxis(ap=slot_idx[:, k, n:n + 1], axis=0)) \
                            .then_inc(SEM[f"gathered{n}"], 16)

            @block.vector
            def _(dve):
                v = nc.vector
                for n in range(NT):
                    dve.wait_ge(SEM[f"gathered{n}"], 16 * TOP_K)
                    for k in range(TOP_K):
                        v.scalar_tensor_tensor(x_rows[:, n, :], back[n][k], rt[:, 7, n, k:k + 1], x_rows[:, n, :], ALU.mult, ALU.add) \
                            .then_inc(SEM["z_added"], 1)
                        dve.wait_ge(SEM["z_added"], TOP_K * n + k + 1)
                dve.wait_ge(SEM["z_sq"], NT)
                v.tensor_scalar(z_var, z_var, 1.0 / D, RMS_EPS, ALU.mult, ALU.add).then_inc(SEM["z_mean"], 1)
                dve.wait_ge(SEM["z_root"], 1)
                v.reciprocal(z_var, z_var).then_inc(SEM["z_mean"], 1)
                dve.wait_ge(SEM["z_mean"], 2)
                for n in range(NT):
                    v.scalar_tensor_tensor(x_rows[:, n, :], x_rows[:, n, :], z_var[:, n:n + 1], fnorm, ALU.mult, ALU.mult) \
                        .then_inc(SEM["z_out"], 1)

            @block.scalar
            def _(act):
                for n in range(NT):
                    act.wait_ge(SEM["z_added"], TOP_K * (n + 1))
                    nc.scalar.activation(back[n][0], x_rows[:, n, :], ACT.Square, accum_out=z_var[:, n:n + 1]).then_inc(SEM["z_sq"], 1)
                act.wait_ge(SEM["z_mean"], 1)
                nc.scalar.activation(z_var, z_var, ACT.Sqrt).then_inc(SEM["z_root"], 1)

            @block.sync
            def _(sp):
                for n in range(NT):
                    sp.wait_ge(SEM["z_out"], n + 1)
                    sp.dma_start(out[n * P:(n + 1) * P], x_rows[:, n, :]).then_inc(SEM["out_stored"], 16)
                sp.wait_ge(SEM["out_stored"], 16 * NT)
        for name, n in given.items():
            assert n == PER[name] or name.startswith("wload"), (name, n, PER[name])


def pack(i):
    f = lambda n: np.asarray(i[n])
    col = lambda a: a.reshape(-1, P).T
    kcols = lambda a: a.reshape(a.shape[0] // P, P, a.shape[1]).transpose(1, 0, 2)

    def blocks(a):
        return [kcols(a[:, j:j + 256]).reshape(P, BLK) for j in range(0, a.shape[1], 256)]

    stream, lpar = [], []
    for l in range(LAYERS):
        stream += blocks(f("w_ada")[l])
    for l in range(LAYERS):
        w_in = f("w_in")[l]
        o = dict(pu=0, pg=512, q=1024, k=1536, v=2048, tg=2560, r=3072, wl=3584, rk=3648, rv=4160, al=4672, rg=4736,
                 gates=5248)
        for name in ("r", "rk", "rv", "pu", "pg", "q", "k", "v", "rg", "tg"):
            stream += blocks(w_in[:, o[name]:o[name] + 512])
        wb = f("w_branch")[l]
        for cp in range(KD // 2):
            for n in range(3):
                a = o["gates"] + n * D + cp * 256
                stream += blocks(w_in[:, a:a + 256])
            for c in (2 * cp, 2 * cp + 1):
                part = wb[:, :, c * P:c * P + P].reshape(3 * CW, P, P).transpose(1, 0, 2).reshape(P, 12 * P)
                stream.append(np.concatenate([part, np.zeros((P, BLK - 12 * P), np.float32)], 1))
        stream += blocks(f("w_out")[l])
        mu = f("rwkv_shift_mu")[l]
        mu13 = np.concatenate([col(mu[0:512]), col(np.concatenate([mu[512:576], mu[1600:1664]])), col(mu[576:1088]),
                               col(mu[1088:1600])], 1)
        lora = np.concatenate([f("rwkv_w2")[l], f("rwkv_a2")[l]], 0)
        w_lora = np.concatenate([w_in[:, o["wl"]:o["wl"] + 64], w_in[:, o["al"]:o["al"] + 64]], 1)
        vecs = [col(f("pool_scale")[l]), col(f("ret_norm_g")[l]), mu13]
        vecs += [col(f("rwkv_" + n)[l].reshape(-1)) for n in ("w0", "a0", "k_k", "k_a", "r_k", "ln_w", "ln_b")]
        vecs += [f("pool_w")[l].transpose(1, 0, 2).reshape(P, 512), lora, kcols(w_lora).reshape(P, KD * P)]
        lpar.append(np.concatenate(vecs, 1))
    w2 = f("w_in_2")[0]
    stream += blocks(w2[:, 0:3072]) + blocks(f("w_out_2")[0])
    norms = np.concatenate([f("out_norm_dil_2")[0], f("out_norm_fox_2")[0]])
    zeros = lambda shape: np.zeros(shape, np.float32)
    tall = lambda a: np.concatenate([a, zeros((P - a.shape[0], a.shape[1]))], 0)
    w_route = np.concatenate([f("w_router_group_2")[0], f("w_router_expert_2")[0]], 1)
    b_route = np.concatenate([f("b_router_group_2")[0], f("b_router_expert_2")[0]])[None, :]
    rel = np.concatenate([f("rel_bias_2"), np.ones((1, DIL_H), np.float32)], 0)
    gpar = [col(f("c")[0])] + [col(f("norm_g")[l]) for l in range(LAYERS)] + [col(f("b_ada")[l]) for l in range(LAYERS)]
    gpar += [col(f("final_g")), col(f("attn_norm_2")[0]), col(norms), col(f("ffn_norm_2")[0]),
            kcols(w2[:, 3072:3080]).reshape(P, KD * FOX_H), kcols(w_route).reshape(P, KD * ROUTE), tall(b_route),
            tall(f("b_forget_2")[0][:, None]), tall(rel)]
    wide = lambda a: a.reshape(EXPERTS, -1, P, a.shape[-1]).transpose(0, 2, 1, 3)
    gate_up = np.concatenate([wide(f("w_expert_gate_2")[0]), wide(f("w_expert_up_2")[0])], 3)
    experts = np.concatenate([gate_up.reshape(EXPERTS, P, -1), wide(f("w_expert_down_2")[0]).reshape(EXPERTS, P, -1)], 2)
    return {
        "wstream": np.stack(stream), "lparams": np.stack(lpar), "gparams": np.concatenate(gpar, 1),
        "consts": constants(), "distances": distance_table(), "experts": experts,
        "last_norm": np.broadcast_to(f("final_norm_2")[None, :], (P, D)),
        "x_in": np.ascontiguousarray(f("x")[0].T.reshape(KD, P, T).transpose(1, 0, 2).reshape(P, KD * T)),
        "pos_in": np.ascontiguousarray(f("positions")[0].reshape(NT, P).T.astype(np.int32)),
    }


def kernel(**inputs):
    import concourse.bacc as bacc
    from concourse.bass_utils import run_bass_kernel_spmd

    nc = bacc.Bacc("TRN2", target_bir_lowering=False, num_devices=1)
    arrays = {k: np.ascontiguousarray(a) for k, a in pack(inputs).items()}
    args = {k: nc.dram_tensor(k, a.shape, mybir.dt.from_np(a.dtype), kind="ExternalInput").ap() for k, a in arrays.items()}
    out = nc.dram_tensor("out", (T, D), F32, kind="ExternalOutput").ap()
    program(nc, out=out, **args)
    r = run_bass_kernel_spmd(nc, [arrays], core_ids=[0])
    got = r.results[0]["out"]
    return got.reshape(1, T, D)
```

```python
import math
from contextlib import ExitStack

import numpy as np

import concourse.bass as bass
from concourse import mybir

F32 = mybir.dt.float32
FR = mybir.dt.float32r
I32 = mybir.dt.int32
ALU = mybir.AluOpType
ACT = mybir.ActivationFunctionType
AX_X = mybir.AxisListType.X

P = 128
T = 512
NT = T // P
D = 1024
KD = D // P
W = 512
CW = W // P
LAYERS = 2
RET_H, RET_D = 4, 128
RW_H, RW_D = 8, 64
WINDOWS = (2, 4, 8, 16)
RMS_EPS = 1e-6
RET_EPS = 1e-5
RW_EPS = 64e-5
DECAY = -math.exp(-0.5)
OFF = -DECAY * P / 2
LEVELS = tuple(2 ** i for i in range(1, 7))
FOX_H = DIL_H = 8
HD = 64
ATT_SCALE = HD ** -0.5
NEG = -1e30
DIL_ROW = T + P
BUCKETS, MAX_DISTANCE = 32, 2048
DILATIONS, SEG = (1, 4, 16), 128

GROUPS, PER_GROUP, TOP_K, FF = 4, 8, 2, 256
EXPERTS = GROUPS * PER_GROUP
ROUTE = GROUPS + EXPERTS
SLOT = 80
EXTRA = (T * TOP_K - TOP_K) // SLOT
TILES = EXPERTS + EXTRA
UNROLL = 4

CHUNK = KD * P
RING = 3
FIRST, LAYER_B = {}, 0
for _n, _w in [("r", CW), ("wl", 1), ("k", CW), ("lora", 1), ("v", CW), ("pu", CW), ("pg", CW), ("pool_w", 1),
               ("retq", CW), ("retk", CW), ("retv", CW), ("rg", CW), ("tg", CW), ("merge", KD // 2 * 9), ("wo", KD)]:
    FIRST[_n] = LAYER_B
    LAYER_B += _w
WHOLE = (FIRST["lora"], FIRST["pool_w"])
assert LAYER_B % RING == 0
ATT_B = 6 * CW + KD
ADA_BLK = KD * 2 * P
ADA_B = 3 * D // 256
SETUP_B = LAYERS * ADA_B

_names = [("pool_scale", 4), ("ret_norm_g", 4), ("mu", 13), ("w0", 4), ("a0", 4),
          ("k_k", 4), ("k_a", 4), ("r_k", 4), ("ln_w", 4), ("ln_b", 4)]
PCOL, NPAR = {}, 0
for _n, _w in _names:
    PCOL[_n] = (NPAR, NPAR + _w)
    NPAR += _w

_names = [("c", 8), ("norm_g", LAYERS * 8), ("b_ada", LAYERS * 24), ("final_g", 8), ("attn_norm", 8), ("out_norm", 8), ("ffn_norm", 8), ("w_f", KD * 8), ("w_route", KD * 36), ("b_route", 1),
          ("b_forget", 1), ("rel", 8)]
GCOL, NGLOB = {}, 0
for _n, _w in _names:
    GCOL[_n] = (NGLOB, NGLOB + _w)
    NGLOB += _w

_names = [("ident", P), ("blk64", P), ("mean", P), ("ones", P), ("gram", W), ("lvl", 6 * P), ("lvl1", 2 * P),
          ("ret_mask", W), ("ret_q", W), ("ret_k", 4), ("freq", 64), ("inv_count", 64), ("off", 2), ("causal", P),
          ("iota", 64), ("rev", 8), ("eps", 1)]
CCOL, NCONST = {}, 0
for _n, _w in _names:
    CCOL[_n] = (NCONST, NCONST + _w)
    NCONST += _w


def constants():
    i = np.arange(P)
    row, col = i[:, None], i[None, :]
    out = np.zeros((P, NCONST), np.float32)

    def put(name, a):
        out[:, CCOL[name][0]:CCOL[name][1]] = a

    put("ident", np.eye(P))
    put("blk64", row // RW_D == col // RW_D)
    put("mean", np.full((P, P), 1.0 / D))
    put("ones", np.ones((P, P)))
    strict, incl = row < col, row <= col
    put("gram", np.concatenate([strict, incl, strict, incl], 1))
    put("lvl", np.concatenate([((row // b) % 2 == 1) & (col // b == row // b - 1) for b in LEVELS], 1))
    pair = (row % 2 == 0) & (col == row + 1)
    put("lvl1", np.concatenate([pair, pair.T], 1))
    log_gamma = np.log1p(-(2.0 ** (-5.0 - np.arange(RET_H))))
    scale = RET_D ** -0.5
    put("ret_mask", np.concatenate([np.where(incl, np.exp(g * np.maximum(col - row, 0)), 0) * scale
                                    for g in log_gamma], 1))
    put("ret_q", np.concatenate([np.exp(g * (col + 1.0)) + 0 * row for g in log_gamma], 1))
    put("ret_k", np.stack([np.exp(g * (P - 1 - i)) * scale for g in log_gamma], 1))
    put("freq", (np.float32(10000.0) ** (-np.arange(64, dtype=np.float32) / np.float32(64)))[None, :])
    t = np.arange(16)
    put("inv_count", np.concatenate([1.0 / np.minimum(t + 1, w) for w in WINDOWS])[None, :])
    put("off", np.array([OFF, -OFF])[None, :])
    put("causal", np.where(col <= row, 0.0, NEG))
    put("iota", np.arange(64)[None, :])
    put("rev", 8.0 - np.arange(8)[None, :])
    put("eps", RMS_EPS)
    return out


def distance_table():
    dist = T - 1 - np.arange(DIL_ROW)
    d = np.maximum(dist, 0)
    exact = BUCKETS // 2
    log = np.log(np.maximum(d, 1).astype(np.float32) / np.float32(exact)) / np.float32(math.log(MAX_DISTANCE / exact))
    large = np.minimum(exact + (log * np.float32(BUCKETS - exact)).astype(np.int32), BUCKETS - 1)
    bucket = np.where(d < exact, d, large)
    count = sum(((dist >= 0) & (dist % r == 0) & (dist // r <= SEG)).astype(np.int32) for r in DILATIONS)
    out = np.zeros((BUCKETS + 1, DIL_ROW), np.float32)
    out[bucket, np.arange(DIL_ROW)] = dist >= 0
    out[BUCKETS] = np.where(count > 0, np.log(np.maximum(count, 1)), NEG)
    return out


def program(nc, ada, wstream, lparams, gparams, consts, distances, experts, last_norm, x_in, pos_in, out):
    with ExitStack() as ctx:
        one_pass = {}

        def sb(name, shape, dt=F32, split=False):
            tensor = ctx.enter_context(nc.sbuf_tensor(name, shape, dt))
            if split:
                one_pass[name] = nc.alloc_sbuf_tensor_at(name + "_r", shape, FR, offset=nc.sbuf_base - 4 * math.prod(shape[1:]))
            return tensor

        def r(a):
            return bass.AP(tensor=one_pass[a.tensor.name], offset=a.offset, ap=a.ap)

        SEM, PER, given = {}, {}, {}

        layer_ctx = ExitStack()

        def sem(name, per=1, owner=ctx):
            SEM[name] = owner.enter_context(nc.semaphore(name))
            PER[name] = per

        def inc(ins, name, by=1):
            given[name] = given.get(name, 0) + by
            ins.then_inc(SEM[name], by)

        wmem = sb("wmem", [P, 2 * RING, CHUNK], split=True)
        xT = sb("xT", [P, KD, T])
        hT = sb("hT", [P, KD, T], split=True)
        h_hi = sb("h_hi", [P, KD, T], split=True)
        lpar = sb("lpar", [P, NPAR])
        gpar = sb("gpar", [P, NGLOB])
        cst = sb("cst", [P, NCONST])
        slots = sb("slots", [P, 9, CW, T], split=True)
        br_pool = sb("br_pool", [P, CW, T], split=True)
        gm_mem = sb("gm_mem", [P, 4096], split=True)
        ztp = sb("ztp", [P, 3, 8, P], split=True)
        w_sb = sb("w_sb", [P, T])
        u_sb = sb("u_sb", [P, T])
        state = sb("state", [P, CW, P], split=True)
        rstd = sb("rstd", [P, T])
        mods = sb("mods", [P, LAYERS, 32])
        mod = sb("mod", [P, 32])
        omm = sb("omm", [P, 13 + CW])
        e_end = sb("e_end", [P, CW, NT])
        c_act = sb("c_act", [P, KD])
        posi = sb("posi", [P, NT], I32)
        posf = sb("posf", [P, NT])
        cosT = sb("cosT", [P, NT, 64])
        sinT = sb("sinT", [P, NT, 64])
        hsum = sb("hsum", [P, 32])
        hvar = sb("hvar", [P, 32])
        slot_idx = sb("slot_idx", [P, TOP_K, NT], I32)
        tile_exp = sb("tile_exp", [P, EXTRA + 1], I32)
        dram = lambda name, shape: nc.dram_tensor(name, shape, F32).ap()
        dil_rows = dram("dil_rows", (DIL_H, P * DIL_ROW))
        x_slots = dram("x_slots", (TILES * SLOT, D))
        y_slots = dram("y_slots", (TILES * SLOT, D))
        banks = ctx.enter_context(nc.psum_tensor("banks", [P, 8, T], F32))

        def par(name, c=None):
            a, b = PCOL[name]
            return lpar[:, a:b] if c is None else lpar[:, a + c:a + c + 1]

        def glob(name, c=None):
            a, b = GCOL[name]
            return gpar[:, a:b] if c is None else gpar[:, a + c:a + c + 1]

        def con(name, c=None):
            a, b = CCOL[name]
            return cst[:, a:b] if c is None else cst[:, a + c:a + c + 1]

        ident = con("ident")
        SL = [slots[:, i] for i in range(9)]
        R_, K_, X1, X2, X3, G_, V_, A_, KK = SL
        gm = gm_mem[:, :].rearrange("p (u k t) -> p u k t", u=8, k=4)
        zt, tt, pt = ztp[:, 0], ztp[:, 1], ztp[:, 2]
        b_tok, v_tok, k_tok, y_tok = (s.rearrange("p n f -> p n f") for s in (X1, G_, V_, X2))
        pool_u = gm_mem[:, 0:2048].rearrange("p (c t) -> p c t", c=CW)
        pool_gate = gm_mem[:, 2048:4096].rearrange("p (c t) -> p c t", c=CW)
        br_rwkv = X3
        rq_raw, rk_raw, rv_tok, ret_gate = X1, V_, KK, K_
        flat_ztp = ztp[:, :, :, :].rearrange("p a u t -> p (a u t)")
        rq_rot = flat_ztp[:, 0:2048].rearrange("p (n f) -> p n f", n=NT)
        rk_rot, qT, qdT = G_, R_, K_
        kT = gm_mem[:, 0:2048].rearrange("p (h t) -> p h t", h=RET_H)
        rot_tmp = [gm_mem[:, 2048 + 1024 * i:3072 + 1024 * i] for i in range(2)]
        k_tail, o_tok, br_ret, o_sq = X1, V_, X2, G_
        p_ret = [w_sb[:, :], u_sb[:, :]]
        sig_gate = slots[:, 6:9].rearrange("p s c t -> p (s c) t")
        mT = gm_mem[:, :].rearrange("p (c t) -> p c t", c=KD)
        m_hi = [K_[:, c, :] for c in range(CW)] + [flat_ztp[:, c * T:c * T + T] for c in range(CW)]
        branches, branches_hi = (br_pool, br_ret, br_rwkv), (R_, G_, X1)

        def products(w, x):
            return ((w[0], x[0]), (w[0], x[1]), (w[1], x[0]))

        jobs = []

        def job(name, drained, k):
            jobs.append((name, drained, k))

        for c in range(CW):
            job(f"r{c}", "mixed", 1 + c)
        job("wl", "mixed", 5)
        for c in range(CW):
            job(f"k{c}", "mixed", 6 + c)
        for c in range(CW):
            job(f"z{c}", "g_ready", 1 + c)
        for c in range(CW):
            job(f"a{c}", "a_ready", 1 + c)
        for c in range(CW):
            job(f"v{c}", "mixed", 10 + c)
        for c in range(CW):
            job(f"kss{c}", "kss_ready", 1 + c)
        for c in range(CW):
            job(f"pu{c}", "pu_ready", 1 + c)
        for c in range(CW):
            job(f"pg{c}", "pg_ready", 1 + c)
        for c in range(CW):
            job(f"bs{c}", "bonus_ready", 1 + c)
        for i, what in enumerate("vbk"):
            for n in range(NT):
                job(f"t{what}{n}", "tok_ready", 1 + NT * i + n)
        for c in range(CW):
            job(f"py{c}", "pool_done", 1 + c)
        for n in range(NT):
            for h in range(RW_H):
                job(f"gram{n}{h}", "gram_ready", 1 + 8 * n + h)
            for g in range(2):
                job(f"ti{n}{g}", "tinit_ready", 1 + 2 * n + g)
            for l in range(6):
                for g in range(2):
                    job(f"p{n}{l}{g}", "p_ready", 1 + 12 * n + 2 * l + g)
                for g in range(2):
                    if l < 5:
                        job(f"tn{n}{l}{g}", "t_ready", 1 + 10 * n + 2 * l + g)
                    job(f"zn{n}{l}{g}", "z_ready", 3 + 14 * n + 2 * l + g)
            job(f"w{n}", "w_ready", 1 + n)
            job(f"u{n}", "u_ready", 1 + n)
            job(f"y{n}", "y_ready", 1 + n)
            if n < NT - 1:
                job(f"s{n}", "s_added", 1 + n)
        for i, what in enumerate("qkv"):
            for b in range(2):
                for tp in range(2):
                    job(f"ret{what}{b}{tp}", "ret_tok", 1 + 4 * i + 2 * b + tp)
        for h in range(RET_H):
            job(f"tq{h}", "qd_ready", 1 + h)
        for h in range(RET_H):
            job(f"tkr{h}", "kT_ready", 1 + h)
        for c in range(CW):
            job(f"rg{c}", "rg_ready", 1 + c)
        job("sc0", "pret_ready", 1)
        for n in range(NT):
            if n < NT - 1:
                job(f"sc{n + 1}", "pret_ready", 2 + n)
            job(f"o{n}", "o_ready", 1 + n)
            if n < NT - 1:
                job(f"kv{n}", "R_ready", 1 + n)
        for c in range(CW):
            job(f"tg{c}", "retg_ready", 1 + c)
        for c in range(CW):
            job(f"ty{c}", "y_scaled", 1 + c)
        for h in range(RET_H):
            job(f"to{h}", "ret_done", 1 + h)
        for cp in range(KD // 2):
            for n in range(3):
                for cc in range(2):
                    job(f"g{cp}{n}{cc}", "gate_sig", 1 + 6 * cp + 2 * n + cc)
            for cc in range(2):
                for n in range(3):
                    job(f"b{cp}{cc}{n}", "merged", 1 + 5 * (2 * cp + cc) + (0, 1, 3)[n])
        for c in range(KD):
            job(f"wo{c}", "x_done", 1 + c)
        job("ss", "rms_sqrt", 1)
        NJ = len(jobs)
        JOB = {name: j for j, (name, _, _) in enumerate(jobs)}
        full_of = lambda name: ("bank_full", JOB[name] + 1)
        chunk_used = [full_of(f"r{c}") for c in range(CW)] + [full_of("wl")]
        chunk_used += [full_of(f"k{c}") for c in range(CW)] + [full_of("a3")]
        chunk_used += [full_of(f"{w}{c}") for w in ("v", "pu", "pg") for c in range(CW)] + [full_of("py3")]
        for i, w in enumerate("qkv"):
            for b in range(2):
                chunk_used += [("half_used", 2 * i + b + 1), full_of(f"ret{w}{b}1")]
        chunk_used += [full_of(f"{w}{c}") for w in ("rg", "tg") for c in range(CW)]
        for cp in range(KD // 2):
            chunk_used += [full_of(f"g{cp}{n}{cc}") for n in range(3) for cc in range(2)]
            chunk_used += [full_of(f"b{cp}{i // 3}{i % 3}") for i in (1, 3, 5)]
        chunk_used += [full_of(f"wo{c}") for c in range(KD)]
        assert len(chunk_used) == LAYER_B
        split_count = lambda b: b + 1 - sum(w <= b for w in WHOLE)

        for s in range(RING):
            sem(f"wload{s}", 16 * LAYER_B // RING)
            sem(f"ada_loaded{s}")
        for name in ("x_loaded", "const_loaded", "glob_loaded", "pos_loaded", "dist_loaded", "dr_full", "dr_drained", "dr_stored",
                     "ada_step", "ada_prod", "ada_pool", "ada_summed", "mods_step", "first_sq", "first_sum", "first_root"):
            sem(name)
        sem("c_ready")
        sem("rope_step")
        sem("rope_arg")
        sem("rope_ready")
        LAYER_SEMS = []
        for name, per in (("bank_full", NJ), ("params_loaded", 16), ("x_done", 8), ("mod_ready", 1), ("omm_ready", 2), ("xsq_ready", 8), ("xsq_summed", 7),
                          ("rms_ready", 1), ("rms_sqrt", 1),
                          ("h_scaled", 8), ("h_ready", 8), ("mix_scaled", 13), ("mixed", 13), ("wl_tanh", 1),
                          ("g_ready", 4), ("a_ready", 4), ("kk_ready", 2), ("kss_ready", 4), ("kss_sqrt", 1),
                          ("k_mod", 2), ("rk_ready", 1), ("kk_unit", 2), ("bonus_ready", 4),
                          ("pu_ready", 4), ("pg_ready", 4), ("pool_step", 10 * 2 + 4 * 4), ("pool_d", 4),
                          ("pool_done", 4), ("g_sum", 1), ("g_prev", 1), ("exp_prev", 1), ("exp_plus", 1),
                          ("exp_minus", 1), ("ar_ready", 2), ("bk_ready", 2), ("tok_ready", 12),
                          ("gram_ready", 32), ("z_masked", 8), ("tinit_ready", 8), ("p_ready", 48),
                          ("t_ready", 40), ("z_ready", 56), ("w_ready", 4), ("u_ready", 4), ("y_ready", 4),
                          ("s_added", 3), ("s_ready", 3), ("y_norm", 7), ("y_sqrt", 1), ("y_scaled", 4),
                          ("rwkv_done", 4), ("rg_ready", 4), ("ret_tok", 12), ("retg_ready", 4),
                          ("rot_step", 6), ("rot_ready", 2), ("qT_ready", 4), ("qd_ready", 4), ("kT_ready", 4),
                          ("ktail_ready", 1), ("pret_ready", 4), ("o_ready", 4), ("R_ready", 3), ("o_norm", 7),
                          ("o_sqrt", 1), ("ret_done", 4), ("gate_sig", 24), ("merged", 40),
                          ("w_high", LAYER_B - len(WHOLE)), ("w_split", LAYER_B - len(WHOLE)), ("half_used", 6), ("h_high", 8),
                          ("br_high", 3), ("br_split", 3), ("m_high", 8), ("m_split", 8)):
            sem(name, per, layer_ctx)
            LAYER_SEMS.append(name)

        def landed(engine, b, base=0):
            engine.wait_ge(SEM[f"wload{b % RING}"], base + 16 * (b // RING + 1))
            return wmem[:, b % RING]

        def chunk(b):
            return wmem[:, RING + b % RING], wmem[:, b % RING]

        HALF_ROW = DIL_ROW // 2
        DIST_FROM, MEAN_FROM = 4, 6
        ANGLES_FROM = 4
        ada_ring = [wmem[:, 2 * i:2 * i + 2].rearrange("p s n -> p (s n)") for i in range(RING)]
        dil_mem = slots[:, 0:3].rearrange("p s c t -> p (s c t)")
        dil_sb = [dil_mem[:, h * DIL_ROW:(h + 1) * DIL_ROW] for h in range(DIL_H)]
        dist_sb = gm_mem[0:BUCKETS + 1, 0:DIL_ROW]
        WEIGHED = 5
        ada_acc = [flat_ztp[:, i * 256:(i + 1) * 256] for i in range(3)]
        ada_prod = [[flat_ztp[:, (3 + 3 * i + j) * 256:(4 + 3 * i + j) * 256] for j in range(KD - WEIGHED)] for i in range(3)]

        with nc.Block() as block:
            @block.sync
            def _(sp):
                def load_ada(b):
                    sp.dma_start(ada_ring[b % RING], ada[b]).then_inc(SEM[f"ada_loaded{b % RING}"], 16)

                sp.dma_start(gpar[:, :], gparams).then_inc(SEM["glob_loaded"], 16)
                load_ada(0)
                sp.dma_start(cst[:, :], consts).then_inc(SEM["const_loaded"], 16)
                for b in range(1, RING):
                    load_ada(b)
                sp.dma_start(posi[:, :], pos_in).then_inc(SEM["pos_loaded"], 16)
                sp.dma_start(dist_sb, distances).then_inc(SEM["dist_loaded"], 16)
                sp.dma_start(xT[:, :, :].rearrange("p k t -> p (k t)"), x_in).then_inc(SEM["x_loaded"], 16)
                for b in range(RING, SETUP_B):
                    sp.wait_ge(SEM["ada_step"], (WEIGHED + 1) * (b - RING + 1))
                    load_ada(b)
                for b in range(RING):
                    used = SETUP_B - RING + b // 2 + 1
                    sp.wait_ge(SEM["ada_step"], (WEIGHED + 1) * used)
                    inc(sp.dma_start(wmem[:, b], wstream[b]), f"wload{b}", 16)

            @block.tensor
            def _(pe):
                def distance_row(j):
                    if j == 0:
                        pe.wait_ge(SEM["dist_loaded"], 16)
                    if j >= 4:
                        pe.wait_ge(SEM["dr_drained"], j - 3)
                    a = GCOL["rel"][0] + j // 2
                    nc.tensor.matmul(banks[:, 4 + j % 4, 0:HALF_ROW], gpar[0:BUCKETS + 1, a:a + 1].broadcast_to([BUCKETS + 1, P]),
                                     dist_sb[:, j % 2 * HALF_ROW:(j % 2 + 1) * HALF_ROW], start=True, stop=True) \
                        .then_inc(SEM["dr_full"], 1)

                pe.wait_ge(SEM["const_loaded"], 16)
                for b in range(SETUP_B):
                    pe.wait_ge(SEM["ada_step"], (WEIGHED + 1) * (b + 1))
                    for m in range(2):
                        mm = nc.tensor.matmul(banks[:, 0, 2 * b + m:2 * b + m + 1], ada_acc[b % 3][:, m * P:m * P + P],
                                              con("ones")[:, 0:1], start=True, stop=True)
                    mm.then_inc(SEM["ada_summed"], 1)
                    if DIST_FROM <= b < DIST_FROM + 2 * DIL_H:
                        distance_row(b - DIST_FROM)
                    if b % 2 == 0 and MEAN_FROM <= b < MEAN_FROM + 2 * KD:
                        k = (b - MEAN_FROM) // 2
                        pe.wait_ge(SEM["first_sq"], k + 1)
                        mm = nc.tensor.matmul(banks[:, 1], con("mean"), hT[:, k, :], start=(k == 0), stop=(k == KD - 1))
                        if k == KD - 1:
                            mm.then_inc(SEM["first_sum"], 1)

            @block.scalar
            def _(act):
                act.wait_ge(SEM["glob_loaded"], 16)
                nc.scalar.activation(c_act[:, :], glob("c"), ACT.Silu).then_inc(SEM["c_ready"], 1)
                act.wait_ge(SEM["const_loaded"], 16)
                act.wait_ge(SEM["c_ready"], 1)
                for b in range(SETUP_B):
                    act.wait_ge(SEM[f"ada_loaded{b % RING}"], 16 * (b // RING + 1))
                    if b >= 3:
                        act.wait_ge(SEM["ada_step"], (WEIGHED + 1) * (b - 2))
                    for k in range(WEIGHED, KD):
                        ins = nc.scalar.activation(ada_prod[b % 3][k - WEIGHED], ada_ring[b % RING][:, k * 256:(k + 1) * 256],
                                                   ACT.Copy, scale=c_act[:, k:k + 1])
                    ins.then_inc(SEM["ada_prod"], 1)
                    if MEAN_FROM <= b < MEAN_FROM + KD:
                        k = b - MEAN_FROM
                        act.wait_ge(SEM["x_loaded"], 16)
                        nc.scalar.activation(hT[:, k, :], xT[:, k, :], ACT.Square).then_inc(SEM["first_sq"], 1)
                    j = b - DIST_FROM - 1
                    if 0 <= j < 2 * DIL_H:
                        act.wait_ge(SEM["dr_full"], j + 1)
                        nc.scalar.activation(dil_sb[j // 2][:, j % 2 * HALF_ROW:(j % 2 + 1) * HALF_ROW],
                                             banks[:, 4 + j % 4, 0:HALF_ROW], ACT.Copy).then_inc(SEM["dr_drained"], 1)
                        if j % 2 == 1:
                            act.wait_ge(SEM["dr_drained"], j + 1)
                            act.dma_start(dil_rows[j // 2].rearrange("(p y) -> p y", y=DIL_ROW), dil_sb[j // 2]) \
                               .then_inc(SEM["dr_stored"], 16)
                    if b == MEAN_FROM + KD:
                        act.wait_ge(SEM["rope_arg"], 1)
                        nc.scalar.activation(sinT[:, :, :], sinT[:, :, :], ACT.Sin)
                        nc.scalar.activation(cosT[:, :, :], cosT[:, :, :], ACT.Sin).then_inc(SEM["rope_ready"], 1)
                    if b == SETUP_B - 3:
                        act.wait_ge(SEM["first_sum"], 1)
                        nc.scalar.activation(rstd[:, :], banks[:, 1], ACT.Sqrt, bias=con("eps")).then_inc(SEM["first_root"], 1)
                act.wait_ge(SEM["dr_stored"], 16 * DIL_H)

            @block.vector
            def _(dve):
                v = nc.vector
                def rotary_angles():
                    dve.wait_ge(SEM["const_loaded"], 16)
                    dve.wait_ge(SEM["pos_loaded"], 16)
                    n_rope = [0]
                    def rope(ins):
                        n_rope[0] += 1
                        ins.then_inc(SEM["rope_step"], 1)
                        dve.wait_ge(SEM["rope_step"], n_rope[0])
                    ang, turns = cosT[:, :, :], sinT[:, :, :]
                    rope(v.tensor_copy(posf[:, :], posi[:, :]))
                    for n in range(NT):
                        last = v.tensor_scalar(cosT[:, n, :], con("freq"), posf[:, n:n + 1], None, ALU.mult)
                    rope(last)
                    MAGIC = 1.5 * 2.0 ** 23
                    rope(v.tensor_scalar(turns, ang, 1.0 / (2 * math.pi), None, ALU.mult))
                    rope(v.tensor_scalar(turns, turns, MAGIC, None, ALU.add))
                    rope(v.tensor_scalar(turns, turns, MAGIC, None, ALU.subtract))
                    c1 = 6.28125
                    c2 = math.floor((2 * math.pi - c1) * 2 ** 20) / 2 ** 20
                    for part in (c1, c2, 2 * math.pi - c1 - c2):
                        rope(v.scalar_tensor_tensor(ang, turns, -part, ang, ALU.mult, ALU.add))
                    rope(v.tensor_scalar(turns, ang, math.pi - 1e-6, -(math.pi - 1e-6), ALU.min, ALU.max))
                    rope(v.scalar_tensor_tensor(ang, turns, -1.0, turns, ALU.mult, ALU.max))
                    v.tensor_scalar(ang, ang, -1.0, math.pi / 2, ALU.mult, ALU.add).then_inc(SEM["rope_arg"], 1)

                dve.wait_ge(SEM["c_ready"], 1)
                for b in range(SETUP_B):
                    if b == ANGLES_FROM:
                        rotary_angles()
                    if b == SETUP_B - 2:
                        dve.wait_ge(SEM["first_root"], 1)
                        v.reciprocal(rstd[:, :], rstd[:, :])
                    dve.wait_ge(SEM[f"ada_loaded{b % RING}"], 16 * (b // RING + 1))
                    if b >= 3:
                        dve.wait_ge(SEM["ada_summed"], b - 2)
                    acc, others = ada_acc[b % 3], ada_prod[b % 3][0]
                    for k in range(WEIGHED):
                        w_k, c_k = ada_ring[b % RING][:, k * 256:(k + 1) * 256], c_act[:, k:k + 1]
                        if k == 0:
                            ins = v.tensor_scalar(acc, w_k, c_k, None, ALU.mult)
                        else:
                            dve.wait_ge(SEM["ada_step"], (WEIGHED + 1) * b + k)
                            ins = v.scalar_tensor_tensor(acc, w_k, c_k, acc, ALU.mult, ALU.add)
                        ins.then_inc(SEM["ada_step"], 1)
                    dve.wait_ge(SEM["ada_step"], (WEIGHED + 1) * b + WEIGHED)
                    dve.wait_ge(SEM["ada_pool"], 2 * b + 2)
                    v.tensor_tensor(acc, acc, others, ALU.add).then_inc(SEM["ada_step"], 1)
                dve.wait_ge(SEM["ada_summed"], SETUP_B)
                parts = banks[:, 0, 0:LAYERS * 24].rearrange("p (l m) -> p l m", l=LAYERS)
                v.tensor_tensor(mods[:, :, 0:24], parts, glob("b_ada").rearrange("p (l m) -> p l m", l=LAYERS), ALU.add) \
                    .then_inc(SEM["mods_step"], 1)
                dve.wait_ge(SEM["mods_step"], 1)
                v.scalar_tensor_tensor(mods[:, :, 24:32], mods[:, :, 8:16], 1.0, glob("norm_g").rearrange("p (l m) -> p l m", l=LAYERS),
                                       ALU.add, ALU.mult)

            @block.gpsimd
            def _(pool):
                for b in range(SETUP_B):
                    first, second, third = ada_prod[b % 3]
                    pool.wait_ge(SEM["ada_prod"], b + 1)
                    nc.gpsimd.tensor_tensor(first, first, second, ALU.add).then_inc(SEM["ada_pool"], 1)
                    pool.wait_ge(SEM["ada_pool"], 2 * b + 1)
                    nc.gpsimd.tensor_tensor(first, first, third, ALU.add).then_inc(SEM["ada_pool"], 1)

        with nc.Fori(0, LAYERS) as L:
          with nc.Block() as block:
            @block.sync
            def _(sp):
                for b in range(LAYER_B):
                    name, count = chunk_used[b]
                    sp.wait_ge(SEM[name], count)
                    inc(sp.dma_start(wmem[:, b % RING], wstream[bass.ds(L * LAYER_B + (b + RING), 1)].rearrange("a p n -> (a p) n")),
                        f"wload{b % RING}", 16)

            @block.tensor
            def _(pe):
                state_ = {"job": 0}

                def after(name, k=None):
                    pe.wait_ge(SEM[name], PER[name] if k is None else k)

                def open_bank(name):
                    j = state_["job"]
                    assert jobs[j][0] == name, (name, jobs[j])
                    if j >= 8:
                        after(*jobs[j - 8][1:])
                    state_["job"] = j + 1
                    return banks[:, j % 8]

                def full(mm):
                    inc(mm, "bank_full")

                def weights(b):
                    after("w_split", split_count(b))
                    return [w.rearrange("p (k n) -> p k n", k=KD) for w in chunk(b)]

                def whole(b):
                    return landed(pe, b, L * PER[f"wload{b % RING}"])

                def feature_job(name, b):
                    w, o = weights(b), open_bank(name)
                    for k in range(KD):
                        for i, (lhs, rhs) in enumerate(products(w, (h_hi, hT))):
                            mm = nc.tensor.matmul(o, r(lhs[:, k, :]), r(rhs[:, k, :]),
                                                  start=(k == 0 and i == 0), stop=(k == KD - 1 and i == 2))
                    full(mm)

                def project(prefix):
                    for c in range(CW):
                        feature_job(f"{prefix}{c}", FIRST[prefix] + c)

                def project_tok(prefix):
                    for b in range(2):
                        o = [open_bank(f"{prefix}{b}{tp}") for tp in range(2)]
                        for half in range(2):
                            at = FIRST[prefix] + 2 * b + half
                            after("w_split", split_count(at))
                            w = [part.rearrange("p (k n) -> p k n", k=KD // 2) for part in chunk(at)]
                            for n in range(NT):
                                cols = slice(n % 2 * 256, n % 2 * 256 + 256)
                                for k in range(KD // 2):
                                    for i, (lhs, rhs) in enumerate(products((h_hi, hT), w)):
                                        mm = nc.tensor.matmul(o[n // 2][:, cols], r(lhs[:, KD // 2 * half + k, n * P:n * P + P]),
                                                              r(rhs[:, k, :]), start=(half == 0 and n % 2 == 0 and k == 0 and i == 0),
                                                              stop=(half == 1 and k == KD // 2 - 1 and i == 2), skip_group_check=True)
                                if half == 1 and n % 2 == 1:
                                    full(mm)
                            if half == 0:
                                inc(mm, "half_used")

                def transposes(name, tiles):
                    o = open_bank(name)
                    for i, s in enumerate(tiles):
                        mm = nc.tensor.transpose(o[:, i * P:i * P + P], s, ident)
                    full(mm)

                o = [open_bank("r0"), open_bank("r1")]
                for c in range(2):
                    w = weights(FIRST["r"] + c)
                    for k in range(KD):
                        if c == 0:
                            after("h_high", k + 1)
                        for i in range(2):
                            nc.tensor.matmul(o[c], r(w[i][:, k, :]), r(h_hi[:, k, :]), start=(k == 0 and i == 0), stop=False)
                for c in range(2):
                    w_hi = weights(FIRST["r"] + c)[0]
                    for k in range(KD):
                        if c == 0:
                            after("h_ready", k + 1)
                        mm = nc.tensor.matmul(o[c], r(w_hi[:, k, :]), r(hT[:, k, :]), start=False, stop=(k == KD - 1))
                    full(mm)
                for c in range(2, CW):
                    feature_job(f"r{c}", FIRST["r"] + c)
                feature_job("wl", FIRST["wl"])
                project("k")
                lora = whole(FIRST["lora"])
                after("wl_tanh")
                for name, p0 in (("z", 0), ("a", 64)):
                    for c in range(CW):
                        o = open_bank(f"{name}{c}")
                        full(nc.tensor.matmul(o, lora[p0:p0 + 64, c * P:c * P + P], w_sb[p0:p0 + 64, :],
                                              start=True, stop=True))
                project("v")
                after("kk_ready")
                for c in range(CW):
                    o = open_bank(f"kss{c}")
                    full(nc.tensor.matmul(o, con("blk64"), X1[:, c, :], start=True, stop=True))
                project("pu")
                project("pg")
                after("rk_ready")
                for c in range(CW):
                    o = open_bank(f"bs{c}")
                    full(nc.tensor.matmul(o, con("blk64"), X3[:, c, :], start=True, stop=True))
                after("mixed")
                for n in range(NT):
                    transposes(f"tv{n}", [V_[:, c, n * P:n * P + P] for c in range(CW)])
                after("bk_ready", 1)
                for n in range(NT):
                    transposes(f"tb{n}", [A_[:, c, n * P:n * P + P] for c in range(CW)])
                after("bk_ready", 2)
                for n in range(NT):
                    transposes(f"tk{n}", [K_[:, c, n * P:n * P + P] for c in range(CW)])
                pool_w = whole(FIRST["pool_w"])
                for c in range(CW):
                    after("pool_d", c + 1)
                    o = open_bank(f"py{c}")
                    full(nc.tensor.matmul(o, pool_w[:, c * P:c * P + P], pool_u[:, c, :], start=True, stop=True))
                after("ar_ready")
                for n in range(NT):
                    t0 = n * P
                    for h in range(RW_H):
                        o = open_bank(f"gram{n}{h}")
                        p0, c = 64 * (h % 2), h // 2
                        for i, (lhs, rhs) in enumerate(((A_, KK), (A_, R_), (K_, KK), (K_, R_))):
                            mm = nc.tensor.matmul(o[:, i * P:i * P + P], lhs[p0:p0 + 64, c, t0:t0 + P],
                                                  rhs[p0:p0 + 64, c, t0:t0 + P], start=True, stop=True)
                        full(mm)
                    for g in range(2):
                        after("z_ready", 14 * n + 1 + g)
                        transposes(f"ti{n}{g}", [zt[:, u, :] for u in range(4 * g, 4 * g + 4)])
                    for l in range(6):
                        for g in range(2):
                            if l == 0:
                                after("tinit_ready", 2 * n + 1 + g)
                            else:
                                after("t_ready", 10 * n + 2 * (l - 1) + 1 + g)
                            o = open_bank(f"p{n}{l}{g}")
                            for i in range(4):
                                u = 4 * g + i
                                mm = nc.tensor.matmul(o[:, i * P:i * P + P], gm[:, u, 0, :], tt[:, u, :],
                                                      start=True, stop=True)
                            full(mm)
                        for g in range(2):
                            after("p_ready", 12 * n + 2 * l + 1 + g)
                            if l > 0:
                                after("z_ready", 14 * n + 2 * l + 1 + g)
                            if l < 5:
                                o = open_bank(f"tn{n}{l}{g}")
                                for i in range(4):
                                    u = 4 * g + i
                                    mm = nc.tensor.matmul(o[:, i * P:i * P + P], zt[:, u, :], pt[:, u, :],
                                                          start=True, stop=True)
                                full(mm)
                            o = open_bank(f"zn{n}{l}{g}")
                            for i in range(4):
                                u = 4 * g + i
                                mm = nc.tensor.matmul(o[:, i * P:i * P + P], pt[:, u, :], zt[:, u, :],
                                                      start=True, stop=True)
                            full(mm)
                    if n == 0:
                        after("tok_ready")
                    else:
                        after("s_ready", n)
                    o = open_bank(f"w{n}")
                    if n > 0:
                        for c in range(CW):
                            nc.tensor.matmul(o[:, c * P:c * P + P], KK[:, c, t0:t0 + P], state[:, c, :],
                                             start=(c == 0), stop=False, skip_group_check=True)
                    for h in range(RW_H):
                        mm = nc.tensor.matmul(o[:, h * 64:h * 64 + 64], gm[:, h, 2, :], v_tok[:, n, h * 64:h * 64 + 64],
                                              start=(n == 0 and h == 0), stop=(h == RW_H - 1), skip_group_check=True)
                    full(mm)
                    o_u, o_y = open_bank(f"u{n}"), open_bank(f"y{n}")
                    if n > 0:
                        for c in range(CW):
                            nc.tensor.matmul(o_y[:, c * P:c * P + P], R_[:, c, t0:t0 + P], state[:, c, :],
                                             start=(c == 0), stop=False, skip_group_check=True)
                    for h in range(RW_H):
                        cols = slice(h * 64, h * 64 + 64)
                        nc.tensor.matmul(o_y[:, cols], gm[:, h, 3, :], v_tok[:, n, cols],
                                         start=(n == 0 and h == 0), stop=False, skip_group_check=True)
                    after("w_ready", n + 1)
                    after("z_ready", 14 * n + 14)
                    for h in range(RW_H):
                        mm = nc.tensor.matmul(o_u[:, h * 64:h * 64 + 64], zt[:, h, :], w_sb[:, h * 64:h * 64 + 64],
                                              start=True, stop=True)
                    full(mm)
                    if n < NT - 1:
                        o_s = open_bank(f"s{n}")
                        for c in range(CW):
                            cols = slice(c * P, c * P + P)
                            nc.tensor.matmul(o_s[:, cols], k_tok[:, n, cols], v_tok[:, n, cols],
                                             start=(c == 0), stop=False, skip_group_check=True)
                    after("u_ready", n + 1)
                    for h in range(RW_H):
                        cols = slice(h * 64, h * 64 + 64)
                        mm = nc.tensor.matmul(o_y[:, cols], gm[:, h, 1, :], u_sb[:, cols],
                                              start=False, stop=(h == RW_H - 1), skip_group_check=True)
                    full(mm)
                    if n < NT - 1:
                        for c in range(CW):
                            cols = slice(c * P, c * P + P)
                            mm = nc.tensor.matmul(o_s[:, cols], b_tok[:, n, cols], u_sb[:, cols],
                                                  start=False, stop=(c == CW - 1), skip_group_check=True)
                        full(mm)
                for what in "qkv":
                    project_tok(f"ret{what}")
                after("rot_ready", 1)
                for h in range(RET_H):
                    transposes(f"tq{h}", [rq_rot[:, n, h * P:h * P + P] for n in range(NT)])
                after("rot_ready", 2)
                for h in range(RET_H):
                    transposes(f"tkr{h}", [rk_rot[:, n, h * P:h * P + P] for n in range(NT)])
                project("rg")
                after("qd_ready")
                after("kT_ready")
                after("ktail_ready")

                def retention_scores(n):
                    o, t0 = open_bank(f"sc{n}"), n * P
                    for h in range(RET_H):
                        mm = nc.tensor.matmul(o[:, h * P:h * P + P], kT[:, h, t0:t0 + P], qT[:, h, t0:t0 + P],
                                              start=True, stop=True)
                    full(mm)

                retention_scores(0)
                for n in range(NT):
                    t0 = n * P
                    if n < NT - 1:
                        retention_scores(n + 1)
                    after("pret_ready", n + 1)
                    if n > 0:
                        after("R_ready", n)
                    o = open_bank(f"o{n}")
                    for h in range(RET_H):
                        cols = slice(h * P, h * P + P)
                        mm = nc.tensor.matmul(o[:, cols], p_ret[n % 2][:, cols], rv_tok[:, n, cols],
                                              start=True, stop=(n == 0))
                        if n > 0:
                            mm = nc.tensor.matmul(o[:, cols], qdT[:, h, t0:t0 + P], state[:, h, :],
                                                  start=False, stop=True)
                    full(mm)
                    if n < NT - 1:
                        o = open_bank(f"kv{n}")
                        for h in range(RET_H):
                            cols = slice(h * P, h * P + P)
                            mm = nc.tensor.matmul(o[:, cols], k_tail[:, n, cols], rv_tok[:, n, cols],
                                                  start=True, stop=True)
                        full(mm)
                project("tg")
                after("y_norm")
                for c in range(CW):
                    transposes(f"ty{c}", [y_tok[:, n, c * P:c * P + P] for n in range(NT)])
                after("o_norm")
                for h in range(RET_H):
                    transposes(f"to{h}", [o_tok[:, n, h * P:h * P + P] for n in range(NT)])
                for cp in range(KD // 2):
                    first = FIRST["merge"] + 9 * cp
                    for n in range(3):
                        for cc in range(2):
                            feature_job(f"g{cp}{n}{cc}", first + 2 * n + cc)
                    for i in range(6):
                        cc, n = i // 3, i % 3
                        w, o = weights(first + 6 + i // 2), open_bank(f"b{cp}{cc}{n}")
                        if cp == 0:
                            after("br_split", n + 1)
                        for k in range(CW):
                            for j, (lhs, rhs) in enumerate(products(w, (branches_hi[n], branches[n]))):
                                mm = nc.tensor.matmul(o, r(lhs[:, i % 2 * CW + k, :]), r(rhs[:, k, :]),
                                                      start=(k == 0 and j == 0), stop=(k == CW - 1 and j == 2))
                        full(mm)
                for c in range(KD):
                    w, o = weights(FIRST["wo"] + c), open_bank(f"wo{c}")
                    for k in range(KD):
                        if c == 0:
                            after("m_split", k + 1)
                        for i, (lhs, rhs) in enumerate(((w[0], m_hi[k]), (w[0], mT[:, k, :]), (w[1], m_hi[k]))):
                            mm = nc.tensor.matmul(o, r(lhs[:, k, :]), r(rhs), start=(k == 0 and i == 0),
                                                  stop=(k == KD - 1 and i == 2))
                    full(mm)
                o = open_bank("ss")
                after("xsq_summed")
                full(nc.tensor.matmul(o, con("mean"), hT[:, 0, :], start=True, stop=True))
                assert state_["job"] == NJ

            @block.scalar
            def _(act):
                def after(name, k=None):
                    act.wait_ge(SEM[name], PER[name] if k is None else k)

                def bank(name):
                    act.wait_ge(SEM["bank_full"], JOB[name] + 1)
                    return banks[:, JOB[name] % 8]

                inc(nc.scalar.activation(mod[:, :], mods[:, bass.ds(L, 1), :].rearrange("p a m -> p (a m)"), ACT.Copy), "mod_ready")
                act.dma_start(lpar[:, :], lparams[bass.ds(L, 1)].rearrange("a p n -> (a p) n")) \
                   .then_inc(SEM["params_loaded"], 16)
                after("mod_ready")

                def high(b):
                    if b in WHOLE or b >= LAYER_B:
                        return
                    w = landed(act, b, L * PER[f"wload{b % RING}"])
                    inc(nc.scalar.activation(r(chunk(b)[0]), w, ACT.Copy), "w_high")

                high(0)
                high(1)
                for k in range(KD):
                    after("h_scaled", k + 1)
                    inc(nc.scalar.activation(r(h_hi[:, k, :]), hT[:, k, :], ACT.Identity, bias=mod[:, k:k + 1]), "h_high")
                high(2)
                after("omm_ready")
                after("params_loaded")
                for c in range(CW):
                    inc(nc.scalar.activation(R_[:, c, :], bank(f"r{c}"), ACT.Copy, scale=omm[:, c:c + 1]), "mix_scaled")
                    high(FIRST["r"] + c + RING)
                inc(nc.scalar.activation(w_sb[:, :], bank("wl"), ACT.Copy, scale=omm[:, 4:5]), "mix_scaled")
                high(FIRST["wl"] + RING)
                after("mixed", 5)
                inc(nc.scalar.activation(w_sb[0:64, :], w_sb[0:64, :], ACT.Tanh), "wl_tanh")
                for i, (z, name) in enumerate(((K_, "k"), (V_, "v"))):
                    for c in range(CW):
                        m = 5 + 4 * i + c
                        inc(nc.scalar.activation(z[:, c, :], bank(f"{name}{c}"), ACT.Copy, scale=omm[:, m:m + 1]),
                            "mix_scaled")
                        high(FIRST[name] + c + RING)
                    if name == "k":
                        for c in range(CW):
                            inc(nc.scalar.activation(G_[:, c, :], bank(f"z{c}"), ACT.Sigmoid, bias=par("w0", c)), "g_ready")
                        for c in range(CW):
                            inc(nc.scalar.activation(A_[:, c, :], bank(f"a{c}"), ACT.Sigmoid, bias=par("a0", c)), "a_ready")
                        high(FIRST["lora"] + RING)
                after("kss_ready")
                inc(nc.scalar.activation(X2[:, :, :], X2[:, :, :], ACT.Sqrt), "kss_sqrt")
                for c in range(CW):
                    inc(nc.scalar.activation(pool_u[:, c, :], bank(f"pu{c}"), ACT.Copy), "pu_ready")
                    high(FIRST["pu"] + c + RING)
                for c in range(CW):
                    inc(nc.scalar.activation(pool_gate[:, c, :], bank(f"pg{c}"), ACT.Silu), "pg_ready")
                    high(FIRST["pg"] + c + RING)
                    if c == 1:
                        after("g_sum")
                        nc.scalar.activation(e_end[:, :, :], X2[:, :, P - 1:T:P], ACT.Exp, scale=DECAY)
                        inc(nc.scalar.activation(X1[:, :, :], X2[:, :, :], ACT.Exp, scale=DECAY, bias=con("off", 0)), "exp_plus")
                        after("g_prev")
                        inc(nc.scalar.activation(G_[:, :, :], G_[:, :, :], ACT.Exp, scale=DECAY, bias=con("off", 0)), "exp_prev")
                        after("exp_plus")
                        inc(nc.scalar.activation(X2[:, :, :], X2[:, :, :], ACT.Exp, scale=-DECAY, bias=con("off", 1)), "exp_minus")
                after("ar_ready")
                for n in range(NT):
                    inc(nc.scalar.activation(v_tok[:, n, :], bank(f"tv{n}"), ACT.Copy), "tok_ready")
                for n in range(NT):
                    inc(nc.scalar.activation(b_tok[:, n, :], bank(f"tb{n}"), ACT.Copy), "tok_ready")
                after("bonus_ready")
                for n in range(NT):
                    inc(nc.scalar.activation(k_tok[:, n, :], bank(f"tk{n}"), ACT.Copy), "tok_ready")
                for n in range(NT):
                    for g in range(2):
                        inc(nc.scalar.activation(tt[:, 4 * g:4 * g + 4, :].rearrange("p u t -> p (u t)"),
                                                 bank(f"ti{n}{g}"), ACT.Copy), "tinit_ready")
                    inc(nc.scalar.activation(w_sb[:, :], bank(f"w{n}"), ACT.Copy), "w_ready")
                    if n == 0:
                        after("bk_ready")
                    inc(nc.scalar.activation(y_tok[:, n, :], bank(f"y{n}"), ACT.Copy), "y_ready")
                    if n == 0:
                        high(FIRST["pool_w"] + RING)
                for z, what in ((rq_raw, "q"), (rk_raw, "k"), (rv_tok, "v")):
                    for b in range(2):
                        at = FIRST[f"ret{what}"] + 2 * b
                        high(at + RING)
                        for tp in range(2):
                            o = bank(f"ret{what}{b}{tp}").rearrange("p (n f) -> p n f", n=2)
                            inc(nc.scalar.activation(z[:, 2 * tp:2 * tp + 2, b * 256:b * 256 + 256], o, ACT.Copy), "ret_tok")
                        high(at + 1 + RING)
                        if what == "q" and b == 0:
                            after("y_norm", 5)
                            inc(nc.scalar.activation(hvar[:, :], hvar[:, :], ACT.Sqrt), "y_sqrt")
                for h in range(RET_H):
                    inc(nc.scalar.activation(qT[:, h, :], bank(f"tq{h}"), ACT.Copy), "qT_ready")
                for h in range(RET_H):
                    inc(nc.scalar.activation(kT[:, h, :], bank(f"tkr{h}"), ACT.Copy), "kT_ready")
                for c in range(CW):
                    inc(nc.scalar.activation(A_[:, c, :], bank(f"rg{c}"), ACT.Silu), "rg_ready")
                    high(FIRST["rg"] + c + RING)
                for n in range(NT):
                    inc(nc.scalar.activation(o_tok[:, n, :], bank(f"o{n}"), ACT.Copy), "o_ready")
                for c in range(CW):
                    inc(nc.scalar.activation(ret_gate[:, c, :], bank(f"tg{c}"), ACT.Silu), "retg_ready")
                    high(FIRST["tg"] + c + RING)
                    if c == 0:
                        after("o_norm", 5)
                        inc(nc.scalar.activation(hvar[:, 0:16], hvar[:, 0:16], ACT.Sqrt), "o_sqrt")
                def merged_high(c):
                    after("merged", 5 * c + 5)
                    inc(nc.scalar.activation(r(m_hi[c]), mT[:, c, :], ACT.Copy), "m_high")

                for cp in range(KD // 2):
                    first = FIRST["merge"] + 9 * cp
                    for n in range(3):
                        for cc in range(2):
                            if cp >= 2:
                                after("merged", 5 * (2 * cp - 4 + cc) + (1, 2, 4)[n])
                            elif cp == 0 and n == 0 and cc == 0:
                                after("ret_done")
                            i = 6 * (cp % 2) + 2 * n + cc
                            inc(nc.scalar.activation(sig_gate[:, i, :], bank(f"g{cp}{n}{cc}"), ACT.Sigmoid), "gate_sig")
                            high(first + 2 * n + cc + RING)
                        if cp == 0 and n == 0:
                            for m, done in enumerate(("pool_done", "ret_done", "rwkv_done")):
                                after(done)
                                inc(nc.scalar.activation(r(branches_hi[m]), branches[m][:, :, :], ACT.Copy), "br_high")
                    if cp > 0:
                        for c in (2 * cp - 2, 2 * cp - 1):
                            merged_high(c)
                    for i in range(3):
                        if i == 2 and cp == KD // 2 - 1:
                            merged_high(KD - 2)
                            merged_high(KD - 1)
                        high(first + 6 + i + RING)
                for k in range(KD):
                    after("x_done", k + 1)
                    inc(nc.scalar.activation(hT[:, k, :], xT[:, k, :], ACT.Square), "xsq_ready")
                    high(FIRST["wo"] + k + RING)
                inc(nc.scalar.activation(rstd[:, :], bank("ss"), ACT.Sqrt, bias=con("eps")), "rms_sqrt")

            @block.vector
            def _(dve):
                v = nc.vector

                def after(name, k=None):
                    dve.wait_ge(SEM[name], PER[name] if k is None else k)

                def bank(name):
                    dve.wait_ge(SEM["bank_full"], JOB[name] + 1)
                    return banks[:, JOB[name] % 8]

                done = {}

                def step(ins, name):
                    inc(ins, name)
                    done[name] = done.get(name, 0) + 1
                    after(name, done[name])

                after("mod_ready")
                for k in range(KD):
                    inc(v.scalar_tensor_tensor(hT[:, k, :], xT[:, k, :], mod[:, 24 + k:25 + k], rstd[:, :], ALU.mult, ALU.mult),
                        "h_scaled")
                for k in range(KD):
                    after("h_high", k + 1)
                    inc(v.scalar_tensor_tensor(r(hT[:, k, :]), hT[:, k, :], mod[:, k:k + 1], r(h_hi[:, k, :]), ALU.add, ALU.subtract),
                        "h_ready")
                after("params_loaded")
                mu = par("mu")
                inc(v.tensor_scalar(omm[:, 0:13], mu, -1.0, 1.0, ALU.mult, ALU.add), "omm_ready")
                inc(v.tensor_scalar(omm[:, 13:17], par("k_a"), -1.0, 1.0, ALU.mult, ALU.add), "omm_ready")

                def mix(z, m, name):
                    o = bank(name)
                    after("mix_scaled", m + 1)
                    inc(v.scalar_tensor_tensor(z[:, 1:T], o[:, 0:T - 1], mu[:, m:m + 1], z[:, 1:T], ALU.mult, ALU.add),
                        "mixed")

                for c in range(CW):
                    mix(R_[:, c, :], c, f"r{c}")
                mix(w_sb[:, :], 4, "wl")
                for c in range(CW):
                    mix(K_[:, c, :], 5 + c, f"k{c}")
                after("mixed", 9)
                for c in range(CW):
                    last = v.tensor_scalar(KK[:, c, :], K_[:, c, :], par("k_k", c), None, ALU.mult)
                inc(last, "kk_ready")
                after("kk_ready", 1)
                inc(v.tensor_tensor(X1[:, :, :], KK[:, :, :], KK[:, :, :], ALU.mult), "kk_ready")
                for c in range(CW):
                    mix(V_[:, c, :], 9 + c, f"v{c}")
                for c in range(CW):
                    inc(v.tensor_scalar(X2[:, c, :], bank(f"kss{c}"), 1e-24, None, ALU.max), "kss_ready")
                after("a_ready")
                for c in range(CW):
                    last = v.tensor_scalar(X3[:, c, :], A_[:, c, :], par("k_a", c), omm[:, 13 + c:14 + c], ALU.mult, ALU.add)
                step(last, "k_mod")
                step(v.tensor_tensor(K_[:, :, :], K_[:, :, :], X3[:, :, :], ALU.mult), "k_mod")
                for c in range(CW):
                    last = v.scalar_tensor_tensor(X3[:, c, :], R_[:, c, :], par("r_k", c), K_[:, c, :], ALU.mult, ALU.mult)
                inc(last, "rk_ready")
                after("kss_sqrt")
                step(v.reciprocal(X2[:, :, :], X2[:, :, :]), "kk_unit")
                step(v.tensor_tensor(KK[:, :, :], KK[:, :, :], X2[:, :, :], ALU.mult), "kk_unit")
                v.tensor_tensor(A_[:, :, :], A_[:, :, :], KK[:, :, :], ALU.mult)
                after("g_ready")
                for c in range(CW):
                    for n in range(NT):
                        t0 = n * P
                        last = v.tensor_tensor_scan(X2[:, c, t0:t0 + P], con("ones"), G_[:, c, t0:t0 + P], 0.0,
                                                    ALU.mult, ALU.add)
                step(last, "g_sum")
                inc(v.tensor_tensor(G_[:, :, :], X2[:, :, :], G_[:, :, :], ALU.subtract), "g_prev")
                after("exp_plus")
                inc(v.tensor_tensor(R_[:, :, :], R_[:, :, :], X1[:, :, :], ALU.mult), "ar_ready")
                after("exp_prev")
                inc(v.scalar_tensor_tensor(KK[:, :, :], KK[:, :, :], -1.0, G_[:, :, :], ALU.mult, ALU.mult), "ar_ready")
                after("exp_minus")
                inc(v.tensor_tensor(A_[:, :, :], A_[:, :, :], X2[:, :, :], ALU.mult), "bk_ready")
                inc(v.tensor_tensor(K_[:, :, :], K_[:, :, :], X2[:, :, :], ALU.mult), "bk_ready")
                after("mixed")
                for c in range(CW):
                    inc(v.tensor_tensor(X3[:, c, :], bank(f"bs{c}"), V_[:, c, :], ALU.mult), "bonus_ready")
                for c in range(CW):
                    o = bank(f"py{c}")
                    after("pg_ready", c + 1)
                    inc(v.scalar_tensor_tensor(br_pool[:, c, :], o, par("pool_scale", c), pool_gate[:, c, :],
                                               ALU.mult, ALU.mult), "pool_done")

                flat = lambda a, g: a[:, 4 * g:4 * g + 4, :]
                lvl1 = con("lvl1")
                for n in range(NT):
                    for g in range(2):
                        for h in range(4 * g, 4 * g + 4):
                            inc(v.tensor_tensor(gm[:, h].rearrange("p k t -> p (k t)"), bank(f"gram{n}{h}"), con("gram"), ALU.mult),
                                "gram_ready")
                        after("gram_ready", 8 * n + 4 * g + 4)
                        step(v.tensor_tensor(flat(zt, g), gm[:, 4 * g:4 * g + 4, 0, :],
                                             lvl1[:, 0:P].unsqueeze(1).broadcast_to([P, 4, P]), ALU.mult), "z_masked")
                        inc(v.tensor_tensor(flat(zt, g), flat(zt, g), ident.unsqueeze(1).broadcast_to([P, 4, P]), ALU.add),
                            "z_ready")
                    for l in range(6):
                        mask = con("lvl")[:, l * P:l * P + P].unsqueeze(1).broadcast_to([P, 4, P])
                        for g in range(2):
                            o = bank(f"p{n}{l}{g}").rearrange("p (u t) -> p u t", u=4)
                            inc(v.tensor_tensor(flat(pt, g), o, mask, ALU.mult), "p_ready")
                        for g in range(2):
                            if l < 5:
                                o = bank(f"tn{n}{l}{g}").rearrange("p (u t) -> p u t", u=4)
                                if l == 0:
                                    after("tinit_ready", 2 * n + 1 + g)
                                else:
                                    after("t_ready", 10 * n + 2 * (l - 1) + 1 + g)
                                inc(v.tensor_tensor(flat(tt, g), o, flat(tt, g), ALU.add), "t_ready")
                            o = bank(f"zn{n}{l}{g}").rearrange("p (u t) -> p u t", u=4)
                            after("z_ready", 14 * n + 2 * l + 1 + g)
                            inc(v.tensor_tensor(flat(zt, g), o, flat(zt, g), ALU.add), "z_ready")
                    inc(v.tensor_copy(u_sb[:, :], bank(f"u{n}")), "u_ready")
                    if n < NT - 1:
                        flat_state = state[:, :, :].rearrange("p c f -> p (c f)")
                        o = bank(f"s{n}")
                        if n == 0:
                            step(v.tensor_copy(flat_state, o), "s_added")
                        else:
                            step(v.tensor_tensor(flat_state, o, flat_state, ALU.add), "s_added")
                        for c in range(CW):
                            last = v.scalar_tensor_tensor(state[:, c, :], state[:, c, :], e_end[:, c, n:n + 1], con("blk64"),
                                                          ALU.mult, ALU.mult)
                        inc(last, "s_ready")
                        after("s_ready", n + 1)

                def head_norm(z, squares, heads, width, eps, name, sqrt_name):
                    z3 = z.rearrange("p n (h d) -> p (n h) d", d=width)
                    q3 = squares.rearrange("p n (h d) -> p (n h) d", d=width)
                    mean, var = hsum[:, 0:heads], hvar[:, 0:heads]
                    wide = [a.unsqueeze(2).broadcast_to([P, heads, width]) for a in (mean, var)]
                    step(v.tensor_reduce(mean, z3, AX_X, ALU.add), name)
                    step(v.scalar_tensor_tensor(z3, wide[0], -1.0 / width, z3, ALU.mult, ALU.add), name)
                    step(v.tensor_tensor(q3, z3, z3, ALU.mult), name)
                    step(v.tensor_reduce(var, q3, AX_X, ALU.add), name)
                    step(v.tensor_scalar(var, var, 1.0 / width, eps, ALU.mult, ALU.add), name)
                    after(sqrt_name)
                    step(v.reciprocal(var, var), name)
                    step(v.tensor_tensor(z3, z3, wide[1], ALU.mult), name)

                after("y_ready")
                head_norm(y_tok, G_, 32, RW_D, RW_EPS, "y_norm", "y_sqrt")
                for i, (raw, rot) in enumerate(((rq_raw, rq_rot), (rk_raw, rk_rot))):
                    after("ret_tok", 4 * i + 4)
                    x = raw.rearrange("p n (h e d) -> p n h e d", h=RET_H, e=2)
                    y = rot.rearrange("p n (h e d) -> p n h e d", h=RET_H, e=2)
                    t1, t2 = (a.rearrange("p (n h d) -> p n h d", n=NT, h=RET_H) for a in rot_tmp)
                    cs, sn = (a[:, :, :].unsqueeze(2).broadcast_to([P, NT, RET_H, 64]) for a in (cosT, sinT))
                    if i == 1:
                        after("rot_ready", 1)
                    v.tensor_tensor(t1, x[:, :, :, 0, :], cs, ALU.mult)
                    step(v.tensor_tensor(t2, x[:, :, :, 1, :], sn, ALU.mult), "rot_step")
                    step(v.tensor_tensor(y[:, :, :, 0, :], t1, t2, ALU.subtract), "rot_step")
                    v.tensor_tensor(t1, x[:, :, :, 0, :], sn, ALU.mult)
                    step(v.tensor_tensor(t2, x[:, :, :, 1, :], cs, ALU.mult), "rot_step")
                    inc(v.tensor_tensor(y[:, :, :, 1, :], t1, t2, ALU.add), "rot_ready")
                after("rot_ready")
                for h in range(RET_H):
                    cols = slice(h * P, h * P + P)
                    last = v.tensor_scalar(k_tail[:, :, cols], rk_rot[:, :, cols], con("ret_k", h), None, ALU.mult)
                inc(last, "ktail_ready")
                for h in range(RET_H):
                    o = bank(f"tq{h}").rearrange("p (n t) -> p n t", n=NT)
                    after("qT_ready", h + 1)
                    decay = con("ret_q")[:, h * P:h * P + P].unsqueeze(1).broadcast_to([P, NT, P])
                    inc(v.tensor_tensor(qdT[:, h, :].rearrange("p (n t) -> p n t", n=NT), o, decay, ALU.mult), "qd_ready")
                def retention_mask(n):
                    inc(v.tensor_tensor(p_ret[n % 2], bank(f"sc{n}"), con("ret_mask"), ALU.mult), "pret_ready")

                retention_mask(0)
                for n in range(NT):
                    if n < NT - 1:
                        retention_mask(n + 1)
                        o = bank(f"kv{n}")
                        if n == 0:
                            last = v.tensor_copy(state[:, :, :].rearrange("p h e -> p (h e)"), o)
                        else:
                            for h in range(RET_H):
                                decay = math.exp(math.log1p(-(2.0 ** (-5.0 - h))) * P)
                                last = v.scalar_tensor_tensor(state[:, h, :], state[:, h, :], decay, o[:, h * P:h * P + P],
                                                              ALU.mult, ALU.add)
                        inc(last, "R_ready")
                        after("R_ready", n + 1)
                after("o_ready")
                head_norm(o_tok, o_sq, 16, RET_D, RET_EPS, "o_norm", "o_sqrt")
                after("rg_ready")
                for c in range(CW):
                    step(v.scalar_tensor_tensor(br_rwkv[:, c, :], bank(f"ty{c}"), par("ln_w", c), br_rwkv[:, c, :], ALU.mult, ALU.add),
                         "y_scaled")
                    inc(v.scalar_tensor_tensor(br_rwkv[:, c, :], br_rwkv[:, c, :], par("ln_b", c), A_[:, c, :], ALU.add, ALU.mult),
                        "rwkv_done")
                after("retg_ready")
                for h in range(RET_H):
                    inc(v.scalar_tensor_tensor(br_ret[:, h, :], bank(f"to{h}"), par("ret_norm_g", h), ret_gate[:, h, :],
                                               ALU.mult, ALU.mult), "ret_done")
                for n in range(3):
                    after("br_high", n + 1)
                    inc(v.tensor_tensor(r(branches[n][:, :, :]), branches[n][:, :, :], r(branches_hi[n]), ALU.subtract), "br_split")

                def merged_low(c):
                    after("m_high", c + 1)
                    inc(v.tensor_tensor(r(mT[:, c, :]), mT[:, c, :], r(m_hi[c]), ALU.subtract), "m_split")

                for cp in range(KD // 2):
                    if cp > 0:
                        merged_low(2 * cp - 2)
                        merged_low(2 * cp - 1)
                    for cc in range(2):
                        c = 2 * cp + cc
                        for n in range(3):
                            after("gate_sig", 6 * cp + 2 * n + cc + 1)
                            o = bank(f"b{cp}{cc}{n}")
                            sig = sig_gate[:, 6 * (cp % 2) + 2 * n + cc, :]
                            part = (mT[:, c, :], w_sb[:, :], u_sb[:, :])[n]
                            step(v.tensor_tensor(part, o, sig, ALU.mult), "merged")
                            if n > 0:
                                step(v.tensor_tensor(mT[:, c, :], mT[:, c, :], part, ALU.add), "merged")
                merged_low(KD - 2)
                merged_low(KD - 1)

                def add_square(k):
                    after("xsq_ready", k + 1)
                    step(v.tensor_tensor(hT[:, 0, :], hT[:, 0, :], hT[:, k, :], ALU.add), "xsq_summed")

                for c in range(KD):
                    inc(v.scalar_tensor_tensor(xT[:, c, :], bank(f"wo{c}"), mod[:, 16 + c:17 + c], xT[:, c, :],
                                               ALU.mult, ALU.add), "x_done")
                    if c >= 2:
                        add_square(c - 1)
                add_square(KD - 1)
                after("rms_sqrt")
                inc(v.reciprocal(rstd[:, :], rstd[:, :]), "rms_ready")

            @block.gpsimd
            def _(pool):
                g = nc.gpsimd

                count = [0]

                def low(first, end):
                    for b in range(first, end):
                        if b not in WHOLE:
                            pool.wait_ge(SEM["w_high"], split_count(b))
                            hi, lo = chunk(b)
                            inc(g.tensor_tensor(r(lo), lo, r(hi), ALU.subtract), "w_split")

                def step(ins):
                    inc(ins, "pool_step")
                    count[0] += 1
                    pool.wait_ge(SEM["pool_step"], count[0])

                tmp = [zt.rearrange("p u t -> p (u t)")[:, i * T:i * T + T] for i in range(2)]
                fix = tt.rearrange("p u t -> p (u t)")[:, 0:16]
                low(0, FIRST["pg"])
                for i, w in enumerate(WINDOWS):
                    u = pool_u[:, i, :]
                    pool.wait_ge(SEM["pu_ready"], i + 1)
                    src, lag = u, 1
                    while lag < w:
                        dst = tmp[0] if src is not tmp[0] else tmp[1]
                        inc(g.tensor_copy(dst[:, 0:lag], src[:, 0:lag]), "pool_step")
                        count[0] += 1
                        step(g.tensor_tensor(dst[:, lag:T], src[:, lag:T], src[:, 0:T - lag], ALU.add))
                        src, lag = dst, 2 * lag
                    step(g.tensor_tensor(fix, src[:, 0:16], con("inv_count")[:, 16 * i:16 * i + 16], ALU.mult))
                    step(g.tensor_tensor(fix, fix, u[:, 0:16], ALU.subtract))
                    step(g.tensor_scalar(src, src, 1.0 / w, None, ALU.mult))
                    step(g.tensor_tensor(u, src, u, ALU.subtract))
                    inc(g.tensor_copy(u[:, 0:16], fix), "pool_d")
                    if i < 2:
                        low(FIRST["pg"] + 2 * i, FIRST["pg"] + 2 * i + 2)
                low(FIRST["retq"], LAYER_B)

          numbers = [SEM[name].num for name in LAYER_SEMS]
          assert numbers == list(range(numbers[0], numbers[-1] + 1))
          nc.sync.sem_clear(range(numbers[0], numbers[-1] + 1))
          nc.all_engine_barrier()
        layer_ctx.close()
        jobs = []
        job("ss1", "n_root", 1)
        job("f", "f_step", 1)
        for i, what in enumerate(("qd", "kd", "vd", "qf", "kf", "vf")):
            for c in range(CW):
                job(f"{what}{c}", "qkv_ready", 4 * i + c + 1)
        for h in range(FOX_H):
            job(f"nc{h}", "nc_ready", h + 1)
        heads = [(kind, tb, h) for kind in range(2) for tb in range(NT) for h in range(DIL_H)]
        for i in range(-2, len(heads)):
            if i + 2 < len(heads):
                job(f"s{i + 2}", "s_shifted", i + 3)
            if i >= 0:
                job(f"p{i}", "pt_ready", i + 1)
        for c in range(KD):
            job(f"ot{c}", "oT_ready", c + 1)
        for c in range(KD):
            job(f"ao{c}", "x_att", c + 1)
        job("ss2", "n_root", 2)
        job("logits", "logits_ready", 1)
        for n in range(NT):
            for i in range(2):
                job(f"hk{n}{i}", "h_tok", 2 * n + i + 1)
            if n == 0:
                job("route", "route_step", 1)
        job("rank", "rank_read", 1)
        for n in range(NT):
            for i in range(2):
                job(f"xk{n}{i}", "x_tok", 2 * n + i + 1)
        RB = 6
        JOB = {name: j for j, (name, _, _) in enumerate(jobs)}
        DRAIN = {name: (sem_name, k) for name, sem_name, k in jobs}
        att_jobs = list(jobs)
        full_of = lambda name: ("att_full", JOB[name] + 1)
        chunk_used = []
        for kind in range(2):
            chunk_used += [full_of(f"{w}{c}") for w in (("qd", "kd"), ("qf", "kf"))[kind] for c in range(CW)]
            for b in range(2):
                chunk_used += [("half_read", 2 * kind + b + 1), full_of(f"v{'df'[kind]}{2 * b + 1}")]
        chunk_used += [full_of(f"ao{c}") for c in range(KD)]
        assert len(chunk_used) == ATT_B
        OUT = 6 * CW

        for name in ("att_full", "bias_loaded", "zero_set", "x_zeroed", "fnorm_loaded",
                     "n_sq", "sq_summed", "n_mean", "n_root", "n_out", "f_step", "f_act", "negc_step", "qkv_ready", "nc_ready",
                     "s_shifted", "s_max", "s_exp", "pt_ready", "pv_step", "o_step", "o_sq", "o_root", "o_scaled",
                     "oT_ready", "x_att", "route_step", "route_exp", "m_ready", "rank_read", "h_tok", "x_tok", "idx_ready",
                     "scattered", "half_read", "logits_ready",
                     "a_high", "a_split", "f_high", "f_split", "hn_high", "hn_split", "oT_split"):
            sem(name)

        qd, kd, vd, qf, kf, vf = SL[:6]
        o_tok = [SL[6], SL[7]]
        bias_d = [SL[8][:, h, :] for h in range(4)] + [br_pool[:, h, :] for h in range(4)]
        neg_c = gm_mem[:, :].rearrange("p (h t) -> p h t", h=FOX_H)
        w_f = state[:, 0, :].rearrange("p (i n) -> p i n", i=2)
        w_fk = [w_f[:, i].rearrange("p (k h) -> p k h", k=KD) for i in range(2)]
        att_stat = cosT[:, :, :].rearrange("p a b -> p (a b)")[:, 0:4 * DIL_H * NT].rearrange("p (s i) -> p s i", s=2)
        squares_mem = slots[:, 6:8].rearrange("p s c t -> p (s c) t")
        s_buf = [flat_ztp[:, i * T:i * T + T] for i in range(4)]
        p_buf = [flat_ztp[:, i * T:i * T + T] for i in range(4, 6)]
        f_sb, f_tmp = w_sb[0:FOX_H, :], u_sb[0:FOX_H, :]
        oT = hT
        zeros = h_hi[:, 0:2, :].rearrange("p k t -> p (k t)")
        h_rows = wmem[:, 0:NT]
        x_rows = h_hi[:, :, :].rearrange("p k t -> p (k t)").rearrange("p (n d) -> p n d", n=NT)
        flat_pool = br_pool[:, :, :].rearrange("p c t -> p (c t)")
        rt = flat_pool[:, 0:26 * EXPERTS].rearrange("p (i n g) -> p i n g", n=NT, g=PER_GROUP)
        route = flat_pool[:, 26 * EXPERTS:26 * EXPERTS + NT * ROUTE].rearrange("p (n e) -> p n e", n=NT)
        n_max, n_sum = att_stat[:, 0, :], att_stat[:, 1, :]
        logits = w_sb[0:ROUTE, :]

        for name in ["turned", "xs_act", "xs_dve", "gu_done", "silu_done", "he_ready", "down_done", "y_act", "y_dve"] + \
                [f"{what}{b}" for what in ("xs_loaded", "gu_loaded", "dn_loaded", "ys_stored") for b in range(UNROLL)]:
            sem(name)
        ROUNDS = EXPERTS // UNROLL
        EARLY = 3
        GU, DN = KD * 2 * FF, 2 * D
        flat_slots = slots[:, 0:8].rearrange("p s c t -> p (s c t)")
        flat_x = xT[:, :, :].rearrange("p k t -> p (k t)")
        gu_mem = [flat_slots[:, b * GU:(b + 1) * GU] for b in range(UNROLL)]
        dn_mem = [SL[8].rearrange("p c t -> p (c t)"), flat_x[:, 0:DN], flat_x[:, DN:2 * DN], wmem[:, 0:2].rearrange("p s n -> p (s n)")]
        w_gu = [m.rearrange("p (k f) -> p k f", k=KD) for m in gu_mem]
        w_dn = [m.rearrange("p (f d) -> p f d", f=2) for m in dn_mem]

        with nc.Block() as block:
            @block.sync
            def _(sp):
                def load_chunk(b):
                    name, count = chunk_used[b - RING]
                    sp.wait_ge(SEM[name], count)
                    sp.dma_start(wmem[:, b % RING], wstream[LAYERS * LAYER_B + b]).then_inc(SEM[f"wload{b % RING}"], 16)

                for b in range(RING, OUT + RING):
                    load_chunk(b)
                    if CW < b <= CW + DIL_H:
                        h = b - CW - 1
                        skew = dil_rows[h:h + 1, P - 1:P - 1 + P * (DIL_ROW - 1)].rearrange("a (p y) -> (a p) y", y=DIL_ROW - 1)
                        sp.dma_start(bias_d[h], skew[:, 0:T]).then_inc(SEM["bias_loaded"], 16)
                sp.wait_ge(SEM["zero_set"], 1)
                sp.dma_start(x_slots.rearrange("(i p) d -> p i d", p=SLOT),
                             zeros[0:SLOT].unsqueeze(1).broadcast_to([SLOT, TILES, D])).then_inc(SEM["x_zeroed"], 16)
                sp.dma_start(y_slots[EXPERTS * SLOT:TILES * SLOT].rearrange("(i p) d -> p i d", p=SLOT),
                             zeros[0:SLOT].unsqueeze(1).broadcast_to([SLOT, EXTRA, D])).then_inc(SEM["x_zeroed"], 16)
                for b in range(OUT + RING, ATT_B):
                    load_chunk(b)
                sp.wait_ge(SEM["pv_step"], len(heads))
                sp.dma_start(dn_mem[0], experts[0, :, GU:GU + DN]).then_inc(SEM["dn_loaded0"], 16)
                for b in range(EARLY):
                    sp.dma_start(gu_mem[b], experts[b, :, 0:GU]).then_inc(SEM[f"gu_loaded{b}"], 16)

            @block.tensor
            def _(pe):
                at = [0]

                def after(name, k):
                    pe.wait_ge(SEM[name], k)

                def open_bank(name):
                    j = at[0]
                    assert att_jobs[j][0] == name, (name, att_jobs[j])
                    if j >= RB:
                        after(*att_jobs[j - RB][1:])
                    at[0] = j + 1
                    return banks[:, j % RB]

                def full(mm):
                    mm.then_inc(SEM["att_full"], 1)

                def weights(b):
                    after("a_split", b + 1)
                    return chunk(b)

                def feature_job(name, b, x, fresh=False):
                    w, o = [part.rearrange("p (k n) -> p k n", k=KD) for part in weights(b)], open_bank(name)
                    for k in range(KD):
                        if fresh:
                            after("oT_split", k + 1)
                        for i, (lhs, rhs) in enumerate(products(w, x)):
                            mm = nc.tensor.matmul(o, r(lhs[:, k, :]), r(rhs[:, k, :]),
                                                  start=(k == 0 and i == 0), stop=(k == KD - 1 and i == 2))
                    full(mm)

                o = open_bank("ss1")
                for k in range(KD):
                    after("n_sq", k + 1)
                    mm = nc.tensor.matmul(o, con("mean"), squares_mem[:, k, :], start=(k == 0), stop=(k == KD - 1))
                full(mm)
                after("f_split", 1)
                o = [open_bank("f")[0:FOX_H, :], open_bank("qd0")]
                w = [w_fk, [part.rearrange("p (k n) -> p k n", k=KD) for part in weights(0)]]
                for j in range(2):
                    for k in range(KD):
                        if j == 0:
                            after("hn_high", k + 1)
                        for i in range(2):
                            nc.tensor.matmul(o[j], r(w[j][i][:, k, :]), r(h_hi[:, k, :]), start=(k == 0 and i == 0), stop=False)
                for j in range(2):
                    for k in range(KD):
                        if j == 0:
                            after("hn_split", k + 1)
                        mm = nc.tensor.matmul(o[j], r(w[j][0][:, k, :]), r(hT[:, k, :]), start=False, stop=(k == KD - 1))
                    full(mm)
                for i, what in enumerate(("qd", "kd", "vd", "qf", "kf", "vf")):
                    if what[0] != "v":
                        for c in range(1 if i == 0 else 0, CW):
                            feature_job(f"{what}{c}", CW * i + c, (h_hi, hT))
                        continue
                    for b in range(2):
                        o = [open_bank(f"{what}{2 * b + tp}") for tp in range(2)]
                        for half in range(2):
                            w = [part.rearrange("p (k n) -> p k n", k=KD // 2) for part in weights(CW * i + 2 * b + half)]
                            for n in range(NT):
                                cols = slice(n % 2 * 256, n % 2 * 256 + 256)
                                for k in range(KD // 2):
                                    for j, (lhs, rhs) in enumerate(products((h_hi, hT), w)):
                                        mm = nc.tensor.matmul(o[n // 2][:, cols], r(lhs[:, KD // 2 * half + k, n * P:n * P + P]),
                                                              r(rhs[:, k, :]), start=(half == 0 and n % 2 == 0 and k == 0 and j == 0),
                                                              stop=(half == 1 and k == KD // 2 - 1 and j == 2), skip_group_check=True)
                                if half == 1 and n % 2 == 1:
                                    full(mm)
                            if half == 0:
                                mm.then_inc(SEM["half_read"], 1)
                after("negc_step", 4)
                for h in range(FOX_H):
                    o = open_bank(f"nc{h}")
                    full(nc.tensor.matmul(o, ident[0:FOX_H, h:h + 1].broadcast_to([FOX_H, P]), f_sb, start=True, stop=True))
                after("qkv_ready", 24)

                def scores(i):
                    kind, tb, h = heads[i]
                    q, k = ((qd, kd), (qf, kf))[kind]
                    p0, c, n = 64 * (h % 2), h // 2, (tb + 1) * P
                    o = open_bank(f"s{i}")
                    query, keys = q[p0:p0 + 64, c, tb * P:n], k[p0:p0 + 64, c, :]
                    if kind == 0:
                        mm = nc.tensor.matmul(o[:, 0:n], query, keys[:, 0:n], start=True, stop=True)
                    else:
                        if tb > 0:
                            nc.tensor.matmul(o[:, 0:tb * P], query, keys[:, 0:tb * P], start=True, stop=True)
                        nc.tensor.matmul(o[:, tb * P:n], query, keys[:, tb * P:n], start=True, stop=False)
                        mm = nc.tensor.matmul(o[:, tb * P:n], ident, con("causal"), start=False, stop=True)
                    full(mm)

                def turn(i):
                    kind, tb, h = heads[i]
                    after("s_exp", i + 1)
                    o = open_bank(f"p{i}")
                    for sb_ in range(tb + 1):
                        mm = nc.tensor.matmul(o[:, sb_ * P:sb_ * P + P], s_buf[i % 4][:, sb_ * P:sb_ * P + P], ident, start=True, stop=True)
                    full(mm)

                def values(i):
                    kind, tb, h = heads[i]
                    v = (vd, vf)[kind]
                    after("pt_ready", i + 1)
                    group = 4 * kind + tb
                    if h == 0 and group >= 2:
                        after("o_step", 2 * (group - 1))
                    o = banks[:, 6 + group % 2]
                    for sb_ in range(tb + 1):
                        mm = nc.tensor.matmul(o[:, h * HD:h * HD + HD], p_buf[i % 2][:, sb_ * P:sb_ * P + P],
                                              v[:, sb_, h * HD:h * HD + HD], start=(sb_ == 0), stop=(sb_ == tb))
                    mm.then_inc(SEM["pv_step"], 1)

                for i in range(-2, len(heads) + 1):
                    if i + 2 < len(heads):
                        scores(i + 2)
                    if 0 <= i < len(heads):
                        turn(i)
                    if i >= 1:
                        values(i - 1)
                for c in range(KD):
                    after("o_scaled", 4 * (c // CW) + 4)
                    o = open_bank(f"ot{c}")
                    for n in range(NT):
                        f0 = (c % CW) * P
                        mm = nc.tensor.transpose(o[:, n * P:n * P + P], o_tok[c // CW][:, n, f0:f0 + P], ident)
                    full(mm)
                for c in range(KD):
                    feature_job(f"ao{c}", OUT + c, (h_hi, oT), fresh=(c == 0))
                after("sq_summed", KD - 1)
                full(nc.tensor.matmul(open_bank("ss2"), con("mean"), squares_mem[:, 0, :], start=True, stop=True))
                o = open_bank("logits")
                w_r = glob("w_route").rearrange("p (k e) -> p k e", k=KD)
                for k in range(KD):
                    after("n_out", 2 * KD + k + 1)
                    mm = nc.tensor.matmul(o[0:ROUTE, :], w_r[:, k, :], hT[:, k, :], start=(k == 0), stop=(k == KD - 1))
                full(mm)

                def turn_logits():
                    after("logits_ready", 1)
                    o = open_bank("route")
                    for n in range(NT):
                        mm = nc.tensor.transpose(o[:, n * ROUTE:(n + 1) * ROUTE], logits[:, n * P:n * P + P], ident[0:ROUTE, 0:ROUTE])
                    full(mm)

                def rows_of(name, z):
                    for n in range(NT):
                        for i in range(2):
                            o = open_bank(f"{name}{n}{i}")
                            for k in range(4):
                                mm = nc.tensor.transpose(o[:, k * P:k * P + P], z[:, 4 * i + k, n * P:n * P + P], ident)
                            full(mm)
                        if name == "hk" and n == 0:
                            turn_logits()

                rows_of("hk", hT)
                after("m_ready", 1)
                o = open_bank("rank")
                in_tile, before = (rt[:, i:i + 4].rearrange("p e n g -> p (e n g)") for i in (8, 20))
                nc.tensor.matmul(o[:, 0:NT * EXPERTS], con("gram")[:, 0:P], in_tile, start=True, stop=False, skip_group_check=True)
                full(nc.tensor.matmul(o[:, EXPERTS:(NT + 1) * EXPERTS], con("ones"), before, start=False, stop=True,
                                      skip_group_check=True))
                rows_of("xk", xT)
                assert at[0] == len(att_jobs)

            @block.scalar
            def _(act):
                def after(name, k):
                    act.wait_ge(SEM[name], k)

                def bank(name):
                    act.wait_ge(SEM["att_full"], JOB[name] + 1)
                    return banks[:, JOB[name] % RB]

                def mean_root(i, name, k0):
                    for k in range(KD):
                        after(name, k0 + k + 1)
                        nc.scalar.activation(squares_mem[:, k, :], xT[:, k, :], ACT.Square).then_inc(SEM["n_sq"], 1)
                        if i == 2:
                            high(OUT + k + RING)
                    nc.scalar.activation(rstd[:, :], bank(f"ss{i}"), ACT.Sqrt, bias=con("eps")).then_inc(SEM["n_root"], 1)

                def high(b):
                    if b < ATT_B:
                        w = landed(act, b, 16 * LAYERS * LAYER_B // RING)
                        nc.scalar.activation(r(chunk(b)[0]), w, ACT.Copy).then_inc(SEM["a_high"], 1)

                nc.scalar.activation(r(w_f[:, 0]), glob("w_f"), ACT.Copy).then_inc(SEM["f_high"], 1)
                high(0)
                high(1)
                mean_root(1, "n_out", 0)
                high(2)
                for k in range(KD):
                    after("n_out", KD + k + 1)
                    nc.scalar.activation(r(h_hi[:, k, :]), hT[:, k, :], ACT.Copy).then_inc(SEM["hn_high"], 1)
                after("f_step", 2)
                nc.scalar.activation(f_tmp, f_tmp, ACT.Exp).then_inc(SEM["f_act"], 1)
                after("f_act", 1)
                nc.scalar.activation(f_tmp, f_tmp, ACT.Ln, bias=1.0).then_inc(SEM["f_act"], 1)
                for i, (z, what) in enumerate(((qd, "qd"), (kd, "kd"), (vd, "vd"), (qf, "qf"), (kf, "kf"), (vf, "vf"))):
                    for c in range(CW):
                        if what[0] == "v" and c % 2 == 0:
                            high(CW * i + c + RING)
                        o = bank(f"{what}{c}")
                        dst = z[:, c, :]
                        if what[0] == "v":
                            o = o.rearrange("p (n f) -> p n f", n=2)
                            dst = z[:, 2 * (c % 2):2 * (c % 2) + 2, (c // 2) * 256:(c // 2) * 256 + 256]
                        nc.scalar.activation(dst, o, ACT.Copy).then_inc(SEM["qkv_ready"], 1)
                        if what[0] != "v" or c % 2 == 1:
                            high(CW * i + c + RING)
                for h in range(FOX_H):
                    nc.scalar.activation(neg_c[:, h, :], bank(f"nc{h}"), ACT.Copy).then_inc(SEM["nc_ready"], 1)

                def token_squares(group):
                    after("o_step", 2 * group + 2)
                    if group:
                        after("o_sq", group)
                    nc.scalar.activation(u_sb[:, :], o_tok[group // NT][:, group % NT, :], ACT.Square,
                                         accum_out=hvar[:, group:group + 1]).then_inc(SEM["o_sq"], 1)

                for i, (kind, tb, h) in enumerate(heads):
                    n = (tb + 1) * P
                    after("s_max", i + 1)
                    nc.scalar.activation(s_buf[i % 4][:, 0:n], s_buf[i % 4][:, 0:n], ACT.Exp, bias=n_max[:, i:i + 1],
                                         accum_out=n_sum[:, i:i + 1]).then_inc(SEM["s_exp"], 1)
                    if i >= 1:
                        j = i - 1
                        if j >= 2:
                            after("pv_step", j - 1)
                        m = (heads[j][1] + 1) * P
                        nc.scalar.activation(p_buf[j % 2][:, 0:m], bank(f"p{j}")[:, 0:m], ACT.Copy).then_inc(SEM["pt_ready"], 1)
                    if h == 5 and i > 8:
                        token_squares(i // 8 - 1)
                j = len(heads) - 1
                after("pv_step", j - 1)
                nc.scalar.activation(p_buf[j % 2], bank(f"p{j}"), ACT.Copy).then_inc(SEM["pt_ready"], 1)
                token_squares(2 * NT - 1)
                after("o_step", 17)
                nc.scalar.activation(hvar[:, 0:8], hvar[:, 0:8], ACT.Sqrt).then_inc(SEM["o_root"], 1)
                after("o_step", 18)
                for kind in range(2):
                    for tb in range(NT):
                        j = 4 * kind + tb
                        nc.scalar.activation(o_tok[kind][:, tb, :], o_tok[kind][:, tb, :], ACT.Copy, scale=hvar[:, j:j + 1]) \
                            .then_inc(SEM["o_scaled"], 1)
                after("x_zeroed", 32)
                for c in range(KD):
                    o = bank(f"ot{c}")
                    nc.scalar.activation(r(h_hi[:, c, :]), o, ACT.Copy, scale=glob("out_norm", c))
                    nc.scalar.activation(oT[:, c, :], o, ACT.Copy, scale=glob("out_norm", c)).then_inc(SEM["oT_ready"], 1)
                mean_root(2, "x_att", 0)
                nc.scalar.activation(logits, bank("logits")[0:ROUTE, :], ACT.Identity, bias=glob("b_route")[0:ROUTE, :]) \
                    .then_inc(SEM["logits_ready"], 1)
                for name, rows, done in (("hk", h_rows, "h_tok"), ("xk", x_rows, "x_tok")):
                    for n in range(NT):
                        for i in range(2):
                            nc.scalar.activation(rows[:, n, i * T:i * T + T], bank(f"{name}{n}{i}"), ACT.Copy) \
                                .then_inc(SEM[done], 1)
                    if name == "hk":
                        after("route_step", 5)
                        nc.scalar.activation(rt[:, 0, :, 0:4], rt[:, 0, :, 0:4], ACT.Exp).then_inc(SEM["route_exp"], 1)
                        after("route_step", 30)
                        nc.scalar.activation(rt[:, 4, :, 3:4], rt[:, 4, :, 2:3], ACT.Exp).then_inc(SEM["route_exp"], 1)

            @block.vector
            def _(dve):
                v = nc.vector
                count = {}

                def after(name, k):
                    dve.wait_ge(SEM[name], k)

                def bank(name):
                    dve.wait_ge(SEM["att_full"], JOB[name] + 1)
                    return banks[:, JOB[name] % RB]

                def step(ins, name):
                    ins.then_inc(SEM[name], 1)
                    count[name] = count.get(name, 0) + 1
                    after(name, count[name])

                def scale(out_, gain):
                    for k in range(KD):
                        v.scalar_tensor_tensor(out_[:, k, :], xT[:, k, :], glob(gain, k), rstd[:, :], ALU.mult, ALU.mult) \
                            .then_inc(SEM["n_out"], 1)

                def norm(i, out_, gain):
                    after("n_root", i)
                    step(v.reciprocal(rstd[:, :], rstd[:, :]), "n_mean")
                    scale(out_, gain)

                def add_square(k):
                    after("n_sq", KD + k + 1)
                    step(v.tensor_tensor(squares_mem[:, 0, :], squares_mem[:, 0, :], squares_mem[:, k, :], ALU.add), "sq_summed")

                def gather(group):
                    kind, tb = group // NT, group % NT
                    after("pv_step", DIL_H * (group + 1))
                    after("s_exp", DIL_H * (group + 1))
                    inv = n_sum[:, DIL_H * group:DIL_H * (group + 1)]
                    step(v.reciprocal(inv, inv), "o_step")
                    o = banks[:, 6 + group % 2].rearrange("p (h d) -> p h d", h=DIL_H)
                    step(v.tensor_tensor(o_tok[kind][:, tb, :].rearrange("p (h d) -> p h d", h=DIL_H), o,
                                         inv.unsqueeze(2).broadcast_to([P, DIL_H, HD]), ALU.mult), "o_step")

                scale(xT, "final_g")
                norm(1, hT, "attn_norm")
                for k in range(KD):
                    after("hn_high", k + 1)
                    v.tensor_tensor(r(hT[:, k, :]), hT[:, k, :], r(h_hi[:, k, :]), ALU.subtract).then_inc(SEM["hn_split"], 1)
                step(v.tensor_scalar(f_sb, bank("f")[0:FOX_H, :], glob("b_forget")[0:FOX_H, :], None, ALU.add), "f_step")
                step(v.scalar_tensor_tensor(f_tmp, f_sb, -1.0, f_sb, ALU.mult, ALU.min), "f_step")
                step(v.tensor_scalar(f_sb, f_sb, 0.0, None, ALU.min), "f_step")
                after("f_act", 2)
                step(v.tensor_tensor(f_tmp, f_tmp, f_sb, ALU.subtract), "f_step")
                for n in range(NT):
                    first = 0.0 if n == 0 else f_sb[:, n * P - 1:n * P]
                    step(v.tensor_tensor_scan(f_sb[:, n * P:n * P + P], con("ones")[0:FOX_H, :], f_tmp[:, n * P:n * P + P],
                                              first, ALU.mult, ALU.add), "negc_step")
                after("bias_loaded", 16 * DIL_H)
                for i, (kind, tb, h) in enumerate(heads):
                    n = (tb + 1) * P
                    if kind:
                        after("nc_ready", h + 1)
                        bias = neg_c[:, h, 0:n]
                    else:
                        bias = bias_d[h][:, T - n:T]
                    if i >= 4:
                        after("att_full", JOB[f"p{i - 4}"] + 1)
                    step(v.scalar_tensor_tensor(s_buf[i % 4][:, 0:n], bank(f"s{i}")[:, 0:n], ATT_SCALE, bias,
                                                ALU.mult, ALU.add), "s_shifted")
                    v.tensor_reduce(n_max[:, i:i + 1], s_buf[i % 4][:, 0:n], AX_X, ALU.max, negate=True) \
                        .then_inc(SEM["s_max"], 1)
                    if h == 3 and i > 8:
                        gather(i // 8 - 1)
                gather(2 * NT - 1)
                after("o_sq", 8)
                step(v.tensor_scalar(hvar[:, 0:8], hvar[:, 0:8], 1.0 / (DIL_H * HD), RMS_EPS, ALU.mult, ALU.add), "o_step")
                after("o_root", 1)
                step(v.reciprocal(hvar[:, 0:8], hvar[:, 0:8]), "o_step")
                for c in range(KD):
                    after("oT_ready", c + 1)
                    v.tensor_tensor(r(oT[:, c, :]), oT[:, c, :], r(h_hi[:, c, :]), ALU.subtract).then_inc(SEM["oT_split"], 1)
                for c in range(KD):
                    v.tensor_tensor(xT[:, c, :], bank(f"ao{c}"), xT[:, c, :], ALU.add).then_inc(SEM["x_att"], 1)
                    if c >= 2:
                        add_square(c - 1)
                add_square(KD - 1)
                norm(2, hT, "ffn_norm")
                route_op = lambda ins: step(ins, "route_step")
                route_op(v.tensor_copy(route[:, :, :], bank("route")[:, 0:NT * ROUTE].rearrange("p (n e) -> p n e", n=NT)))
                groups, experts_ = route[:, :, 0:GROUPS], route[:, :, GROUPS:ROUTE]
                t4 = lambda i: rt[:, i, :, 0:4]
                col = lambda i, j: rt[:, i, :, j:j + 1]
                w4 = lambda a: a.broadcast_to([P, NT, 4])
                w8 = lambda a: a.broadcast_to([P, NT, 8])
                rowb = lambda name, a, b: con(name)[:, a:b].unsqueeze(1).broadcast_to([P, NT, b - a])
                gmax, gsum, gbest = col(2, 0), col(2, 1), col(2, 2)
                route_op(v.tensor_reduce(gmax, groups, AX_X, ALU.max))
                route_op(v.tensor_tensor(t4(1), groups, w4(gmax), ALU.is_equal))
                route_op(v.tensor_tensor(t4(1), t4(1), rowb("rev", 0, 4), ALU.mult))
                route_op(v.tensor_tensor(t4(0), groups, w4(gmax), ALU.subtract))
                route_op(v.tensor_reduce(gbest, t4(1), AX_X, ALU.max))
                route_op(v.tensor_scalar(gbest, gbest, -1.0, 8.0, ALU.mult, ALU.add))
                route_op(v.tensor_tensor(t4(1), rowb("iota", 0, 4), w4(gbest), ALU.is_equal))
                sel, part = rt[:, 3], rt[:, 5]
                route_op(v.tensor_tensor(sel, experts_[:, :, 0:8], w8(rt[:, 1, :, 0:1]), ALU.mult))
                for gi in range(1, GROUPS):
                    route_op(v.tensor_tensor(part, experts_[:, :, 8 * gi:8 * gi + 8], w8(rt[:, 1, :, gi:gi + 1]), ALU.mult))
                    route_op(v.tensor_tensor(sel, sel, part, ALU.add))
                for k in range(TOP_K):
                    best, val = col(6, k), col(4, k)
                    route_op(v.tensor_reduce(val, sel, AX_X, ALU.max))
                    route_op(v.tensor_tensor(part, sel, w8(val), ALU.is_equal))
                    route_op(v.tensor_tensor(part, part, rowb("rev", 0, 8), ALU.mult))
                    route_op(v.tensor_reduce(best, part, AX_X, ALU.max))
                    route_op(v.tensor_scalar(best, best, -1.0, 8.0, ALU.mult, ALU.add))
                    if k == 0:
                        route_op(v.tensor_tensor(part, rowb("iota", 0, 8), w8(best), ALU.is_equal))
                        route_op(v.scalar_tensor_tensor(sel, part, -3e38, sel, ALU.mult, ALU.add))
                    route_op(v.scalar_tensor_tensor(best, gbest, 8.0, best, ALU.mult, ALU.add))
                route_op(v.tensor_tensor(col(4, 2), col(4, 1), col(4, 0), ALU.subtract))
                after("route_exp", 2)
                route_op(v.tensor_reduce(gsum, t4(0), AX_X, ALU.add))
                route_op(v.tensor_scalar(col(4, 4), col(4, 3), 1.0, None, ALU.add))
                route_op(v.tensor_tensor(gsum, gsum, col(4, 4), ALU.mult))
                route_op(v.reciprocal(col(7, 0), gsum))
                route_op(v.tensor_tensor(col(7, 1), col(7, 0), col(4, 3), ALU.mult))
                lay = lambda i: rt[:, i:i + 4].rearrange("p e n g -> p (e n g)").rearrange("p (n e) -> p n e", n=NT)
                chosen, hot, where, prod = lay(8), (lay(12), lay(16)), lay(20), lay(8)
                for k in range(TOP_K):
                    route_op(v.tensor_tensor(hot[k], rowb("iota", 0, EXPERTS), col(6, k).broadcast_to([P, NT, EXPERTS]), ALU.is_equal))
                route_op(v.tensor_tensor(chosen, hot[0], hot[1], ALU.add))
                route_op(v.tensor_copy(where[:, 0, :], chosen[:, 0, :]))
                for n in range(1, NT):
                    ins = v.tensor_tensor(where[:, n, :], where[:, n - 1, :], chosen[:, n, :], ALU.add)
                    if n < NT - 1:
                        route_op(ins)
                ins.then_inc(SEM["m_ready"], 1)
                o = bank("rank")
                extra, incl, jump = (rt[:, i].rearrange("p n g -> p (n g)") for i in (24, 25, 0))
                cnt = o[:, NT * EXPERTS:(NT + 1) * EXPERTS]
                route_op(v.tensor_scalar(extra, cnt, float(SLOT), None, ALU.is_gt))
                for k in range(2, -(-T // SLOT)):
                    route_op(v.scalar_tensor_tensor(extra, cnt, float(k * SLOT), extra, ALU.is_gt, ALU.add))
                route_op(v.tensor_tensor_scan(incl, con("ones")[:, 0:EXPERTS], extra, 0.0, ALU.mult, ALU.add))
                numbers = con("iota")[:, 0:EXPERTS]
                route_op(v.tensor_tensor(jump, incl, extra, ALU.subtract))
                route_op(v.scalar_tensor_tensor(jump, jump, EXPERTS - 1.0, numbers, ALU.add, ALU.subtract))
                route_op(v.tensor_scalar(jump, jump, float(SLOT), None, ALU.mult))
                rank = o[:, 0:NT * EXPERTS].rearrange("p (n e) -> p n e", n=NT)
                route_op(v.scalar_tensor_tensor(where, rank, float(SLOT), jump.unsqueeze(1).broadcast_to([P, NT, EXPERTS]),
                                         ALU.is_ge, ALU.mult))
                step(v.scalar_tensor_tensor(prod, rowb("iota", 0, EXPERTS), float(SLOT), rank, ALU.mult, ALU.add), "rank_read")
                route_op(v.tensor_tensor(where, where, prod, ALU.add))
                for k in range(TOP_K):
                    route_op(v.tensor_tensor(prod, hot[k], where, ALU.mult))
                    route_op(v.tensor_reduce(col(6, 2 + k), prod, AX_X, ALU.add))
                    v.tensor_copy(slot_idx[:, k, :], rt[:, 6, :, 2 + k]).then_inc(SEM["idx_ready"], 1)
                ends = gm_mem[:, 0:EXTRA * EXPERTS].rearrange("p (i e) -> p i e", e=EXPERTS)
                route_op(v.tensor_tensor(ends, incl.unsqueeze(1).broadcast_to([P, EXTRA, EXPERTS]),
                                  con("iota")[:, 0:EXTRA].unsqueeze(2).broadcast_to([P, EXTRA, EXPERTS]), ALU.is_le))
                of_tile = w_sb[:, 0:EXTRA + 1]
                route_op(v.tensor_reduce(of_tile[:, 0:EXTRA], ends, AX_X, ALU.add))
                route_op(v.tensor_scalar(of_tile[:, 0:EXTRA], of_tile[:, 0:EXTRA], float(EXPERTS - 1), None, ALU.min))
                route_op(v.tensor_copy(of_tile[:, EXTRA:EXTRA + 1], incl[:, EXPERTS - 1:EXPERTS]))
                v.tensor_copy(tile_exp[:, :], of_tile).then_inc(SEM["idx_ready"], 1)

            @block.gpsimd
            def _(pool):
                def low(first, end):
                    for b in range(first, end):
                        pool.wait_ge(SEM["a_high"], b + 1)
                        hi, lo = chunk(b)
                        nc.gpsimd.tensor_tensor(r(lo), lo, r(hi), ALU.subtract).then_inc(SEM["a_split"], 1)

                pool.wait_ge(SEM["f_high"], 1)
                nc.gpsimd.tensor_tensor(r(w_f[:, 1]), glob("w_f"), r(w_f[:, 0]), ALU.subtract).then_inc(SEM["f_split"], 1)
                low(0, OUT + RING)
                pool.wait_ge(SEM["att_full"], JOB["vf3"] + 1)
                nc.gpsimd.memset(zeros, 0.0).then_inc(SEM["zero_set"], 1)
                low(OUT + RING, ATT_B)
                pool.wait_ge(SEM["x_zeroed"], 32)
                pool.wait_ge(SEM["h_tok"], 2 * NT)
                for k in range(TOP_K):
                    pool.wait_ge(SEM["idx_ready"], k + 1)
                    for n in range(NT):
                        pool.indirect_dma_start(out=x_slots, out_offset=bass.IndirectOffsetOnAxis(ap=slot_idx[:, k, n:n + 1], axis=0),
                                                in_=h_rows[:, n, :], in_offset=None).then_inc(SEM["scattered"], 16)
                pool.wait_ge(SEM["scattered"], 16 * NT * TOP_K)

        rows = hT[:, :, :].rearrange("p k t -> p (k t)")
        ys_mem = [flat_ztp[:, 0:D], flat_ztp[:, D:2 * D]] + [wmem[:, 2 + i] for i in range(2)]
        xs = [rows[0:SLOT, b * D:(b + 1) * D] for b in range(UNROLL)]
        ys = [m[0:SLOT, :] for m in ys_mem]
        XT, HE = KD * SLOT, 2 * SLOT
        xsT = [gm_mem[:, b * XT:(b + 1) * XT] for b in range(UNROLL)]
        sil = [gm_mem[:, UNROLL * XT + b * HE:UNROLL * XT + (b + 1) * HE] for b in range(UNROLL)]
        heT = [flat_ztp[:, 2 * D + b * HE:2 * D + (b + 1) * HE] for b in range(UNROLL)]
        halves = [slice(0, T), slice(T, 2 * T)]

        def turn_rows(b, i, bank):
            for k in range(4):
                mm = nc.tensor.transpose(bank[:, k * SLOT:(k + 1) * SLOT], xs[b][:, (4 * i + k) * P:(4 * i + k + 1) * P],
                                         ident[0:SLOT, 0:SLOT])
            return mm

        def gate_up(b, bank):
            for f in range(4):
                for k in range(KD):
                    mm = nc.tensor.matmul(bank[:, f * SLOT:(f + 1) * SLOT], w_gu[b][:, k, f * P:f * P + P],
                                          xsT[b][:, k * SLOT:(k + 1) * SLOT], start=(k == 0), stop=(k == KD - 1))
            return mm

        def down(b, i, bank):
            for f in range(2):
                mm = nc.tensor.matmul(bank[0:SLOT, :], heT[b][:, f * SLOT:(f + 1) * SLOT], w_dn[b][:, f, halves[i]],
                                      start=(f == 0), stop=(f == 1))
            return mm

        def rounds(engine, body):
            body(0, True, False)
            with engine.Fori(1, ROUNDS - 1) as it:
                body(it, False, False)
            body(ROUNDS - 1, False, True)

        with nc.Block() as block:
            @block.sync
            def _(sp):
                def load_rows(b, tile):
                    sp.dma_start(xs[b], x_slots[bass.ds(tile * SLOT, SLOT)]).then_inc(SEM[f"xs_loaded{b}"], 16)

                def load_gate_up(b, tile):
                    sp.dma_start(gu_mem[b], experts[bass.ds(tile, 1), :, 0:GU].rearrange("a p w -> (a p) w")) \
                      .then_inc(SEM[f"gu_loaded{b}"], 16)

                def load_down(b, tile):
                    sp.dma_start(dn_mem[b], experts[bass.ds(tile, 1), :, GU:GU + DN].rearrange("a p w -> (a p) w")) \
                      .then_inc(SEM[f"dn_loaded{b}"], 16)

                for b in range(UNROLL):
                    load_rows(b, b)
                    if b >= EARLY:
                        load_gate_up(b, b)
                    if b > 0:
                        load_down(b, b)
                with sp.Fori(0, ROUNDS - 1) as it:
                    for b in range(UNROLL):
                        tile = UNROLL * it + b
                        sp.wait_ge(SEM["turned"], 2 * tile + 2)
                        load_rows(b, tile + UNROLL)
                        sp.wait_ge(SEM["gu_done"], tile + 1)
                        load_gate_up(b, tile + UNROLL)
                        sp.wait_ge(SEM["down_done"], 2 * tile + 2)
                        load_down(b, tile + UNROLL)

            @block.tensor
            def _(pe):
                def turn(b, it):
                    pe.wait_ge(SEM[f"xs_loaded{b}"], 16 * it + 16)
                    for i in range(2):
                        turn_rows(b, i, banks[:, i]).then_inc(SEM["turned"], 1)

                def body(it, first, last):
                    for b in range(UNROLL):
                        tile = UNROLL * it + b
                        pe.wait_ge(SEM[f"gu_loaded{b}"], 16 * it + 16)
                        pe.wait_ge(SEM["xs_act"], tile + 1)
                        pe.wait_ge(SEM["xs_dve"], tile + 1)
                        if not (first and b < 2):
                            pe.wait_ge(SEM["he_ready"], tile - 1)
                        gate_up(b, banks[:, 2 + b % 2]).then_inc(SEM["gu_done"], 1)
                        if not (last and b == UNROLL - 1):
                            turn((b + 1) % UNROLL, it + (b + 1) // UNROLL)
                        pe.wait_ge(SEM[f"dn_loaded{b}"], 16 * it + 16)
                        pe.wait_ge(SEM["he_ready"], tile + 1)
                        for i in range(2):
                            if not (first and b < 2):
                                pe.wait_ge(SEM[("y_act", "y_dve")[i]], tile - 1)
                            down(b, i, banks[:, 4 + (2 * b + i) % 4]).then_inc(SEM["down_done"], 1)

                turn(0, 0)
                rounds(pe, body)

            @block.scalar
            def _(act):
                def copy_turned(b, tile, early):
                    act.wait_ge(SEM["turned"], 2 * tile + 1)
                    if not early:
                        act.wait_ge(SEM["gu_done"], tile - (UNROLL - 1))
                    nc.scalar.activation(xsT[b][:, 0:4 * SLOT], banks[:, 0, 0:4 * SLOT], ACT.Copy).then_inc(SEM["xs_act"], 1)

                def body(it, first, last):
                    for b in range(UNROLL):
                        tile = UNROLL * it + b
                        act.wait_ge(SEM["gu_done"], tile + 1)
                        if not first:
                            act.wait_ge(SEM["he_ready"], tile - (UNROLL - 1))
                        nc.scalar.activation(sil[b], banks[:, 2 + b % 2, 0:HE], ACT.Silu).then_inc(SEM["silu_done"], 1)
                        if not (last and b == UNROLL - 1):
                            copy_turned((b + 1) % UNROLL, tile + 1, first and b < UNROLL - 1)
                        act.wait_ge(SEM["down_done"], 2 * tile + 1)
                        if not first:
                            act.wait_ge(SEM[f"ys_stored{b}"], 16 * it)
                        nc.scalar.activation(ys[b][:, halves[0]], banks[0:SLOT, 4 + (2 * b) % 4], ACT.Copy).then_inc(SEM["y_act"], 1)

                copy_turned(0, 0, True)
                rounds(act, body)

            @block.vector
            def _(dve):
                def copy_turned(b, tile, early):
                    dve.wait_ge(SEM["turned"], 2 * tile + 2)
                    if not early:
                        dve.wait_ge(SEM["gu_done"], tile - (UNROLL - 1))
                    nc.vector.tensor_copy(xsT[b][:, 4 * SLOT:8 * SLOT], banks[:, 1, 0:4 * SLOT]).then_inc(SEM["xs_dve"], 1)

                def body(it, first, last):
                    for b in range(UNROLL):
                        tile = UNROLL * it + b
                        dve.wait_ge(SEM["silu_done"], tile + 1)
                        if not first:
                            dve.wait_ge(SEM["down_done"], 2 * tile - 2 * (UNROLL - 1))
                        nc.vector.tensor_tensor(heT[b], banks[:, 2 + b % 2, HE:2 * HE], sil[b], ALU.mult).then_inc(SEM["he_ready"], 1)
                        if not (last and b == UNROLL - 1):
                            copy_turned((b + 1) % UNROLL, tile + 1, first and b < UNROLL - 1)
                        dve.wait_ge(SEM["down_done"], 2 * tile + 2)
                        if not first:
                            dve.wait_ge(SEM[f"ys_stored{b}"], 16 * it)
                        nc.vector.tensor_copy(ys[b][:, halves[1]], banks[0:SLOT, 4 + (2 * b + 1) % 4]).then_inc(SEM["y_dve"], 1)

                copy_turned(0, 0, True)
                rounds(dve, body)

            @block.gpsimd
            def _(pool):
                with pool.Fori(0, ROUNDS) as it:
                    for b in range(UNROLL):
                        tile = UNROLL * it + b
                        pool.wait_ge(SEM["y_act"], tile + 1)
                        pool.wait_ge(SEM["y_dve"], tile + 1)
                        pool.dma_start(y_slots[bass.ds(tile * SLOT, SLOT)], ys[b]).then_inc(SEM[f"ys_stored{b}"], 16)
                for b in range(UNROLL):
                    pool.wait_ge(SEM[f"ys_stored{b}"], 16 * ROUNDS)

        for name in ("e_loaded", "e_turned", "e_xs", "e_gu", "e_silu", "e_he", "e_down", "e_y", "e_stored"):
            sem(name)

        def further(engine, body):
            needed = engine.value_load(tile_exp[0:1, EXTRA:EXTRA + 1], min_val=0, max_val=EXTRA)
            with engine.If(needed > 0):
                body(0, True)
                with engine.Fori(1, EXTRA) as i:
                    with engine.If(needed > i):
                        body(i, False)

        with nc.Block() as block:
            @block.sync
            def _(sp):
                def body(i, first):
                    if not first:
                        sp.wait_ge(SEM["e_stored"], 16 * i)
                    e = sp.value_load(tile_exp[0:1, bass.ds(i, 1)], min_val=0, max_val=EXPERTS - 1)
                    sp.dma_start(xs[0], x_slots[bass.ds((i + EXPERTS) * SLOT, SLOT)]).then_inc(SEM["e_loaded"], 16)
                    sp.dma_start(gu_mem[0], experts[bass.ds(e, 1), :, 0:GU].rearrange("a p w -> (a p) w")).then_inc(SEM["e_loaded"], 16)
                    sp.dma_start(dn_mem[0], experts[bass.ds(e, 1), :, GU:GU + DN].rearrange("a p w -> (a p) w")) \
                      .then_inc(SEM["e_loaded"], 16)
                further(sp, body)

            @block.gpsimd
            def _(pool):
                def body(i, first):
                    pool.wait_ge(SEM["e_y"], i + 1)
                    pool.dma_start(y_slots[bass.ds((i + EXPERTS) * SLOT, SLOT)], ys[0]).then_inc(SEM["e_stored"], 16)
                    pool.wait_ge(SEM["e_stored"], 16 * i + 16)
                further(pool, body)

            @block.tensor
            def _(pe):
                def body(i, first):
                    pe.wait_ge(SEM["e_loaded"], 48 * i + 48)
                    turn_rows(0, 0, banks[:, 0])
                    turn_rows(0, 1, banks[:, 1]).then_inc(SEM["e_turned"], 1)
                    pe.wait_ge(SEM["e_xs"], i + 1)
                    gate_up(0, banks[:, 2]).then_inc(SEM["e_gu"], 1)
                    pe.wait_ge(SEM["e_he"], i + 1)
                    down(0, 0, banks[:, 4])
                    down(0, 1, banks[:, 5]).then_inc(SEM["e_down"], 1)
                further(pe, body)

            @block.scalar
            def _(act):
                def body(i, first):
                    act.wait_ge(SEM["e_turned"], i + 1)
                    nc.scalar.activation(xsT[0].rearrange("p (i w) -> p i w", i=2), banks[:, 0:2, 0:4 * SLOT], ACT.Copy) \
                        .then_inc(SEM["e_xs"], 1)
                    act.wait_ge(SEM["e_gu"], i + 1)
                    nc.scalar.activation(sil[0], banks[:, 2, 0:HE], ACT.Silu).then_inc(SEM["e_silu"], 1)
                    act.wait_ge(SEM["e_down"], i + 1)
                    nc.scalar.activation(ys[0].rearrange("p (i w) -> p i w", i=2), banks[0:SLOT, 4:6], ACT.Copy).then_inc(SEM["e_y"], 1)
                further(act, body)

            @block.vector
            def _(dve):
                def body(i, first):
                    dve.wait_ge(SEM["e_silu"], i + 1)
                    nc.vector.tensor_tensor(heT[0], banks[:, 2, HE:2 * HE], sil[0], ALU.mult).then_inc(SEM["e_he"], 1)
                further(dve, body)

        for name in ["z_added", "z_sq", "z_mean", "z_root", "z_out", "out_stored"] + [f"gathered{n}" for n in range(NT)]:
            sem(name)
        back = [[flat_slots[:, (2 * n + k) * D:(2 * n + k + 1) * D] for k in range(TOP_K)] for n in range(NT)]
        z_var = hvar[:, 0:NT]
        fnorm = gm_mem[:, 0:D]

        with nc.Block() as block:
            @block.gpsimd
            def _(pool):
                for n in range(NT):
                    for k in range(TOP_K):
                        pool.indirect_dma_start(out=back[n][k], out_offset=None, in_=y_slots,
                                                in_offset=bass.IndirectOffsetOnAxis(ap=slot_idx[:, k, n:n + 1], axis=0)) \
                            .then_inc(SEM[f"gathered{n}"], 16)

            @block.vector
            def _(dve):
                v = nc.vector
                for n in range(NT):
                    dve.wait_ge(SEM[f"gathered{n}"], 16 * TOP_K)
                    for k in range(TOP_K):
                        v.scalar_tensor_tensor(x_rows[:, n, :], back[n][k], rt[:, 7, n, k:k + 1], x_rows[:, n, :], ALU.mult, ALU.add) \
                            .then_inc(SEM["z_added"], 1)
                        dve.wait_ge(SEM["z_added"], TOP_K * n + k + 1)
                dve.wait_ge(SEM["z_sq"], NT)
                v.tensor_scalar(z_var, z_var, 1.0 / D, RMS_EPS, ALU.mult, ALU.add).then_inc(SEM["z_mean"], 1)
                dve.wait_ge(SEM["z_root"], 1)
                v.reciprocal(z_var, z_var).then_inc(SEM["z_mean"], 1)
                dve.wait_ge(SEM["z_mean"], 2)
                dve.wait_ge(SEM["fnorm_loaded"], 16)
                for n in range(NT):
                    v.scalar_tensor_tensor(x_rows[:, n, :], x_rows[:, n, :], z_var[:, n:n + 1], fnorm, ALU.mult, ALU.mult) \
                        .then_inc(SEM["z_out"], 1)

            @block.scalar
            def _(act):
                for n in range(NT):
                    act.wait_ge(SEM["z_added"], TOP_K * (n + 1))
                    nc.scalar.activation(back[n][0], x_rows[:, n, :], ACT.Square, accum_out=z_var[:, n:n + 1]).then_inc(SEM["z_sq"], 1)
                act.wait_ge(SEM["z_mean"], 1)
                nc.scalar.activation(z_var, z_var, ACT.Sqrt).then_inc(SEM["z_root"], 1)

            @block.sync
            def _(sp):
                sp.dma_start(fnorm, last_norm).then_inc(SEM["fnorm_loaded"], 16)
                for n in range(NT):
                    sp.wait_ge(SEM["z_out"], n + 1)
                    sp.dma_start(out[n * P:(n + 1) * P], x_rows[:, n, :]).then_inc(SEM["out_stored"], 16)
                sp.wait_ge(SEM["out_stored"], 16 * NT)
        for name, n in given.items():
            assert n == PER[name] or name.startswith("wload"), (name, n, PER[name])


def pack(i):
    f = lambda n: np.asarray(i[n])
    col = lambda a: a.reshape(-1, P).T
    kcols = lambda a: a.reshape(a.shape[0] // P, P, a.shape[1]).transpose(1, 0, 2)

    def cut(a, width):
        return [kcols(a[:, j:j + width]).reshape(P, -1) for j in range(0, a.shape[1], width)]

    def halves(a):
        return [b[:, j:j + CHUNK] for b in cut(a, 256) for j in (0, CHUNK)]

    zeros = lambda shape: np.zeros(shape, np.float32)
    stream, lpar = [], []
    ada = [b for l in range(LAYERS) for b in cut(f("w_ada")[l], 256)]
    for l in range(LAYERS):
        w_in = f("w_in")[l]
        o = dict(pu=0, pg=512, q=1024, k=1536, v=2048, tg=2560, r=3072, wl=3584, rk=3648, rv=4160, al=4672, rg=4736,
                 gates=5248)
        part = lambda name: w_in[:, o[name]:o[name] + 512]
        pad = lambda a: np.concatenate([a, zeros((P, CHUNK - a.shape[1]))], 1)
        stream += cut(part("r"), P)
        stream += cut(np.concatenate([w_in[:, o["wl"]:o["wl"] + 64], w_in[:, o["al"]:o["al"] + 64]], 1), P)
        stream += cut(part("rk"), P)
        stream.append(pad(np.concatenate([f("rwkv_w2")[l], f("rwkv_a2")[l]], 0)))
        for name in ("rv", "pu", "pg"):
            stream += cut(part(name), P)
        stream.append(pad(f("pool_w")[l].transpose(1, 0, 2).reshape(P, 512)))
        for name in "qkv":
            stream += halves(part(name))
        for name in ("rg", "tg"):
            stream += cut(part(name), P)
        wb = f("w_branch")[l]
        for cp in range(KD // 2):
            for n in range(3):
                a = o["gates"] + n * D + cp * 256
                stream += cut(w_in[:, a:a + 256], P)
            pairs = [(n, c) for c in (2 * cp, 2 * cp + 1) for n in range(3)]
            for j in range(0, 6, 2):
                stream.append(np.concatenate([kcols(wb[n][:, c * P:c * P + P]).reshape(P, -1) for n, c in pairs[j:j + 2]], 1))
        stream += cut(f("w_out")[l], P)
        mu = f("rwkv_shift_mu")[l]
        mu13 = np.concatenate([col(mu[0:512]), col(np.concatenate([mu[512:576], mu[1600:1664]])), col(mu[576:1088]),
                               col(mu[1088:1600])], 1)
        vecs = [col(f("pool_scale")[l]), col(f("ret_norm_g")[l]), mu13]
        vecs += [col(f("rwkv_" + n)[l].reshape(-1)) for n in ("w0", "a0", "k_k", "k_a", "r_k", "ln_w", "ln_b")]
        lpar.append(np.concatenate(vecs, 1))
    w2 = f("w_in_2")[0]
    for j in range(0, 3072, 1536):
        stream += cut(w2[:, j:j + 1024], P) + halves(w2[:, j + 1024:j + 1536])
    stream += cut(f("w_out_2")[0], P)
    norms = np.concatenate([f("out_norm_dil_2")[0], f("out_norm_fox_2")[0]])
    tall = lambda a: np.concatenate([a, zeros((P - a.shape[0], a.shape[1]))], 0)
    w_route = np.concatenate([f("w_router_group_2")[0], f("w_router_expert_2")[0]], 1)
    b_route = np.concatenate([f("b_router_group_2")[0], f("b_router_expert_2")[0]])[:, None]
    rel = np.concatenate([f("rel_bias_2"), np.ones((1, DIL_H), np.float32)], 0)
    gpar = [col(f("c")[0])] + [col(f("norm_g")[l]) for l in range(LAYERS)] + [col(f("b_ada")[l]) for l in range(LAYERS)]
    gpar += [col(f("final_g")), col(f("attn_norm_2")[0]), col(norms), col(f("ffn_norm_2")[0]),
            kcols(w2[:, 3072:3080]).reshape(P, KD * FOX_H), kcols(w_route).reshape(P, KD * ROUTE), tall(b_route),
            tall(f("b_forget_2")[0][:, None]), tall(rel)]
    wide = lambda a: a.reshape(EXPERTS, -1, P, a.shape[-1]).transpose(0, 2, 1, 3)
    gate_up = np.concatenate([wide(f("w_expert_gate_2")[0]), wide(f("w_expert_up_2")[0])], 3)
    experts = np.concatenate([gate_up.reshape(EXPERTS, P, -1), wide(f("w_expert_down_2")[0]).reshape(EXPERTS, P, -1)], 2)
    return {
        "ada": np.stack(ada), "wstream": np.stack(stream), "lparams": np.stack(lpar), "gparams": np.concatenate(gpar, 1),
        "consts": constants(), "distances": distance_table(), "experts": experts,
        "last_norm": np.broadcast_to(f("final_norm_2")[None, :], (P, D)),
        "x_in": np.ascontiguousarray(f("x")[0].T.reshape(KD, P, T).transpose(1, 0, 2).reshape(P, KD * T)),
        "pos_in": np.ascontiguousarray(f("positions")[0].reshape(NT, P).T.astype(np.int32)),
    }


def kernel(**inputs):
    import concourse.bacc as bacc
    from concourse.bass_utils import run_bass_kernel_spmd

    nc = bacc.Bacc("TRN2", target_bir_lowering=False, num_devices=1)
    arrays = {k: np.ascontiguousarray(a) for k, a in pack(inputs).items()}
    args = {k: nc.dram_tensor(k, a.shape, mybir.dt.from_np(a.dtype), kind="ExternalInput").ap() for k, a in arrays.items()}
    out = nc.dram_tensor("out", (T, D), F32, kind="ExternalOutput").ap()
    program(nc, out=out, **args)
    r = run_bass_kernel_spmd(nc, [arrays], core_ids=[0])
    got = r.results[0]["out"]
    return got.reshape(1, T, D)
```
